# Optimizing a Trainium2 kernel written in Bass

```python
import math
import jax, jax.numpy as jnp
from jax import lax
import numpy as np

D_MODEL = 1024
BATCH = 1
SEQ = 256
DEPTH = 2
DEC_BATCH = 8
DEC_SEQ = 8
PAST_LEN = 2048
PAGE_SIZE = 128

D_MIX = D_MODEL
D_A = D_MIX // 2
N_A = 64
H_A = D_A // N_A
D_B = D_MIX - D_A
H_B = 4
DK_B = D_B // H_B
R_W = 64
R_A = 64
R_G = 128
RWKV_COLS = 3 * D_A + R_W + R_A + R_G
MLSTM_COLS = 4 * D_B + 2 * H_B
IN_COLS = RWKV_COLS + MLSTM_COLS
RWKV_SPLITS = [D_A, 2 * D_A, 3 * D_A, 3 * D_A + R_W, 3 * D_A + R_W + R_A]
MLSTM_SPLITS = [2 * D_B, 3 * D_B, 4 * D_B, 4 * D_B + H_B]
CONV_W = 4
CHUNK = 64
D_FF = 2816
ALPHA = (2.0 * DEPTH) ** 0.25
BETA = (8.0 * DEPTH) ** -0.25
LN_EPS = 1e-5
GN_EPS = 64e-5
MH_EPS = 1e-6

kernel_name = 'hymba_rwkv7_mlstm_macaron_deepnorm_step'

def _layer_norm(x, g, b):
    xf = x.astype(jnp.float32)
    mu = xf.mean(-1, keepdims=True)
    var = jnp.mean(jnp.square(xf - mu), -1, keepdims=True)
    return ((xf - mu) * lax.rsqrt(var + LN_EPS)).astype(x.dtype) * g + b

def _swiglu(x, wg, wu, wd):
    return (jax.nn.silu(x @ wg) * (x @ wu)) @ wd

def _rwkv7(p, shift_prev, wkv0, mu_shift, w0, w2, a0, a2, g2, k_k, k_a, r_k, gn_g, gn_b):
    B, T, _ = p.shape
    dt = p.dtype
    f32 = jnp.float32
    p_prev = jnp.concatenate([shift_prev[:, None, :].astype(dt), p[:, :-1]], axis=1)
    pm = p + (p_prev - p) * mu_shift
    r, k, v, xw, xa, xg = jnp.split(pm, RWKV_SPLITS, axis=-1)
    w_raw = -jax.nn.softplus(-(w0 + jnp.tanh(xw) @ w2)) - 0.5
    decay = jnp.exp(-jnp.exp(w_raw.astype(f32)))
    a = jax.nn.sigmoid(a0 + xa @ a2)
    g = jax.nn.sigmoid(xg) @ g2
    heads = lambda t: t.reshape(B, T, H_A, N_A)
    kk = heads(k * k_k).astype(f32)
    kk = kk * lax.rsqrt(jnp.maximum(jnp.sum(kk * kk, -1, keepdims=True), 1e-24))
    k = k * (1 + (a - 1) * k_a)
    rh, kh, vh, ah = heads(r), heads(k), heads(v), heads(a)
    tm = lambda t: jnp.moveaxis(t.astype(f32), 1, 0)

    def step(S, inp):
        r_t, w_t, k_t, v_t, kk_t, a_t = inp
        sa = jnp.einsum('bhvk,bhk->bhv', S, -kk_t)
        S = (S * w_t[:, :, None, :] + sa[..., None] * (kk_t * a_t)[:, :, None, :]
             + v_t[..., None] * k_t[:, :, None, :])
        return S, jnp.einsum('bhvk,bhk->bhv', S, r_t)

    S_T, ys = lax.scan(step, wkv0.astype(f32), (tm(rh), tm(heads(decay)), tm(kh), tm(vh), tm(kk), tm(ah)))
    y = jnp.moveaxis(ys, 0, 1)
    mu = y.mean(-1, keepdims=True)
    var = jnp.mean(jnp.square(y - mu), -1, keepdims=True)
    y = ((y - mu) * lax.rsqrt(var + GN_EPS)).reshape(B, T, D_A).astype(dt) * gn_g + gn_b
    bonus = (jnp.sum(rh * kh * r_k, -1, keepdims=True) * vh).reshape(B, T, D_A)
    out = (y + bonus) * g
    return out, p[:, -1], S_T.astype(wkv0.dtype)

def _mlstm(p, conv_prev, C0, n0, m0, conv_w, conv_b, i_bias, f_bias, mh_g):
    B, T, _ = p.shape
    dt = p.dtype
    f32 = jnp.float32
    qk_pre, v, o_pre, i_pre, f_pre = jnp.split(p, MLSTM_SPLITS, axis=-1)
    ext = jnp.concatenate([conv_prev.astype(dt), qk_pre], axis=1)
    conv = conv_b + sum(ext[:, j:j + T] * conv_w[j] for j in range(CONV_W))
    q, k = jnp.split(jax.nn.silu(conv), 2, axis=-1)
    k = k * DK_B ** -0.5
    log_i = (i_pre + i_bias).astype(f32)
    log_f = jax.nn.log_sigmoid((f_pre + f_bias).astype(f32))
    L = math.gcd(T, CHUNK)
    NC = T // L
    ch4 = lambda t: t.astype(f32).reshape(B, NC, L, H_B, DK_B).transpose(1, 0, 3, 2, 4)
    ch3 = lambda t: t.reshape(B, NC, L, H_B).transpose(1, 0, 3, 2)
    causal = jnp.tril(jnp.ones((L, L), dtype=bool))

    def chunk_step(carry, inp):
        C, n, m = carry
        qc, kc, vc, lic, lfc = inp
        b = jnp.cumsum(lfc, axis=-1)
        dmat = jnp.where(causal, b[..., :, None] - b[..., None, :] + lic[..., None, :], -jnp.inf)
        inter = b + m[..., None]
        m_t = jnp.maximum(inter, dmat.max(-1))
        g_inter = jnp.exp(inter - m_t)
        s = jnp.einsum('bhtd,bhsd->bhts', qc, kc) * jnp.exp(dmat - m_t[..., None])
        num = g_inter[..., None] * jnp.einsum('bhtd,bhde->bhte', qc, C) + jnp.einsum('bhts,bhse->bhte', s, vc)
        den = g_inter * jnp.einsum('bhtd,bhd->bht', qc, n) + s.sum(-1)
        h = num / jnp.maximum(jnp.abs(den), jnp.exp(-m_t))[..., None]
        bL = b[..., -1]
        last = bL[..., None] - b + lic
        m_new = jnp.maximum(bL + m, last.max(-1))
        ws = jnp.exp(last - m_new[..., None])
        dec = jnp.exp(bL + m - m_new)
        C = dec[..., None, None] * C + jnp.einsum('bhs,bhsd,bhse->bhde', ws, kc, vc)
        n = dec[..., None] * n + jnp.einsum('bhs,bhsd->bhd', ws, kc)
        return (C, n, m_new), h

    (C_T, n_T, m_T), hs = lax.scan(
        chunk_step, (C0.astype(f32), n0.astype(f32), m0.astype(f32)),
        (ch4(q), ch4(k), ch4(v), ch3(log_i), ch3(log_f)))
    h = hs.transpose(1, 0, 3, 2, 4).reshape(B, T, H_B, DK_B)
    mu = h.mean(-1, keepdims=True)
    var = jnp.mean(jnp.square(h - mu), -1, keepdims=True)
    h = ((h - mu) * lax.rsqrt(var + MH_EPS)).reshape(B, T, D_B).astype(dt) * mh_g
    out = jax.nn.sigmoid(o_pre) * h
    return out, ext[:, T:], C_T.astype(C0.dtype), n_T.astype(n0.dtype), m_T.astype(m0.dtype)

def _layer(x, st, w):
    x = _layer_norm(ALPHA * x + 0.5 * _swiglu(x, w['ffn1_wg'], w['ffn1_wu'], w['ffn1_wd']), w['ln1_g'], w['ln1_b'])
    p = x @ w['w_in']
    ya, shift, wkv = _rwkv7(p[..., :RWKV_COLS], st[0], st[1], w['mu_shift'], w['w0'], w['w2'], w['a0'],
                            w['a2'], w['g2'], w['k_k'], w['k_a'], w['r_k'], w['gn_g'], w['gn_b'])
    yb, conv, C, n, m = _mlstm(p[..., RWKV_COLS:], st[2], st[3], st[4], st[5], w['conv_w'], w['conv_b'],
                               w['i_bias'], w['f_bias'], w['mh_g'])
    mix = jnp.concatenate([ya, yb], axis=-1) @ w['w_out']
    x = _layer_norm(ALPHA * x + mix, w['ln2_g'], w['ln2_b'])
    x = _layer_norm(ALPHA * x + 0.5 * _swiglu(x, w['ffn2_wg'], w['ffn2_wu'], w['ffn2_wd']), w['ln3_g'], w['ln3_b'])
    return x, (shift, wkv, conv, C, n, m)

def _trunk(x, states, weights):
    new = [[] for _ in range(len(states))]
    for l in range(DEPTH):
        w = {name: arr[l] for name, arr in weights.items()}
        x, st_new = _layer(x, [s[l] for s in states], w)
        for j, s in enumerate(st_new):
            new[j].append(s)
    return x, [jnp.stack(s) for s in new]

def setup_inputs(seed: int = 0) -> dict:
    key = jax.random.key(seed)
    ks = iter(jax.random.split(key, 48))
    nrm = lambda shape, s: jax.random.normal(next(ks), shape, jnp.float32) * s
    Lr = DEPTH
    speed = -7.0 + 5.0 * jnp.linspace(0.0, 1.0, D_A) ** 0.9 + 0.5
    return {
        'x_prompt': nrm((BATCH, SEQ, D_MODEL), 1.0),
        'x_sample': nrm((DEC_BATCH, DEC_SEQ, D_MODEL), 1.0),
        'state_shift': nrm((Lr, DEC_BATCH, RWKV_COLS), 1.0),
        'state_wkv': nrm((Lr, DEC_BATCH, H_A, N_A, N_A), 0.3),
        'state_conv': nrm((Lr, DEC_BATCH, CONV_W - 1, 2 * D_B), 1.0),
        'state_C': nrm((Lr, DEC_BATCH, H_B, DK_B, DK_B), 0.1),
        'state_n': nrm((Lr, DEC_BATCH, H_B, DK_B), 0.3),
        'state_m': nrm((Lr, DEC_BATCH, H_B), 1.0),
        'ffn1_wg': nrm((Lr, D_MODEL, D_FF), D_MODEL ** -0.5),
        'ffn1_wu': nrm((Lr, D_MODEL, D_FF), D_MODEL ** -0.5),
        'ffn1_wd': nrm((Lr, D_FF, D_MODEL), BETA * D_FF ** -0.5),
        'ln1_g': 1.0 + nrm((Lr, D_MODEL), 0.02),
        'ln1_b': nrm((Lr, D_MODEL), 0.02),
        'w_in': nrm((Lr, D_MODEL, IN_COLS), D_MODEL ** -0.5),
        'mu_shift': jax.random.uniform(next(ks), (Lr, RWKV_COLS), jnp.float32),
        'w0': speed[None, :] + nrm((Lr, D_A), 0.1),
        'w2': nrm((Lr, R_W, D_A), 0.1 * R_W ** -0.5),
        'a0': nrm((Lr, D_A), 0.1),
        'a2': nrm((Lr, R_A, D_A), 0.1 * R_A ** -0.5),
        'g2': nrm((Lr, R_G, D_A), R_G ** -0.5),
        'k_k': 0.85 + nrm((Lr, D_A), 0.05),
        'k_a': 1.0 + nrm((Lr, D_A), 0.05),
        'r_k': nrm((Lr, H_A, N_A), 0.1),
        'gn_g': 1.0 + nrm((Lr, D_A), 0.02),
        'gn_b': nrm((Lr, D_A), 0.02),
        'conv_w': nrm((Lr, CONV_W, 2 * D_B), CONV_W ** -0.5),
        'conv_b': nrm((Lr, 2 * D_B), 0.02),
        'i_bias': nrm((Lr, H_B), 0.1),
        'f_bias': jnp.linspace(3.0, 6.0, H_B)[None, :] + nrm((Lr, H_B), 0.1),
        'mh_g': 1.0 + nrm((Lr, D_B), 0.02),
        'w_out': nrm((Lr, D_MIX, D_MODEL), BETA * D_MIX ** -0.5),
        'ln2_g': 1.0 + nrm((Lr, D_MODEL), 0.02),
        'ln2_b': nrm((Lr, D_MODEL), 0.02),
        'ffn2_wg': nrm((Lr, D_MODEL, D_FF), D_MODEL ** -0.5),
        'ffn2_wu': nrm((Lr, D_MODEL, D_FF), D_MODEL ** -0.5),
        'ffn2_wd': nrm((Lr, D_FF, D_MODEL), BETA * D_FF ** -0.5),
        'ln3_g': 1.0 + nrm((Lr, D_MODEL), 0.02),
        'ln3_b': nrm((Lr, D_MODEL), 0.02),
    }

def reference(x_prompt, x_sample, state_shift, state_wkv, state_conv, state_C, state_n, state_m,
              ffn1_wg, ffn1_wu, ffn1_wd, ln1_g, ln1_b, w_in, mu_shift, w0, w2, a0, a2, g2, k_k, k_a, r_k,
              gn_g, gn_b, conv_w, conv_b, i_bias, f_bias, mh_g, w_out, ln2_g, ln2_b,
              ffn2_wg, ffn2_wu, ffn2_wd, ln3_g, ln3_b):
    weights = dict(ffn1_wg=ffn1_wg, ffn1_wu=ffn1_wu, ffn1_wd=ffn1_wd, ln1_g=ln1_g, ln1_b=ln1_b, w_in=w_in,
                   mu_shift=mu_shift, w0=w0, w2=w2, a0=a0, a2=a2, g2=g2, k_k=k_k, k_a=k_a, r_k=r_k,
                   gn_g=gn_g, gn_b=gn_b, conv_w=conv_w, conv_b=conv_b, i_bias=i_bias, f_bias=f_bias,
                   mh_g=mh_g, w_out=w_out, ln2_g=ln2_g, ln2_b=ln2_b, ffn2_wg=ffn2_wg, ffn2_wu=ffn2_wu,
                   ffn2_wd=ffn2_wd, ln3_g=ln3_g, ln3_b=ln3_b)
    B = x_prompt.shape[0]
    dt = x_prompt.dtype
    init = [jnp.zeros((DEPTH, B, RWKV_COLS), dt),
            jnp.zeros((DEPTH, B, H_A, N_A, N_A), dt),
            jnp.zeros((DEPTH, B, CONV_W - 1, 2 * D_B), dt),
            jnp.zeros((DEPTH, B, H_B, DK_B, DK_B), dt),
            jnp.zeros((DEPTH, B, H_B, DK_B), dt),
            jnp.zeros((DEPTH, B, H_B), dt)]
    y_prompt, (p_shift, p_wkv, p_conv, p_C, p_n, p_m) = _trunk(x_prompt, init, weights)
    y_sample, (s_shift, s_wkv, s_conv, s_C, s_n, s_m) = _trunk(
        x_sample, [state_shift, state_wkv, state_conv, state_C, state_n, state_m], weights)
    return (y_prompt, y_sample, p_shift, p_wkv, p_conv, p_C, p_n, p_m,
            s_shift, s_wkv, s_conv, s_C, s_n, s_m)


_drawn_inputs = setup_inputs


def setup_inputs(seed=0):
    import zlib

    import numpy as np

    out = dict(_drawn_inputs(seed))
    spreads = {}
    factors = {'w2': 8.0, 'gn_g': 8.0, 'gn_b': 8.0, 'mh_g': 8.0}
    for name, (base, spread) in spreads.items():
        noise = np.random.default_rng([zlib.crc32(name.encode()), seed]).standard_normal(out[name].shape)
        drawn = base * np.exp(spread * noise) if base else spread * noise
        out[name] = __import__('jax').numpy.asarray(drawn.astype(out[name].dtype))
    for name, factor in factors.items():
        out[name] = (out[name] * factor).astype(out[name].dtype)
    return out
```

```python
import math
from contextlib import ExitStack

import concourse.bass as bass
from concourse import mybir

ALU = mybir.AluOpType
ACT = mybir.ActivationFunctionType
F32 = mybir.dt.float32
F32R = mybir.dt.float32r
AX_X = mybir.AxisListType.X
P = 128
NEG = -1e30
E_HALF = math.exp(-0.5)


class Signal:

    def __init__(self, sem, n, head=0):
        self.sem, self.n, self.head = sem, n, head

    def by(self, L, k):
        return L * self.n + (self.head + k)


def hymba_kernel(nc, I, O):
    DEPTH, DM, FF = I["ffn1_wg"].shape
    TP = I["x_prompt"].shape[1]
    SB, ST, _ = I["x_sample"].shape
    TS = SB * ST
    T = TP + TS
    HA, NA = I["state_wkv"].shape[2:4]
    HB, DK = I["state_C"].shape[2:4]
    CW = I["conv_w"].shape[1]
    DA, DB = HA * NA, HB * DK
    RW = I["w2"].shape[1]
    ALPHA = (2.0 * DEPTH) ** 0.25
    LN_EPS, GN_EPS, MH_EPS = 1e-5, 64e-5, 1e-6
    KSCALE = DK ** -0.5
    KT = DM // P
    NFF = FF // P
    CH = 64
    NPC = TP // CH
    NCH = NPC + 1
    NJ = DA // P
    NRW = 3 * NJ + 2
    NQK = 2 * DB // P
    NIN = NQK + 2 * HB + NRW
    TV, TO, TR = NQK, NQK + HB, NQK + 2 * HB
    RCOLS = I["mu_shift"].shape[1]
    GCOL = RCOLS + 4 * DB
    LEAD = CW - 1
    SEG = LEAD + ST
    S0C = LEAD + TP
    W = S0C + SB * SEG
    NTT = 3
    TT = [(0, P), (P, P), (2 * P, TS)]
    assert T == 320 and TP == 2 * P and NA == CH == TS and 2 * NA == P == DK and RW == CH and KT == 8 and ST == 8

    RS = 4
    NUP, NDN = 2 * NFF, NFF // 2
    FFN = NUP + 2 * NDN
    up4 = lambda n: -(-n // RS) * RS
    U1 = 0
    WI = up4(FFN)
    WO = WI + up4(NIN)
    U2 = WO + KT
    NPOS = U2 + up4(FFN)
    PADS = [(U1 + FFN, WI), (WI + NIN, WO), (U2 + FFN, NPOS)]
    REAL = [p for p in range(NPOS) if not any(a <= p < b for a, b in PADS)]
    steps_of = {p: 1 + sum(b - a for a, b in PADS if a == p + 1) for p in REAL}
    loads_before = {p: sum(q % RS == p % RS and q < p for q in REAL) for p in REAL}
    slot_loads = [sum(p % RS == s for p in REAL) for s in range(RS)]
    LOOK = 3
    assert NUP % RS == 0 and NDN == 2 * RS + 3 and NIN == 7 * RS + 2

    with ExitStack() as ctx:
        def sb(name, shape, dt=F32):
            return ctx.enter_context(nc.sbuf_tensor(name, shape, dt))

        def signal(name, n, head=0):
            return Signal(ctx.enter_context(nc.semaphore(name)), n, head)

        raw = sb("raw", [P, RS, KT * P])
        whi = sb("whi", [P, RS, KT * P], F32R)
        wlo = sb("wlo", [P, RS, KT * P], F32R)
        x = sb("x", [P, KT, T])
        with ExitStack() as split:
            xh = split.enter_context(nc.sbuf_tensor("xh", [P, KT, T], F32R))
            xl = split.enter_context(nc.sbuf_tensor("xl", [P, KT, T], F32R))
        spare = sb("spare", [P, 2 * KT * T])
        z = sb("z", [P, KT, T])
        ident = sb("ident", [P, P])
        ones = sb("ones", [P, P])
        headones = sb("headones", [P, P])
        scmask = sb("scmask", [P, 2, 2, CH])
        lvmask = sb("lvmask", [P, 6, CH])
        negmask = sb("negmask", [P, 2, P])
        bmask = sb("bmask", [P, SB])
        keep64 = sb("keep64", [P, T])
        keep128 = sb("keep128", [HB, T])
        segneg = sb("segneg", [HB, TS])
        sel = sb("sel", [HB, HB, P])
        gbias = sb("gbias", [HB, 3])
        mark = gbias[0:1, 2:3]
        V_MU = 0
        V_W0, V_A0, V_KK, V_KA, V_RK, V_GG, V_GB, V_MH = (NRW + NJ * i for i in range(8))
        V_CB = NRW + 8 * NJ
        V_CW = V_CB + NQK
        NV1 = V_CW + CW * NQK
        V_LN = NV1
        NV2 = 6 * KT
        vec = sb("vec", [P, NV1 + NV2])

        with ExitStack() as hidden:
            hh = hidden.enter_context(nc.sbuf_tensor("hh", [P, NFF, T], F32R))
            hl = hidden.enter_context(nc.sbuf_tensor("hl", [P, NFF, T], F32R))
        SCW = 28032
        scratch = sb("scratch", [P, SCW])
        OPEN = 2 * NFF * T

        def area(at, *dims, rows=P, of=scratch):
            n = math.prod(dims)
            assert at + n <= of.shape[1], (at, dims)
            v = of[0:rows, at:at + n]
            if len(dims) == 1:
                return v
            names = " ".join(f"d{i}" for i in range(len(dims)))
            return v.rearrange(f"p ({names}) -> p {names}", **{f"d{i}": d for i, d in enumerate(dims)})

        FB = 16000 + RCOLS + 2 * DB
        silu = area(FB, 2, T)
        hval = area(FB + 2 * T, 2, T)
        sq = area(FB + 4 * T, KT, T)
        mean, var, rstd = (area(FB + (4 + KT + i) * T, T) for i in range(3))
        vrow1 = area(OPEN, P)
        vrow2 = area(OPEN + P, P)
        hist_shift = area(16000, RCOLS, rows=SB)
        hist_conv = area(16000 + RCOLS, 2 * DB, rows=SB * LEAD)
        xrows = area(OPEN, NTT, DM)
        proj = area(0, NIN, W)
        A0 = NIN * W
        qk = area(A0, NQK, T)
        og = area(A0 + NQK * T, HB, T)
        A1 = A0 + (NQK + HB) * T
        row = area(A1, 12, T, rows=HB)
        lim = area(A1 + 12 * T, 32, rows=HB)
        A2 = A1 + 12 * T + 32
        va = area(A2, NTT, HB, DK + 1)
        kt = area(A2 + NTT * HB * (DK + 1), NTT, HB, DK)
        A3 = A2 + NTT * HB * (2 * DK + 1)
        qh = area(A3, HB, T)
        ends = area(A3 + 1280, NQK, SB + 1, LEAD)
        vs = area(A3 + 1280 + NQK * (SB + 1) * LEAD, HB, TS)
        num = area(A3 + 1280, HB, DK + 1)
        hc = area(A3 + 1796, HB, DK)
        hsq = area(A3 + 2308, HB, DK)
        wexp = area(A3 + 2820, HB, P)
        rexp = area(A3 + 3332, HB, P)
        Caug = area(A3 + 3844, HB, DK + 1)
        cols = area(A3 + 4360, NTT, 4, HB)
        small = area(A3 + 4408, 64)
        n0 = area(A3 + 4472, SB, HB)
        nout = area(A3 + 4504, HB + SB * HB)
        nrow = area(A3 + 4540, DK, rows=HB + SB * HB)
        gatew = area(A3 + 4668, KT, CH)
        yb_new = area(A3 + 4668 + KT * CH, HB, T)
        tail = area(0, 2 * DB + RCOLS, rows=LEAD * (SB + 1), of=spare)
        C0 = area(0, SB, HB, DK, of=spare)
        yb = area((KT + NJ) * T, HB, T, of=spare)
        vmask = area(0, SB, HB, DK, rows=TS)
        inter = area(4200, HB, TS)
        assert TO * W <= 4200
        ar = area(0, NJ, NCH, 2, 2, CH)
        zv = area(5552, NJ, NCH, 2, CH)
        bk = area(8112, NJ, NCH, 2, CH)
        rm = area(10752, NRW, T)
        C1 = 15232
        lw, cum, aa, kk, e1, e2, kn, gg = (area(C1 + i * NJ * T, NJ, T) for i in range(8))
        bkh = area(25472, NJ, NCH, 2, CH)
        w2p, a2p, g2s = (area(25472 + i * DA, DA) for i in range(3))
        scores = area(10752, NCH, NJ, 2, 2, CH)
        bkt = area(16512, NCH, NJ, 2, CH)
        uv = area(19072, NCH, NJ, 2, CH)
        bonus = kn
        ati = area(0, NCH, NJ, P, of=spare)
        xti = area(25472, NCH, NJ, P)
        xi = z[:, :, :].rearrange("p a b -> p (a b)").rearrange("p (c j n) -> p c j n", c=NCH, j=NJ)
        t1 = area(8112, NCH, NJ, P)
        SMALLR = 5120
        dlast = area(SMALLR, NJ, NPC + SB)
        gnst = area(SMALLR + 48, 2, NCH * NJ)
        state = area(9648, 2, NJ, NA)
        sdec = area(9648 + 512, NJ, NA)
        rsb = area(9648 + 768, NJ, NA)
        wkv_rows = area(5552, SB, NJ, 2, NA, rows=NA)
        s0 = area(0, SB, NJ, NA, of=spare)
        uvm = area(5552, SB, NJ, 2, CH)
        snew = z[:, :, :].rearrange("p a b -> p (a b)")[:, 0:SB * NJ * NA].rearrange(
            "p (b j n) -> p b j n", b=SB, j=NJ)
        s0sum = area(15872, NJ, 2, TS)
        wkv_out = area(0, SB, NJ, 2, NA, rows=NA)
        pwkv_out = area(15872, NJ, 2, NA, rows=NA)
        yr = area(21632, NCH, NJ, NA)
        yc = area(10752, NCH, NJ, NA)
        ysq = area(12032, NCH, NJ, NA)
        ya = area(13312, NJ, T)

        bank = [ctx.enter_context(nc.psum_tensor(f"bank{i}", [P, 512], F32)) for i in range(8)]

        raw_in = [signal(f"raw_in{s}", 16 * slot_loads[s]) for s in range(RS)]
        hi_ready = signal("hi_ready", NPOS)
        lo_ready = signal("lo_ready", NPOS)
        used = signal("used", NPOS)
        consts = signal("consts", 0, 1)
        rows_in = signal("rows_in", 0, 16 * NTT)
        x_turned = signal("x_turned", 0, KT)
        x0_ready = signal("x0_ready", 0, KT)
        x0_hi = signal("x0_hi", 0, KT)
        x_ready = signal("x_ready", 3 * KT, KT)
        silu_ready = signal("silu_ready", 2 * NFF)
        up_done = signal("up_done", 2 * NFF, 2)
        hl_done = signal("hl_done", 2 * NFF, 2)
        z_ready = signal("z_ready", 3 * KT)
        sq_ready = signal("sq_ready", 3 * KT)
        stats_ready = signal("stats_ready", 3)
        var_ready = signal("var_ready", 3)
        sd_ready = signal("sd_ready", 3)
        norm_ready = signal("norm_ready", 3 * KT)
        xh_ready = signal("xh_ready", 3 * KT)
        vrows_in = signal("vrows_in", 16 * 17)
        vec_turned = signal("vec_turned", 1)
        vec_ready = signal("vec_ready", 1)
        hist_in = signal("hist_in", 32)
        hist_turned = signal("hist_turned", 1)
        hist_ready = signal("hist_ready", 1)
        leads_zero = signal("leads_zero", 1)
        proj_ready = signal("proj_ready", NIN, RS)
        conv_ready = signal("conv_ready", NQK)
        qk_ready = signal("qk_ready", 1)
        og_ready = signal("og_ready", 1)
        gatew_in = signal("gatew_in", 64)
        gates_mm = signal("gates_mm", 1)
        m_in = signal("m_in", 16)
        absf_ready = signal("absf_ready", 1)
        lnf_ready = signal("lnf_ready", 1)
        rows_ready = signal("rows_ready", 1)
        m_out = signal("m_out", 32)
        ends_ready = signal("ends_ready", 1)
        tail_turned = signal("tail_turned", 1)
        tail_ready = signal("tail_ready", 1)
        tail_out = signal("tail_out", 64)
        c0_in = signal("c0_in", 32)
        n0_turned = signal("n0_turned", 1)
        n0_ready = signal("n0_ready", 1)
        kv_turned = signal("kv_turned", NTT)
        kv_ready = signal("kv_ready", NTT)
        cols_turned = signal("cols_turned", 1)
        cols_ready = signal("cols_ready", 1)
        kw_ready = signal("kw_ready", 1)
        tile_mm = signal("tile_mm", NTT)
        wlog_ready = signal("wlog_ready", NTT)
        wexp_ready = signal("wexp_ready", NTT)
        tile_w = signal("tile_w", NTT)
        inter_mm = signal("inter_mm", 1)
        inter_ready = signal("inter_ready", 1)
        num_mm = signal("num_mm", NTT)
        num_ready = signal("num_ready", NTT)
        cadd_mm = signal("cadd_mm", 2)
        caug_ready = signal("caug_ready", 2)
        hvar_ready = signal("hvar_ready", NTT)
        hsd_ready = signal("hsd_ready", NTT)
        h_ready = signal("h_ready", NTT)
        h_turned = signal("h_turned", NTT)
        yb_ready = signal("yb_ready", NTT)
        vmask_ready = signal("vmask_ready", 1)
        c0_decayed = signal("c0_decayed", 1)
        cs_mm = signal("cs_mm", 2 * HB)
        cs_ready = signal("cs_ready", 2 * HB)
        ns_mm = signal("ns_mm", 1)
        nout_ready = signal("nout_ready", 1)
        nout_turned = signal("nout_turned", 1)
        nrow_ready = signal("nrow_ready", 1)
        c_out = signal("c_out", 16 * 4)
        yb_moved = signal("yb_moved", 1)
        shift_ready = signal("shift_ready", 1)
        lora_in = signal("lora_in", 48)
        lora_act = signal("lora_act", 1)
        lora_mm = signal("lora_mm", 2)
        lora_ready = signal("lora_ready", 2)
        pads_zero = signal("pads_zero", 1)
        kk_raw = signal("kk_raw", 1)
        kk_sq = signal("kk_sq", 1)
        kk_mm = signal("kk_mm", 1)
        kk_norm2 = signal("kk_norm2", 1)
        kk_norm = signal("kk_norm", 1)
        rk_ready = signal("rk_ready", 1)
        rk_mm = signal("rk_mm", 1)
        cum_ready = signal("cum_ready", 1)
        exp_ready = signal("exp_ready", 3)
        cumx_ready = signal("cumx_ready", 1)
        at_ready = signal("at_ready", 1)
        ab_ready = signal("ab_ready", 1)
        score_mm = signal("score_mm", 2 * NCH)
        score_ready = signal("score_ready", 2 * NCH)
        ati_ready = signal("ati_ready", NCH)
        turned = signal("turned", 2 * NCH)
        turned_out = signal("turned_out", 2 * NCH)
        NLV = [6] * NPC + [3]
        NSTEP = sum(NLV)
        t1_mm = signal("t1_mm", NSTEP)
        t1_ready = signal("t1_ready", NSTEP)
        x_mm = signal("x_mm", NSTEP)
        x_copied = signal("x_copied", NSTEP)
        wkv_in = signal("wkv_in", 16)
        s0_turned = signal("s0_turned", SB)
        s0_ready = signal("s0_ready", SB)
        s0_mm = signal("s0_mm", 1)
        s0sum_ready = signal("s0sum_ready", 1)
        r_mm = signal("r_mm", NCH)
        r_ready = signal("r_ready", NCH)
        u_mm = signal("u_mm", NCH)
        u_ready = signal("u_ready", NCH)
        y_mm = signal("y_mm", NCH)
        y_ready = signal("y_ready", NCH)
        s_mm = signal("s_mm", NPC)
        s_ready = signal("s_ready", NPC)
        uvm_ready = signal("uvm_ready", 1)
        s0_decayed = signal("s0_decayed", 1)
        ss_mm = signal("ss_mm", NJ)
        snew_ready = signal("snew_ready", 1)
        pw_turned = signal("pw_turned", 1)
        sw_turned = signal("sw_turned", SB)
        sw_ready = signal("sw_ready", SB + 1)
        wkv_left = signal("wkv_left", 32)
        bonus_read = signal("bonus_read", 1)
        t1_zero = signal("t1_zero", 1)
        gvar_ready = signal("gvar_ready", 1)
        gsd_ready = signal("gsd_ready", 1)
        yn_ready = signal("yn_ready", 1)
        y_back = signal("y_back", 1)
        ya_ready = signal("ya_ready", 1)
        mix_hi = signal("mix_hi", 1)
        mix_ready = signal("mix_ready", 1)
        end_turned = signal("end_turned", 0, 2 * NTT)
        end_low = signal("end_low", 0, NTT)
        end_high = signal("end_high", 0, NTT)
        y_out = signal("y_out", 0, 16 * NTT)

        block = ctx.enter_context(nc.Block())

        def carry(pool):
            pool.tensor_tensor(mark[:, :], ones[0:1, 0:1], ones[0:1, 0:1], ALU.mult)
            pool.drain()

        def seqs(ap):
            s = ap.shape
            names = " ".join(f"q{i}" for i in range(len(s) - 1))
            return ap.rearrange(f"{names} (b t) -> {names} b t", t=ST)

        def hist(ap):
            s = ap.shape
            names = " ".join(f"q{i}" for i in range(len(s) - 1))
            return ap[(slice(None),) * (len(s) - 1) + (slice(S0C, W),)].rearrange(
                f"{names} (b t) -> {names} b t", t=SEG)

        def bcast(ap, dim, n):
            sh = list(ap.shape)
            sh[dim] = n
            return ap.broadcast_to(sh)

        def conv(dve, L, n):
            dve.wait_ge(proj_ready.sem, proj_ready.by(L, n + 1))
            if n == 0:
                dve.wait_ge(hist_ready.sem, hist_ready.by(L, 1))
                dve.wait_ge(leads_zero.sem, leads_zero.by(L, 1))
            out_p, out_s = qk[:, n, 0:TP], seqs(qk[:, n, TP:T])
            hs = hist(proj[:, n, :])
            for j in range(CW):
                w = vec[:, V_CW + j * NQK + n:V_CW + j * NQK + n + 1]
                src_p, src_s = proj[:, n, j:j + TP], hs[:, :, j:j + ST]
                if j:
                    dve.drain()
                    dve.scalar_tensor_tensor(out=out_p, in0=src_p, scalar=w, in1=out_p, op0=ALU.mult, op1=ALU.add)
                    last = dve.scalar_tensor_tensor(out=out_s, in0=src_s, scalar=w, in1=out_s, op0=ALU.mult,
                                                    op1=ALU.add)
                else:
                    b = vec[:, V_CB + n:V_CB + n + 1]
                    dve.tensor_scalar(out_p, src_p, w, b, ALU.mult, ALU.add)
                    dve.tensor_scalar(out_s, src_s, w, b, ALU.mult, ALU.add)
            last.then_inc(conv_ready.sem, 1)

        def tile_views(n):
            at, rows = TT[n]
            return at, rows, 0 if n < 2 else 1

        def v_tokens(h, n):
            if n < 2:
                return proj[:, TV + h, LEAD + n * P:LEAD + (n + 1) * P]
            return vs[:, h, :]

        def turn(pe, out, src):
            rows = src.shape[0]
            if tuple(src.shape) == (P, P):
                return pe.transpose(out, src, ident[:, :])
            return pe.matmul(out, src, ident[0:rows, 0:rows], start=True, stop=True)

        def tensor_mixers(pe, L):
            pe.wait_ge(gatew_in.sem, gatew_in.by(L, 64))
            pe.wait_ge(proj_ready.sem, proj_ready.by(L, NIN))
            for k in range(KT):
                last = pe.matmul(bank[3][0:CH, 0:T], gatew[:, k, :], x[:, k, :], start=(k == 0), stop=(k == KT - 1))
            last.then_inc(gates_mm.sem, 1)
            pe.wait_ge(ends_ready.sem, ends_ready.by(L, 1))
            for n in range(NQK):
                pe.transpose(bank[n // 4][0:LEAD * (SB + 1), (n % 4) * P:(n % 4 + 1) * P],
                             ends[:, n, :, :].rearrange("p s j -> p (s j)"), ident[:, :])
            for n in range(NRW):
                b = 4 + n // 4
                src = proj[:, TR + n, S0C - SEG:W].rearrange("p (s t) -> p s t", t=SEG)[:, :, SEG - 1]
                last = pe.transpose(bank[b][0:SB + 1, (n % 4) * P:(n % 4 + 1) * P], src, ident[:, :])
            last.then_inc(tail_turned.sem, 1)
            pe.wait_ge(tail_ready.sem, tail_ready.by(L, 1))
            pe.wait_ge(qk_ready.sem, qk_ready.by(L, 1))
            for n in range(NTT):
                at, rows, _ = tile_views(n)
                if n >= 1:
                    pe.wait_ge(kv_ready.sem, kv_ready.by(L, n))
                for h in range(HB):
                    turn(pe, bank[4][0:rows, h * DK:(h + 1) * DK], qk[:, HB + h, at:at + rows])
                for h in range(HB):
                    last = pe.transpose(bank[5][0:rows, h * DK:(h + 1) * DK], v_tokens(h, n), ident[:, :])
                last.then_inc(kv_turned.sem, 1)
            pe.wait_ge(c0_in.sem, c0_in.by(L, 32))
            turn(pe, bank[6][:, 0:SB * HB], nrow[0:SB * HB, :]).then_inc(
                n0_turned.sem, 1)
            pe.wait_ge(rows_ready.sem, rows_ready.by(L, 1))
            for n in range(NTT):
                at, rows, _ = tile_views(n)
                for q, r in enumerate((5, 9, 10, 11)):
                    last = turn(pe, bank[7][0:rows, (n * 4 + q) * HB:(n * 4 + q + 1) * HB], row[:, r, at:at + rows])
            last.then_inc(cols_turned.sem, 1)
            pe.wait_ge(n0_ready.sem, n0_ready.by(L, 1))
            pe.wait_ge(cols_ready.sem, cols_ready.by(L, 1))
            pe.wait_ge(kv_ready.sem, kv_ready.by(L, NTT))
            for n in range(NTT):
                at, rows, _ = tile_views(n)
                if n:
                    pe.wait_ge(tile_w.sem, tile_w.by(L, n))
                for h in range(HB):
                    pe.matmul(bank[0][:, h * rows:(h + 1) * rows], sel[:, h, :], row[:, 7, at:at + rows],
                              start=True, stop=True)
                for h in range(HB):
                    pe.matmul(bank[1][:, h * rows:(h + 1) * rows], sel[:, h, :], row[:, 9, at:at + rows],
                              start=True, stop=True)
                for h in range(HB):
                    last = pe.matmul(bank[2][0:rows, h * rows:(h + 1) * rows], qk[:, HB + h, at:at + rows],
                                     qk[:, h, at:at + rows], start=True, stop=True)
                last.then_inc(tile_mm.sem, 1)
                pe.wait_ge(tile_w.sem, tile_w.by(L, n + 1))
                if n == 2:
                    pe.wait_ge(h_ready.sem, h_ready.by(L, 2))
                    for h in range(HB):
                        for b in range(SB):
                            last = pe.matmul(bank[7][:, h * TS + b * ST:h * TS + (b + 1) * ST], C0[:, b, h, :],
                                             qh[:, h, TP + b * ST:TP + (b + 1) * ST], start=True, stop=True)
                    for h in range(HB):
                        last = pe.matmul(bank[6][0:TS, h * SB:(h + 1) * SB], qh[:, h, TP:T], n0[:, :, h],
                                         start=True, stop=True)
                    last.then_inc(inter_mm.sem, 1)
                    pe.wait_ge(inter_ready.sem, inter_ready.by(L, 1))
                if n:
                    pe.wait_ge(num_ready.sem, num_ready.by(L, n))
                for h in range(HB):
                    out = bank[3 + h // 2][0:rows, (h % 2) * (DK + 1):(h % 2 + 1) * (DK + 1)]
                    if n == 2:
                        pe.matmul(out[:, 0:DK], inter[:, h, :], ident[:, :], start=True, stop=False,
                                  skip_group_check=True)
                    last = pe.matmul(out, wexp[0:rows, h, 0:rows], va[0:rows, n, h, :], start=(n < 2),
                                     stop=(n != 1), skip_group_check=(n == 2))
                    if n == 1:
                        if h == 0:
                            pe.wait_ge(caug_ready.sem, caug_ready.by(L, 1))
                        last = pe.matmul(out, qh[:, h, at:at + rows], Caug[:, h, :], start=False, stop=True)
                last.then_inc(num_mm.sem, 1)
                if n < 2:
                    pe.wait_ge(kw_ready.sem, kw_ready.by(L, 1))
                    if n == 1:
                        pe.wait_ge(caug_ready.sem, caug_ready.by(L, 1))
                    for h in range(HB):
                        out = bank[5 + h // 2][:, (h % 2) * (DK + 1):(h % 2 + 1) * (DK + 1)]
                        last = pe.matmul(out, kt[0:rows, n, h, :], va[0:rows, n, h, :], start=True, stop=True)
                    last.then_inc(cadd_mm.sem, 1)
                pe.wait_ge(h_ready.sem, h_ready.by(L, n + 1))
                if n:
                    pe.wait_ge(yb_ready.sem, yb_ready.by(L, n))
                for h in range(HB):
                    last = turn(pe, bank[7][:, h * rows:(h + 1) * rows], hc[0:rows, h, :])
                last.then_inc(h_turned.sem, 1)
            pe.wait_ge(vmask_ready.sem, vmask_ready.by(L, 1))
            pe.wait_ge(caug_ready.sem, caug_ready.by(L, 2))
            for h in range(HB):
                for half in range(2):
                    i = 2 * h + half
                    if i >= 4:
                        pe.wait_ge(cs_ready.sem, cs_ready.by(L, i - 3))
                    last = pe.matmul(bank[i % 4][:, :], kt[0:TS, 2, h, :],
                                     vmask[:, 4 * half:4 * half + 4, h, :], start=True, stop=True)
                    last.then_inc(cs_mm.sem, 1)
            for h in range(HB):
                last = pe.matmul(bank[6][:, h * SB:(h + 1) * SB], kt[0:TS, 2, h, :], bmask[0:TS, :],
                                 start=True, stop=True)
            last.then_inc(ns_mm.sem, 1)
            pe.wait_ge(nout_ready.sem, nout_ready.by(L, 1))
            turn(pe, bank[5][0:HB + SB * HB, 0:P], nout[:, :]).then_inc(nout_turned.sem, 1)

            pe.wait_ge(cs_ready.sem, cs_ready.by(L, 2 * HB))
            pe.wait_ge(lora_act.sem, lora_act.by(L, 1))
            pe.wait_ge(lora_in.sem, lora_in.by(L, 48))
            for j in range(NJ):
                pe.matmul(bank[j][:, 0:T], w2p[:, j * P:(j + 1) * P], rm[:, 3 * NJ, :], start=True, stop=True)
            pe.wait_ge(yb_ready.sem, yb_ready.by(L, NTT))
            pe.wait_ge(nrow_ready.sem, nrow_ready.by(L, 1))
            for j in range(NJ):
                last = pe.matmul(bank[4 + j][:, 0:T], a2p[:, j * P:(j + 1) * P], rm[:, 3 * NJ, :],
                                 start=True, stop=True)
            last.then_inc(lora_mm.sem, 1)
            pe.wait_ge(lora_ready.sem, lora_ready.by(L, 1))
            for j in range(NJ):
                last = pe.matmul(bank[j][:, 0:T], g2s[:, j * P:(j + 1) * P], rm[:, 3 * NJ + 1, :],
                                 start=True, stop=True)
            last.then_inc(lora_mm.sem, 1)
            pe.wait_ge(kk_sq.sem, kk_sq.by(L, 1))
            for j in range(NJ):
                last = pe.matmul(bank[4 + j][:, 0:T], headones[:, :], e1[:, j, :], start=True, stop=True)
            last.then_inc(kk_mm.sem, 1)
            pe.wait_ge(rk_ready.sem, rk_ready.by(L, 1))
            pe.wait_ge(kk_norm2.sem, kk_norm2.by(L, 1))
            for j in range(NJ):
                last = pe.matmul(bank[4 + j][:, 0:T], headones[:, :], e2[:, j, :], start=True, stop=True)
            last.then_inc(rk_mm.sem, 1)
            pe.wait_ge(lora_ready.sem, lora_ready.by(L, 2))
            pe.wait_ge(ab_ready.sem, ab_ready.by(L, 1))
            for c in range(NCH):
                for g in range(2):
                    i = 2 * c + g
                    if i >= 4:
                        pe.wait_ge(score_ready.sem, score_ready.by(L, i - 3))
                    for q in range(2):
                        j = 2 * g + q
                        last = pe.matmul(bank[i % 4][:, q * 256:(q + 1) * 256],
                                         bk[:, j, c, :, :].rearrange("p s t -> p (s t)"),
                                         ar[:, j, c, :, :, :].rearrange("p q s t -> p (q s t)"),
                                         start=True, stop=True)
                    last.then_inc(score_mm.sem, 1)
            pe.wait_ge(bonus_read.sem, bonus_read.by(L, 1))
            for c in range(NCH):
                for q, src in enumerate((bkh, zv)):
                    i = 2 * c + q
                    if i >= 2:
                        pe.wait_ge(turned_out.sem, turned_out.by(L, i - 1))
                    for j in range(NJ):
                        last = pe.transpose(bank[4 + q][:, j * P:(j + 1) * P],
                                            src[:, j, c, :, :].rearrange("p s t -> p (s t)"), ident[:, :])
                    last.then_inc(turned.sem, 1)
            pe.wait_ge(turned_out.sem, turned_out.by(L, 2 * NCH))
            step = 0
            for lv in range(6):
                live = [c for c in range(NCH) if lv < NLV[c]]
                for n, c in enumerate(live):
                    if lv == 0:
                        pe.wait_ge(ati_ready.sem, ati_ready.by(L, c + 1))
                        pe.wait_ge(score_ready.sem, score_ready.by(L, 2 * NCH))
                    else:
                        pe.wait_ge(x_copied.sem, x_copied.by(L, step - len(live_before) + live_before.index(c) + 1))
                    if step + n >= 2:
                        pe.wait_ge(t1_ready.sem, t1_ready.by(L, step + n - 1))
                    for j in range(NJ):
                        rhs = ident[:, :] if lv == 0 else xi[:, c, j, :]
                        last = pe.matmul(bank[(step + n) % 2][:, j * P:(j + 1) * P], ati[:, c, j, :], rhs,
                                         start=True, stop=True)
                    last.then_inc(t1_mm.sem, 1)
                    if n >= 1:
                        grow(pe, L, lv, live[n - 1], step + n - 1)
                grow(pe, L, lv, live[-1], step + len(live) - 1)
                step += len(live)
                live_before = live
            for c in range(NCH):
                out = bank[0][:, 0:NJ * NA]
                if c == NPC:
                    samples_memory_in(pe, L)
                if c == 0:
                    pe.wait_ge(x_copied.sem, x_copied.by(L, NSTEP))
                if 1 <= c < NPC:
                    pe.wait_ge(s_ready.sem, s_ready.by(L, c))
                for j in range(NJ):
                    for q in range(2):
                        o = bank[0][q * CH:(q + 1) * CH, j * NA:(j + 1) * NA]
                        last = pe.matmul(o, scores[:, c, j, q, 0, :], uv[:, c, j, q, :], start=True, stop=(c == 0))
                        if 0 < c < NPC:
                            last = pe.matmul(o, ar[:, j, c, q, 0, :], state[:, c % 2, j, :], start=False, stop=True)
                        if c == NPC:
                            last = pe.matmul(o, s0sum[:, j, 0, :], ident[:, q * CH:(q + 1) * CH], start=False,
                                             stop=True)
                last.then_inc(r_mm.sem, 1)
                pe.wait_ge(r_ready.sem, r_ready.by(L, c + 1))
                for j in range(NJ):
                    last = pe.matmul(bank[1][:, j * NA:(j + 1) * NA], xti[:, c, j, :], rsb[:, j, :],
                                     start=True, stop=True)
                last.then_inc(u_mm.sem, 1)
                pe.wait_ge(u_ready.sem, u_ready.by(L, c + 1))
                if c < NPC:
                    for j in range(NJ):
                        for q in range(2):
                            last = pe.matmul(bank[3][q * CH:(q + 1) * CH, j * NA:(j + 1) * NA],
                                             bkt[:, c, j, q, :], uv[:, c, j, q, :], start=True, stop=True)
                    last.then_inc(s_mm.sem, 1)
                if c:
                    pe.wait_ge(y_ready.sem, y_ready.by(L, c))
                for j in range(NJ):
                    for q in range(2):
                        o = bank[2][q * CH:(q + 1) * CH, j * NA:(j + 1) * NA]
                        last = pe.matmul(o, scores[:, c, j, q, 1, :], uv[:, c, j, q, :], start=True, stop=(c == 0))
                        if 0 < c < NPC:
                            last = pe.matmul(o, ar[:, j, c, q, 1, :], state[:, c % 2, j, :], start=False, stop=True)
                        if c == NPC:
                            last = pe.matmul(o, s0sum[:, j, 1, :], ident[:, q * CH:(q + 1) * CH], start=False,
                                             stop=True)
                last.then_inc(y_mm.sem, 1)
            pe.wait_ge(uvm_ready.sem, uvm_ready.by(L, 1))
            for j in range(NJ):
                for q in range(2):
                    last = pe.matmul(bank[4 + j][q * CH:(q + 1) * CH, :], bkt[:, NPC, j, q, :],
                                     uvm[:, :, j, q, :], start=True, stop=True)
                last.then_inc(ss_mm.sem, 1)
            pe.wait_ge(yn_ready.sem, yn_ready.by(L, 1))
            for j in range(NJ):
                for c in range(NCH):
                    for q in range(2):
                        last = pe.matmul(bank[j][q * CH:(q + 1) * CH, c * CH:(c + 1) * CH], yc[:, c, j, :],
                                         ident[:, q * CH:(q + 1) * CH], start=True, stop=True)
            last.then_inc(y_back.sem, 1)
            pe.wait_ge(snew_ready.sem, snew_ready.by(L, 1))
            for j in range(NJ):
                last = turn(pe, bank[4][0:NA, j * P:(j + 1) * P], state[:, NPC % 2, j, :])
            last.then_inc(pw_turned.sem, 1)
            for b in range(SB):
                if b >= 3:
                    pe.wait_ge(sw_ready.sem, sw_ready.by(L, b - 1))
                for j in range(NJ):
                    last = turn(pe, bank[5 + b % 3][0:NA, j * P:(j + 1) * P], snew[:, b, j, :])
                last.then_inc(sw_turned.sem, 1)

        def grow(pe, L, lv, c, n):
            pe.wait_ge(t1_ready.sem, t1_ready.by(L, n + 1))
            if n >= 2:
                pe.wait_ge(x_copied.sem, x_copied.by(L, n - 1))
            for j in range(NJ):
                pe.matmul(bank[2 + n % 2][:, j * P:(j + 1) * P], ident[:, :] if lv == 0 else xti[:, c, j, :],
                          t1[:, c, j, :], start=True, stop=True)
            for j in range(NJ):
                last = pe.matmul(bank[4 + n % 2][:, j * P:(j + 1) * P], t1[:, c, j, :],
                                 ident[:, :] if lv == 0 else xti[:, c, j, :], start=True, stop=True)
            last.then_inc(x_mm.sem, 1)

        def samples_memory_in(pe, L):
            pe.wait_ge(wkv_in.sem, wkv_in.by(L, 16))
            for b in range(SB):
                if b >= 2:
                    pe.wait_ge(s0_ready.sem, s0_ready.by(L, b - 1))
                for j in range(NJ):
                    last = turn(pe, bank[4 + b % 2][:, j * NA:(j + 1) * NA],
                                wkv_rows[:, b, j, :, :].rearrange("v q k -> v (q k)"))
                last.then_inc(s0_turned.sem, 1)
            pe.wait_ge(s0_ready.sem, s0_ready.by(L, SB))
            for j in range(NJ):
                for q in range(2):
                    for b in range(SB):
                        out = bank[6][q * CH:(q + 1) * CH, j * 2 * TS:(j + 1) * 2 * TS].rearrange(
                            "p (s t) -> p s t", s=2)[:, :, b * ST:(b + 1) * ST]
                        last = pe.matmul(out, s0[:, b, j, :], ar[:, j, NPC, q, :, b * ST:(b + 1) * ST],
                                         start=True, stop=True)
            last.then_inc(s0_mm.sem, 1)
            pe.wait_ge(s0sum_ready.sem, s0sum_ready.by(L, 1))

        LEVELS = [(lv, c) for lv in range(6) for c in range(NCH) if lv < NLV[c]]

        def scalar_mixers(act, L):
            act.activation(ends[:, :, :, :], proj[:, 0:NQK, S0C - SEG:W].rearrange(
                "p n (s t) -> p n s t", t=SEG)[:, :, :, SEG - LEAD:SEG], ACT.Copy)
            act.activation(seqs(vs[:, :, :]), hist(proj[:, TV:TO, :])[:, :, :, LEAD:SEG],
                           ACT.Copy).then_inc(ends_ready.sem, 1)
            act.activation(og[:, :, 0:TP], proj[:, TO:TR, LEAD:LEAD + TP], ACT.Sigmoid)
            act.activation(seqs(og[:, :, TP:T]), hist(proj[:, TO:TR, :])[:, :, :, LEAD:SEG],
                           ACT.Sigmoid).then_inc(og_ready.sem, 1)
            act.wait_ge(conv_ready.sem, conv_ready.by(L, NQK))
            act.activation(qk[:, :, :], qk[:, :, :], ACT.Silu).then_inc(qk_ready.sem, 1)
            act.wait_ge(tail_turned.sem, tail_turned.by(L, 1))
            for i in range(2):
                act.activation(tail[:, i * 512:(i + 1) * 512], bank[i][0:LEAD * (SB + 1), :], ACT.Copy)
            for i in range(4):
                n = min(512, RCOLS - i * 512)
                last = act.activation(tail[0:SB + 1, 2 * DB + i * 512:2 * DB + i * 512 + n],
                                      bank[4 + i][0:SB + 1, 0:n], ACT.Copy)
            last.then_inc(tail_ready.sem, 1)
            act.wait_ge(absf_ready.sem, absf_ready.by(L, 1))
            act.activation(row[:, 2, :], row[:, 2, :], ACT.Exp, scale=-1.0)
            act.drain()
            act.activation(row[:, 2, :], row[:, 2, :], ACT.Ln, bias=ones[0:HB, 0:1]).then_inc(lnf_ready.sem, 1)
            for n in range(NTT):
                at, rows, _ = tile_views(n)
                act.wait_ge(kv_turned.sem, kv_turned.by(L, n + 1))
                act.activation(kt[0:rows, n, :, :], bank[4][0:rows, :].rearrange("p (h d) -> p h d", h=HB), ACT.Copy)
                act.activation(va[0:rows, n, :, 0:DK], bank[5][0:rows, :].rearrange("p (h d) -> p h d", h=HB),
                               ACT.Copy).then_inc(kv_ready.sem, 1)
            act.wait_ge(n0_turned.sem, n0_turned.by(L, 1))
            act.activation(n0[:, :, :], bank[6][:, 0:SB * HB].rearrange("p (b h) -> p b h", b=SB),
                           ACT.Copy).then_inc(n0_ready.sem, 1)
            act.wait_ge(cols_turned.sem, cols_turned.by(L, 1))
            for n in range(NTT):
                rows = TT[n][1]
                src = bank[7][0:rows, n * 4 * HB:(n + 1) * 4 * HB].rearrange("p (q h) -> p q h", q=4)
                act.activation(cols[0:rows, n, 0, :], src[:, 0, :], ACT.Copy)
                last = act.activation(cols[0:rows, n, 1:4, :], src[:, 1:4, :], ACT.Exp)
            last.then_inc(cols_ready.sem, 1)
            for n in range(NTT):
                at, rows, _ = tile_views(n)
                flat = lambda t: t[:, :, :].rearrange("p a b -> p (a b)")
                act.wait_ge(tile_mm.sem, tile_mm.by(L, n + 1))
                if n == 2:
                    act.wait_ge(caug_ready.sem, caug_ready.by(L, 2))
                elif n:
                    act.wait_ge(tile_w.sem, tile_w.by(L, n))
                act.activation(flat(rexp)[:, 0:HB * rows], bank[1][:, 0:HB * rows], ACT.Exp)
                act.wait_ge(wlog_ready.sem, wlog_ready.by(L, n + 1))
                act.activation(wexp[0:rows, :, 0:rows], wexp[0:rows, :, 0:rows], ACT.Exp).then_inc(wexp_ready.sem, 1)
                if n == 2:
                    act.wait_ge(inter_mm.sem, inter_mm.by(L, 1))
                    act.activation(inter[:, :, :], bank[7][:, 0:HB * TS].rearrange("p (h t) -> p h t", h=HB),
                                   ACT.Copy).then_inc(inter_ready.sem, 1)
                act.wait_ge(num_mm.sem, num_mm.by(L, n + 1))
                if n:
                    act.wait_ge(h_ready.sem, h_ready.by(L, n))
                for g in range(2):
                    last = act.activation(num[0:rows, 2 * g:2 * g + 2, :], bank[3 + g][0:rows, 0:2 * (DK + 1)]
                                          .rearrange("p (h d) -> p h d", h=2), ACT.Copy)
                last.then_inc(num_ready.sem, 1)
                act.wait_ge(hvar_ready.sem, hvar_ready.by(L, n + 1))
                act.activation(small[0:rows, 16:20], small[0:rows, 12:16], ACT.Sqrt).then_inc(hsd_ready.sem, 1)
            act.wait_ge(nout_turned.sem, nout_turned.by(L, 1))
            act.activation(nrow[:, :], bank[5][0:HB + SB * HB, 0:P], ACT.Copy).then_inc(nrow_ready.sem, 1)
            act.wait_ge(shift_ready.sem, shift_ready.by(L, 1))
            act.activation(rm[:, 3 * NJ + 1, :], rm[:, 3 * NJ + 1, :], ACT.Sigmoid)
            act.activation(rm[0:RW, 3 * NJ, :], rm[0:RW, 3 * NJ, :], ACT.Tanh).then_inc(lora_act.sem, 1)
            act.wait_ge(lora_mm.sem, lora_mm.by(L, 1))
            for j in range(NJ):
                act.activation(lw[:, j, :], bank[j][:, 0:T], ACT.Sigmoid, bias=vec[:, V_W0 + j:V_W0 + j + 1])
            for j in range(NJ):
                last = act.activation(aa[:, j, :], bank[4 + j][:, 0:T], ACT.Sigmoid,
                                      bias=vec[:, V_A0 + j:V_A0 + j + 1])
            last.then_inc(lora_ready.sem, 1)
            act.wait_ge(kk_raw.sem, kk_raw.by(L, 1))
            act.activation(e1[:, :, :], kk[:, :, :], ACT.Square).then_inc(kk_sq.sem, 1)
            act.wait_ge(lora_mm.sem, lora_mm.by(L, 2))
            for j in range(NJ):
                last = act.activation(gg[:, j, :], bank[j][:, 0:T], ACT.Copy)
            last.then_inc(lora_ready.sem, 1)
            act.wait_ge(kk_norm2.sem, kk_norm2.by(L, 1))
            act.activation(e1[:, :, :], e1[:, :, :], ACT.Sqrt).then_inc(kk_norm.sem, 1)
            act.wait_ge(cum_ready.sem, cum_ready.by(L, 1))
            act.activation(e1[:, :, :], cum[:, :, :], ACT.Exp).then_inc(exp_ready.sem, 1)
            act.wait_ge(cumx_ready.sem, cumx_ready.by(L, 1))
            act.activation(e2[:, :, :], e2[:, :, :], ACT.Exp).then_inc(exp_ready.sem, 1)
            act.wait_ge(at_ready.sem, at_ready.by(L, 1))
            act.activation(e2[:, :, :], cum[:, :, :], ACT.Exp, scale=-1.0).then_inc(exp_ready.sem, 1)
            for c in range(NCH):
                for q, dst in enumerate((bkt, uv)):
                    act.wait_ge(turned.sem, turned.by(L, 2 * c + q + 1))
                    if c == 0:
                        act.wait_ge(score_mm.sem, score_mm.by(L, 2 * NCH))
                    act.activation(dst[:, c, :, :, :].rearrange("p j s t -> p (j s t)"), bank[4 + q][:, :],
                                   ACT.Copy).then_inc(turned_out.sem, 1)
            for n, (lv, c) in enumerate(LEVELS):
                act.wait_ge(x_mm.sem, x_mm.by(L, n + 1))
                act.activation(xi[:, c, :, :], bank[2 + n % 2][:, :].rearrange("p (j s) -> p j s", j=NJ), ACT.Copy)
                act.activation(xti[:, c, :, :], bank[4 + n % 2][:, :].rearrange("p (j s) -> p j s", j=NJ),
                               ACT.Copy).then_inc(x_copied.sem, 1)
            for c in range(NCH):
                if c == NPC:
                    for b in range(SB):
                        act.wait_ge(s0_turned.sem, s0_turned.by(L, b + 1))
                        act.activation(s0[:, b, :, :], bank[4 + b % 2][:, 0:NJ * NA].rearrange(
                            "p (j v) -> p j v", j=NJ), ACT.Copy).then_inc(s0_ready.sem, 1)
                    act.wait_ge(s0_mm.sem, s0_mm.by(L, 1))
                    act.activation(s0sum[:, :, :, :].rearrange("p j s t -> p (j s t)"), bank[6][:, :],
                                   ACT.Copy).then_inc(s0sum_ready.sem, 1)
                act.wait_ge(r_mm.sem, r_mm.by(L, c + 1))
                act.activation(rsb[:, :, :], bank[0][:, 0:NJ * NA].rearrange("p (j v) -> p j v", j=NJ),
                               ACT.Copy).then_inc(r_ready.sem, 1)
                act.wait_ge(y_mm.sem, y_mm.by(L, c + 1))
                act.activation(yr[:, c, :, :], bank[2][:, 0:NJ * NA].rearrange("p (j v) -> p j v", j=NJ),
                               ACT.Copy).then_inc(y_ready.sem, 1)
            act.wait_ge(gvar_ready.sem, gvar_ready.by(L, 1))
            act.activation(gnst[:, 1, :], gnst[:, 1, :], ACT.Sqrt).then_inc(gsd_ready.sem, 1)
            act.wait_ge(pw_turned.sem, pw_turned.by(L, 1))
            act.activation(pwkv_out[:, :, :, :].rearrange("p j q k -> p (j q k)"), bank[4][0:NA, :],
                           ACT.Copy).then_inc(sw_ready.sem, 1)
            for b in range(SB):
                act.wait_ge(sw_turned.sem, sw_turned.by(L, b + 1))
                act.activation(wkv_out[:, b, :, :, :].rearrange("p j q k -> p (j q k)"), bank[5 + b % 3][0:NA, :],
                               ACT.Copy).then_inc(sw_ready.sem, 1)
            act.wait_ge(ya_ready.sem, ya_ready.by(L, 1))
            act.activation(xh[:, 0:NJ, :], ya[:, :, :], ACT.Copy)
            act.activation(xh[:, NJ:KT, :], yb[:, :, :], ACT.Copy).then_inc(mix_hi.sem, 1)

        def vector_mixers(dve, L):
            tt, stt, ts = dve.tensor_tensor, dve.scalar_tensor_tensor, dve.tensor_scalar
            dve.memset(va[:, :, :, DK:DK + 1], 1.0)
            dve.wait_ge(gates_mm.sem, gates_mm.by(L, 1))
            dve.wait_ge(gatew_in.sem, gatew_in.by(L, 64))
            ts(row[:, 0, :], bank[3][0:HB, 0:T], gbias[:, 0:1], None, ALU.add)
            ts(row[:, 1, :], bank[3][32:32 + HB, 0:T], gbias[:, 1:2], None, ALU.add)
            dve.drain()
            stt(out=row[:, 2, :], in0=row[:, 1, :], scalar=-1.0, in1=row[:, 1, :], op0=ALU.mult,
                op1=ALU.max).then_inc(absf_ready.sem, 1)
            dve.wait_ge(og_ready.sem, og_ready.by(L, 1))
            for h in range(HB):
                ts(og[:, h, :], og[:, h, :], vec[:, V_MH + h:V_MH + h + 1], None, ALU.mult)
            dve.wait_ge(lnf_ready.sem, lnf_ready.by(L, 1))
            stt(out=row[:, 3, :], in0=row[:, 1, :], scalar=0.0, in1=row[:, 2, :], op0=ALU.min, op1=ALU.subtract)
            dve.drain()
            dve.tensor_tensor_scan(row[:, 4, :], keep128[:, :], row[:, 3, :], 0.0, ALU.mult, ALU.add)
            dve.drain()
            tt(row[:, 5, :], row[:, 0, :], row[:, 4, :], ALU.subtract)
            dve.drain()
            dve.wait_ge(m_in.sem, m_in.by(L, 16))
            b_, g_, m_ = row[:, 4, :], row[:, 5, :], row[:, 6, :]
            dve.tensor_tensor_scan(m_[:, 0:P], ones[0:HB, :], g_[:, 0:P], 0.0, ALU.mult, ALU.max)
            dve.tensor_copy(row[:, 2, TP:T], g_[:, TP:T])
            dve.drain()
            tt(lim[:, 0:1], b_[:, P - 1:P], m_[:, P - 1:P], ALU.add)
            tt(row[:, 2, TP:T:ST], g_[:, TP:T:ST], lim[:, 8:8 + SB], ALU.max)
            dve.drain()
            dve.tensor_tensor_scan(m_[:, P:TP], ones[0:HB, :], g_[:, P:TP], lim[:, 0:1], ALU.mult, ALU.max)
            dve.tensor_tensor_scan(m_[:, TP:T], segneg[:, :], row[:, 2, TP:T], 0.0, ALU.add, ALU.max)
            dve.drain()
            tt(lim[:, 1:2], b_[:, TP - 1:TP], m_[:, TP - 1:TP], ALU.add)
            tt(lim[:, 16:16 + SB], b_[:, TP + ST - 1:T:ST], m_[:, TP + ST - 1:T:ST], ALU.add)
            ts(row[:, 7, :], m_, -1.0, None, ALU.mult)
            ts(row[:, 9, 0:P], m_[:, 0:P], -1.0, None, ALU.mult)
            ts(row[:, 9, P:TP], m_[:, P:TP], -1.0, lim[:, 0:1], ALU.mult, ALU.add)
            per_seq = lambda ap: bcast(ap.rearrange("h (b t) -> h b t", t=1), 2, ST)
            tt(seqs(row[:, 9, TP:T]), per_seq(lim[:, 8:8 + SB]), seqs(m_[:, TP:T]), ALU.subtract)
            stt(out=row[:, 10, :], in0=b_, scalar=-1.0, in1=m_, op0=ALU.mult, op1=ALU.subtract)
            for at in (0, P):
                ts(row[:, 11, at:at + P], g_[:, at:at + P], m_[:, at + P - 1:at + P], None, ALU.subtract)
            tt(seqs(row[:, 11, TP:T]), seqs(g_[:, TP:T]), per_seq(m_[:, TP + ST - 1:T:ST]),
               ALU.subtract).then_inc(rows_ready.sem, 1)
            dve.wait_ge(cols_ready.sem, cols_ready.by(L, 1))
            dve.wait_ge(kv_ready.sem, kv_ready.by(L, NTT))
            for n in range(NTT):
                rows = TT[n][1]
                ts(cols[0:rows, n, 3, :], cols[0:rows, n, 3, :], KSCALE, None, ALU.mult)
            dve.drain()
            for n in range(NTT):
                rows = TT[n][1]
                ws = cols[0:rows, n, 3, :].rearrange("p (h o) -> p h o", o=1)
                last = tt(kt[0:rows, n, :, :], kt[0:rows, n, :, :], bcast(ws, 2, DK), ALU.mult)
            last.then_inc(kw_ready.sem, 1)
            for n in range(NTT):
                at, rows, kind = tile_views(n)
                dve.wait_ge(tile_mm.sem, tile_mm.by(L, n + 1))
                if n:
                    dve.wait_ge(num_mm.sem, num_mm.by(L, n))
                for h in range(HB):
                    last = stt(out=wexp[0:rows, h, 0:rows], in0=bank[0][0:rows, h * rows:(h + 1) * rows],
                               scalar=cols[0:rows, n, 0, h:h + 1], in1=negmask[0:rows, kind, 0:rows],
                               op0=ALU.add, op1=ALU.add)
                last.then_inc(wlog_ready.sem, 1)
                dve.wait_ge(wexp_ready.sem, wexp_ready.by(L, n + 1))
                if n:
                    tt(qh[:, :, at:at + rows], qk[:, 0:HB, at:at + rows],
                       rexp[:, :, :].rearrange("p h t -> p (h t)")[:, 0:HB * rows].rearrange(
                           "p (h t) -> p h t", h=HB), ALU.mult)
                stt(out=wexp[0:rows, :, 0:rows],
                    in0=bank[2][0:rows, 0:HB * rows].rearrange("p (h t) -> p h t", h=HB), scalar=KSCALE,
                    in1=wexp[0:rows, :, 0:rows], op0=ALU.mult, op1=ALU.mult).then_inc(tile_w.sem, 1)
                if n == 2:
                    dve.wait_ge(inter_mm.sem, inter_mm.by(L, 1))
                    sel_b = bcast(bmask[0:TS, :].rearrange("p (o b) -> p o b", o=1), 1, HB)
                    tmp = small[0:TS, 32:64].rearrange("p (h b) -> p h b", h=HB)
                    tt(tmp, bank[6][0:TS, 0:HB * SB].rearrange("p (h b) -> p h b", h=HB), sel_b, ALU.mult)
                    dve.drain()
                    dve.tensor_reduce(small[0:TS, 20:24], tmp, AX_X, ALU.add)
                    dve.drain()
                dve.wait_ge(num_ready.sem, num_ready.by(L, n + 1))
                if n == 2:
                    tt(num[0:rows, :, DK], num[0:rows, :, DK], small[0:rows, 20:24], ALU.add)
                    dve.drain()
                if n < 2:
                    dve.wait_ge(cadd_mm.sem, cadd_mm.by(L, n + 1))
                    for h in range(HB):
                        add = bank[5 + h // 2][:, (h % 2) * (DK + 1):(h % 2 + 1) * (DK + 1)]
                        if n == 0:
                            last = dve.tensor_copy(Caug[:, h, :], add)
                        else:
                            last = stt(out=Caug[:, h, :], in0=Caug[:, h, :], scalar=rexp[:, h, P - 1:P], in1=add,
                                       op0=ALU.mult, op1=ALU.add)
                    last.then_inc(caug_ready.sem, 1)
                den = num[0:rows, :, DK]
                s4 = lambda i: small[0:rows, 4 * i:4 * i + 4]
                wide = lambda i: bcast(s4(i).rearrange("p (h o) -> p h o", o=1), 2, DK)
                stt(out=s4(0), in0=den, scalar=-1.0, in1=den, op0=ALU.mult, op1=ALU.max)
                dve.drain()
                tt(s4(0), s4(0), cols[0:rows, n, 2, :], ALU.max)
                dve.drain()
                dve.reciprocal(s4(0), s4(0))
                dve.drain()
                if n:
                    dve.wait_ge(h_turned.sem, h_turned.by(L, n))
                tt(hc[0:rows, :, :], num[0:rows, :, 0:DK], wide(0), ALU.mult)
                dve.drain()
                dve.tensor_reduce(s4(1), hc[0:rows, :, :], AX_X, ALU.add)
                dve.drain()
                ts(s4(1), s4(1), 1.0 / DK, None, ALU.mult)
                dve.drain()
                tt(hc[0:rows, :, :], hc[0:rows, :, :], wide(1), ALU.subtract)
                dve.drain()
                tt(hsq[0:rows, :, :], hc[0:rows, :, :], hc[0:rows, :, :], ALU.mult)
                dve.drain()
                dve.tensor_reduce(s4(2), hsq[0:rows, :, :], AX_X, ALU.add)
                dve.drain()
                ts(s4(3), s4(2), 1.0 / DK, MH_EPS, ALU.mult, ALU.add).then_inc(hvar_ready.sem, 1)
                dve.wait_ge(hsd_ready.sem, hsd_ready.by(L, n + 1))
                dve.reciprocal(s4(4), s4(4))
                dve.drain()
                tt(hc[0:rows, :, :], hc[0:rows, :, :], wide(4), ALU.mult).then_inc(h_ready.sem, 1)
                dve.wait_ge(h_turned.sem, h_turned.by(L, n + 1))
                tt(yb_new[:, :, at:at + rows], bank[7][:, 0:HB * rows].rearrange("p (h t) -> p h t", h=HB),
                   og[:, :, at:at + rows], ALU.mult).then_inc(yb_ready.sem, 1)
            dve.wait_ge(c0_decayed.sem, c0_decayed.by(L, 1))
            for h in range(HB):
                for half in range(2):
                    i = 2 * h + half
                    dve.wait_ge(cs_mm.sem, cs_mm.by(L, i + 1))
                    mem = C0[:, 4 * half:4 * half + 4, h, :]
                    tt(mem, mem, bank[i % 4][:, :].rearrange("p (b e) -> p b e", b=4),
                       ALU.add).then_inc(cs_ready.sem, 1)
            dve.wait_ge(ns_mm.sem, ns_mm.by(L, 1))
            dve.tensor_copy(nout[:, 0:HB], Caug[:, :, DK])
            nb = nout[:, HB:HB + SB * HB].rearrange("p (b h) -> p b h", b=SB)
            dec = rexp[:, :, :].rearrange("p h t -> p (h t)")[:, 0:HB * TS].rearrange(
                "p (h b t) -> p b h t", h=HB, t=ST)[:, :, :, ST - 1]
            tt(nb, n0[:, :, :], dec, ALU.mult)
            dve.drain()
            tt(nb, nb, bank[6][:, 0:HB * SB].rearrange("p (h b) -> p b h", h=HB), ALU.add).then_inc(
                nout_ready.sem, 1)
            dve.wait_ge(c_out.sem, c_out.by(L, 64))
            dve.tensor_copy(yb[:, :, :], yb_new[:, :, :]).then_inc(yb_moved.sem, 1)
            cur = proj[:, TR:NIN, :]
            tt(rm[:, :, 0:TP], cur[:, :, LEAD - 1:LEAD - 1 + TP], cur[:, :, LEAD:LEAD + TP], ALU.subtract)
            tt(seqs(rm[:, :, TP:T]), hist(cur)[:, :, :, LEAD - 1:SEG - 1], hist(cur)[:, :, :, LEAD:SEG],
               ALU.subtract)
            dve.drain()
            for n in range(NRW):
                mu = vec[:, V_MU + n:V_MU + n + 1]
                stt(out=rm[:, n, 0:TP], in0=rm[:, n, 0:TP], scalar=mu, in1=cur[:, n, LEAD:LEAD + TP],
                    op0=ALU.mult, op1=ALU.add)
                last = stt(out=seqs(rm[:, n, TP:T]), in0=seqs(rm[:, n, TP:T]), scalar=mu,
                           in1=hist(cur[:, n, :])[:, :, LEAD:SEG], op0=ALU.mult, op1=ALU.add)
            last.then_inc(shift_ready.sem, 1)
            dve.drain()
            r, k, v = rm[:, 0:NJ, :], rm[:, NJ:2 * NJ, :], rm[:, 2 * NJ:3 * NJ, :]
            flat = lambda t: t.rearrange("p j t -> p (j t)")
            col = lambda at, j: vec[:, at + j:at + j + 1]
            for j in range(NJ):
                last = ts(kk[:, j, :], k[:, j, :], col(V_KK, j), None, ALU.mult)
            last.then_inc(kk_raw.sem, 1)
            dve.wait_ge(lora_ready.sem, lora_ready.by(L, 1))
            ts(flat(lw[:, :, :]), flat(lw[:, :, :]), -E_HALF, None, ALU.mult)
            for j in range(NJ):
                ts(kn[:, j, :], aa[:, j, :], -1.0, col(V_KA, j), ALU.add, ALU.mult)
            dve.drain()
            stt(out=flat(kn[:, :, :]), in0=flat(kn[:, :, :]), scalar=1.0, in1=flat(k), op0=ALU.add, op1=ALU.mult)
            for j in range(NJ):
                dve.tensor_tensor_scan(cum[:, j, :], keep64[:, :], lw[:, j, :], 0.0, ALU.mult, ALU.add)
            dve.drain()
            for j in range(NJ):
                last = stt(out=e2[:, j, :], in0=r[:, j, :], scalar=col(V_RK, j), in1=kn[:, j, :],
                           op0=ALU.mult, op1=ALU.mult)
            last.then_inc(rk_ready.sem, 1)
            dve.wait_ge(kk_mm.sem, kk_mm.by(L, 1))
            for j in range(NJ):
                last = ts(e1[:, j, :], bank[4 + j][:, 0:T], 1e-24, None, ALU.max)
            last.then_inc(kk_norm2.sem, 1)
            dve.wait_ge(kk_norm.sem, kk_norm.by(L, 1))
            dve.reciprocal(flat(e1[:, :, :]), flat(e1[:, :, :]))
            dve.drain()
            stt(out=flat(kk[:, :, :]), in0=flat(kk[:, :, :]), scalar=-1.0, in1=flat(e1[:, :, :]), op0=ALU.mult,
                op1=ALU.mult).then_inc(cum_ready.sem, 1)
            dve.wait_ge(rk_mm.sem, rk_mm.by(L, 1))
            tt(e2[:, :, :], cum[:, :, :], lw[:, :, :], ALU.subtract).then_inc(cumx_ready.sem, 1)
            dve.drain()
            stt(out=flat(aa[:, :, :]), in0=flat(kk[:, :, :]), scalar=-1.0, in1=flat(aa[:, :, :]), op0=ALU.mult,
                op1=ALU.mult)
            halves = [(q, slice(q * CH, (q + 1) * CH)) for q in range(2)]
            chunks = lambda t: t.rearrange("p j (c t) -> p j c t", t=CH)
            dve.wait_ge(exp_ready.sem, exp_ready.by(L, 1))
            dve.wait_ge(pads_zero.sem, pads_zero.by(L, 1))
            for q, part in halves:
                tt(ar[part, :, :, q, 1, :], chunks(r[part]), chunks(e1[part, :, :]), ALU.mult)
            dve.tensor_copy(dlast[:, :, 0:NPC], e1[:, :, CH - 1:TP:CH])
            dve.tensor_copy(dlast[:, :, NPC:NPC + SB], e1[:, :, TP + ST - 1:T:ST])
            dve.wait_ge(exp_ready.sem, exp_ready.by(L, 2))
            for q, part in halves:
                last = tt(ar[part, :, :, q, 0, :], chunks(kk[part, :, :]), chunks(e2[part, :, :]), ALU.mult)
            last.then_inc(at_ready.sem, 1)
            for q, part in halves:
                dve.tensor_copy(zv[part, :, :, 1 - q, :], chunks(v[part]))
            dve.wait_ge(exp_ready.sem, exp_ready.by(L, 3))
            for q, part in halves:
                tt(bk[part, :, :, q, :], chunks(aa[part, :, :]), chunks(e2[part, :, :]), ALU.mult)
                last = tt(bk[part, :, :, 1 - q, :], chunks(kn[part, :, :]), chunks(e2[part, :, :]), ALU.mult)
            last.then_inc(ab_ready.sem, 1)
            dve.drain()
            dve.wait_ge(lora_ready.sem, lora_ready.by(L, 2))
            two = lambda t: t.rearrange("p j c s t -> p j c (s t)")
            tt(two(bkh[:, :, 0:NPC, :, :]), two(bk[:, :, 0:NPC, :, :]),
               bcast(dlast[:, :, 0:NPC].rearrange("p j (c o) -> p j c o", o=1), 3, 2 * CH), ALU.mult)
            for s in range(2):
                tt(seqs(bkh[:, :, NPC, s, :]), seqs(bk[:, :, NPC, s, :]),
                   bcast(dlast[:, :, NPC:NPC + SB].rearrange("p j (c o) -> p j c o", o=1), 3, ST), ALU.mult)
            for j in range(NJ):
                last = tt(bonus[:, j, :], bank[4 + j][:, 0:T], v[:, j, :], ALU.mult)
            last.then_inc(bonus_read.sem, 1)
            dve.drain()
            for c in range(NCH):
                for g in range(2):
                    dve.wait_ge(score_mm.sem, score_mm.by(L, 2 * c + g + 1))
                    tri = scmask[:, 0 if c < NPC else 1, :, :].rearrange("p (o s) t -> p o (s t)", o=1)
                    tt(scores[:, c, 2 * g:2 * g + 2, :, :, :].rearrange("p j q s t -> p (j q) (s t)"),
                       bank[(2 * c + g) % 4][:, :].rearrange("p (i s) -> p i s", i=4), bcast(tri, 1, 4),
                       ALU.mult).then_inc(score_ready.sem, 1)
            dve.wait_ge(t1_zero.sem, t1_zero.by(L, 1))
            for n, (lv, c) in enumerate(LEVELS):
                dve.wait_ge(t1_mm.sem, t1_mm.by(L, n + 1))
                for q, part in halves:
                    m = bcast(lvmask[part, lv, :].rearrange("p (o t) -> p o t", o=1), 1, NJ)
                    last = tt(t1[part, c, :, part], bank[n % 2][part, :].rearrange("p (j s) -> p j s", j=NJ)[
                        :, :, part], m, ALU.mult)
                last.then_inc(t1_ready.sem, 1)
            for c in range(NCH):
                dve.wait_ge(u_mm.sem, u_mm.by(L, c + 1))
                for q, part in halves:
                    last = dve.tensor_copy(uv[part, c, :, q, :],
                                           bank[1][part, 0:NJ * NA].rearrange("p (j v) -> p j v", j=NJ))
                last.then_inc(u_ready.sem, 1)
                if c < NPC:
                    dve.wait_ge(s_mm.sem, s_mm.by(L, c + 1))
                    add = bank[3][:, 0:NJ * NA].rearrange("p (j v) -> p j v", j=NJ)
                    if c == 0:
                        last = dve.tensor_copy(state[:, 1, :, :], add)
                    else:
                        last = tt(state[:, (c + 1) % 2, :, :], sdec[:, :, :], add, ALU.add)
                    last.then_inc(s_ready.sem, 1)
                    if c + 1 < NPC:
                        dve.drain()
                        tt(sdec[:, :, :], state[:, (c + 1) % 2, :, :],
                           bcast(dlast[:, :, c + 1:c + 2], 2, NA), ALU.mult)
                        dve.drain()
            dve.drain()
            for b in range(SB):
                last = ts(uvm[:, b, :, :, :].rearrange("p j q v -> p (j q v)"),
                          uv[:, NPC, :, :, :].rearrange("p j q v -> p (j q v)"), bmask[:, b:b + 1], None, ALU.mult)
            last.then_inc(uvm_ready.sem, 1)
            dve.wait_ge(y_ready.sem, y_ready.by(L, NCH))
            hd = lambda t: t[:, :, :, :].rearrange("p c j v -> p (c j) v")
            st = lambda i: bcast(gnst[:, i, :].rearrange("p (n o) -> p n o", o=1), 2, NA)
            dve.tensor_reduce(gnst[:, 0, :], hd(yr), AX_X, ALU.add)
            dve.drain()
            ts(gnst[:, 0, :], gnst[:, 0, :], 1.0 / NA, None, ALU.mult)
            dve.drain()
            tt(hd(yc), hd(yr), st(0), ALU.subtract)
            dve.drain()
            tt(hd(ysq), hd(yc), hd(yc), ALU.mult)
            dve.drain()
            dve.tensor_reduce(gnst[:, 1, :], hd(ysq), AX_X, ALU.add)
            dve.drain()
            ts(gnst[:, 1, :], gnst[:, 1, :], 1.0 / NA, GN_EPS, ALU.mult, ALU.add).then_inc(gvar_ready.sem, 1)
            dve.wait_ge(s0_decayed.sem, s0_decayed.by(L, 1))
            for j in range(NJ):
                dve.wait_ge(ss_mm.sem, ss_mm.by(L, j + 1))
                last = tt(snew[:, :, j, :], s0[:, :, j, :], bank[4 + j][:, :].rearrange("p (b v) -> p b v", b=SB),
                          ALU.add)
            last.then_inc(snew_ready.sem, 1)
            dve.wait_ge(gsd_ready.sem, gsd_ready.by(L, 1))
            dve.reciprocal(gnst[:, 1, :], gnst[:, 1, :])
            dve.drain()
            tt(hd(yc), hd(yc), st(1), ALU.mult).then_inc(yn_ready.sem, 1)
            dve.wait_ge(y_back.sem, y_back.by(L, 1))
            for j in range(NJ):
                stt(out=ya[:, j, :], in0=bank[j][:, 0:T], scalar=col(V_GG, j), in1=bonus[:, j, :], op0=ALU.mult,
                    op1=ALU.add)
            dve.drain()
            for j in range(NJ):
                last = stt(out=ya[:, j, :], in0=ya[:, j, :], scalar=col(V_GB, j), in1=gg[:, j, :], op0=ALU.add,
                           op1=ALU.mult)
            last.then_inc(ya_ready.sem, 1)
            dve.wait_ge(mix_hi.sem, mix_hi.by(L, 1))
            tt(xl[:, 0:NJ, :], ya[:, :, :], xh[:, 0:NJ, :].bitcast(F32), ALU.subtract)
            tt(xl[:, NJ:KT, :], yb[:, :, :], xh[:, NJ:KT, :].bitcast(F32), ALU.subtract).then_inc(mix_ready.sem, 1)

        def make_constants(pool):
            def ms(t, value):
                pool.memset(t, value)
                pool.drain()

            def sel_(**how):
                pool.affine_select(**how)
                pool.drain()

            for t, val in ((ident[:, :], 0.0), (ones[:, :], 1.0), (headones[:, :], 0.0), (scmask[:, :, :, :], 1.0),
                           (lvmask[:, :, :], 0.0), (negmask[:, :, :], 0.0), (bmask[:, :], 1.0), (keep64[:, :], 1.0),
                           (keep128[:, :], 1.0), (segneg[:, :], 0.0), (sel[:, :, :], 1.0)):
                ms(t, val)
            sel_(out=ident[:, :], in_=ident[:, :], compare_op=ALU.not_equal, fill=1.0, base=0, pattern=[[-1, P]],
                 channel_multiplier=1)
            for q in range(2):
                part = slice(q * CH, (q + 1) * CH)
                ms(headones[part, part], 1.0)
                for kind in range(2):
                    for incl in range(2):
                        m = scmask[part, kind, incl, :]
                        sel_(out=m, in_=m, compare_op=ALU.is_ge, fill=0.0, base=incl - 1, pattern=[[1, CH]],
                             channel_multiplier=-1)
                for lv in range(6):
                    b = 1 << lv
                    m = lvmask[part, lv, :].rearrange("p (g s t) -> p g s t", s=2, t=b)[:, :, 0, :]
                    ms(m, 1.0)
                bm = bmask[part, :]
                sel_(out=bm, in_=bm, compare_op=ALU.is_ge, fill=0.0, base=0, pattern=[[-ST, SB]],
                     channel_multiplier=1)
            for q in range(2):
                part = slice(q * CH, (q + 1) * CH)
                bm = bmask[part, :]
                sel_(out=bm, in_=bm, compare_op=ALU.is_ge, fill=0.0, base=ST - 1, pattern=[[ST, SB]],
                     channel_multiplier=-1)
                for incl in range(2):
                    m = seqs(scmask[part, 1, incl, :])
                    sel_(out=m, in_=m, compare_op=ALU.is_ge, fill=0.0, base=0, pattern=[[-ST, SB], [0, ST]],
                         channel_multiplier=1)
                for lv in range(6):
                    b = 1 << lv
                    m = lvmask[part, lv, :].rearrange("p (g s t) -> p g s t", s=2, t=b)[:, :, 0, :]
                    n = CH // (2 * b)
                    sel_(out=m, in_=m, compare_op=ALU.is_ge, fill=0.0, base=-b, pattern=[[-2 * b, n], [0, b]],
                         channel_multiplier=1)
            m = negmask[:, 0, :]
            sel_(out=m, in_=m, compare_op=ALU.is_ge, fill=NEG, base=0, pattern=[[1, P]], channel_multiplier=-1)
            m = negmask[0:TS, 1, 0:TS]
            sel_(out=m, in_=m, compare_op=ALU.is_ge, fill=NEG, base=0, pattern=[[1, TS]], channel_multiplier=-1)
            for h in range(HB):
                m = sel[:, h, :]
                sel_(out=m, in_=m, compare_op=ALU.is_equal, fill=0.0, base=-h, pattern=[[0, P]],
                     channel_multiplier=1)
            ms(keep64[:, 0:TP:CH], 0.0)
            ms(keep64[:, TP:T:ST], 0.0)
            ms(keep128[:, 0:TP:P], 0.0)
            ms(keep128[:, TP:T:ST], 0.0)
            ms(segneg[:, 0:TS:ST], NEG)
            for q in range(2):
                part = slice(q * CH, (q + 1) * CH)
                for lv in range(6):
                    b = 1 << lv
                    m = lvmask[part, lv, :].rearrange("p (g s t) -> p g s t", s=2, t=b)[:, :, 0, :]
                    sel_(out=m, in_=m, compare_op=ALU.is_ge, fill=0.0, base=2 * b - 1,
                         pattern=[[2 * b, CH // (2 * b)], [0, b]], channel_multiplier=-1)
            m = seqs(negmask[0:TS, 1, 0:TS])
            sel_(out=m, in_=m, compare_op=ALU.is_ge, fill=NEG, base=0, pattern=[[-ST, SB], [0, ST]],
                 channel_multiplier=1)
            for q in range(2):
                part = slice(q * CH, (q + 1) * CH)
                for lv in range(6):
                    m = lvmask[part, lv, :]
                    sel_(out=m, in_=m, compare_op=ALU.not_equal, fill=1.0, base=0, pattern=[[-1, CH]],
                         channel_multiplier=1)
            pool.nop().then_inc(consts.sem, 1)

        def start_layer(pool, L):
            at = 0
            lay = lambda w: w[bass.ds(L, 1)]
            for name, n in (("mu_shift", NRW), ("w0", NJ), ("a0", NJ), ("k_k", NJ), ("k_a", NJ), ("r_k", NJ),
                            ("gn_g", NJ), ("gn_b", NJ), ("mh_g", NJ), ("conv_b", NQK), ("conv_w", CW * NQK)):
                w = lay(I[name])
                if name == "r_k":
                    src = w.rearrange("l (j h) n -> (l j) (h n)", h=2)
                elif name == "conv_w":
                    src = w.rearrange("l c (n p) -> (l c n) p", p=P)
                else:
                    src = w.rearrange("l (n p) -> (l n) p", p=P)
                pool.dma_start(vrow1[at:at + n, :], src).then_inc(vrows_in.sem, 16)
                at += n
            assert at == NV1
            for i, name in enumerate(("ln1_g", "ln1_b", "ln2_g", "ln2_b", "ln3_g", "ln3_b")):
                pool.dma_start(vrow2[i * KT:(i + 1) * KT, :], lay(I[name]).rearrange(
                    "l (n p) -> (l n) p", p=P)).then_inc(vrows_in.sem, 16)
            pool.dma_start(hist_shift[:, :], lay(I["state_shift"]).rearrange("l b c -> (l b) c")).then_inc(
                hist_in.sem, 16)
            pool.dma_start(hist_conv[:, :], lay(I["state_conv"]).rearrange("l b j c -> (l b j) c")).then_inc(
                hist_in.sem, 16)

        def pool_mixers(pool, L):
            lay = lambda w: w[bass.ds(L, 1)]
            dma = pool.dma_start
            pool.memset(proj[:, :, 0:LEAD], 0.0).then_inc(leads_zero.sem, 1)
            pool.memset(gatew[:, :, :], 0.0)
            pool.drain()
            for q, at in enumerate((0, 32)):
                src = lay(I["w_in"])[:, :, GCOL + q * HB:GCOL + (q + 1) * HB].rearrange(
                    "l (k p) n -> p (l k) n", p=P)
                dma(gatew[:, :, at:at + HB], src).then_inc(gatew_in.sem, 16)
            for q, name in enumerate(("i_bias", "f_bias")):
                dma(gbias[:, q:q + 1], lay(I[name]).rearrange("l h -> h l")).then_inc(gatew_in.sem, 16)
            pool.wait_ge(hist_ready.sem, hist_ready.by(L, 1))
            carry(pool)
            dma(lim[:, 8:8 + SB], lay(I["state_m"]).rearrange("l b h -> h (l b)"),
                allow_slow_non_contiguous=True).then_inc(m_in.sem, 16)
            pool.wait_ge(tail_ready.sem, tail_ready.by(L, 1))
            carry(pool)
            nc_ = LEAD
            dma(lay(O["p_conv"]).rearrange("l b j c -> (l b j) c"), tail[0:nc_, 0:2 * DB]).then_inc(tail_out.sem, 16)
            dma(lay(O["s_conv"]).rearrange("l b j c -> (l b j) c"), tail[nc_:nc_ * (SB + 1), 0:2 * DB]).then_inc(
                tail_out.sem, 16)
            dma(lay(O["p_shift"]).rearrange("l b c -> (l b) c"), tail[0:1, 2 * DB:2 * DB + RCOLS]).then_inc(
                tail_out.sem, 16)
            dma(lay(O["s_shift"]).rearrange("l b c -> (l b) c"), tail[1:SB + 1, 2 * DB:2 * DB + RCOLS]).then_inc(
                tail_out.sem, 16)
            pool.wait_ge(tail_out.sem, tail_out.by(L, 64))
            pool.wait_ge(gates_mm.sem, gates_mm.by(L, 1))
            carry(pool)
            dma(C0[:, :, :, :].rearrange("d b h e -> d (b h) e"),
                lay(I["state_C"]).rearrange("l b h d e -> d (l b h) e")).then_inc(c0_in.sem, 16)
            dma(nrow[0:SB * HB, :], lay(I["state_n"]).rearrange("l b h d -> (l b h) d")).then_inc(c0_in.sem, 16)
            pool.wait_ge(kv_ready.sem, kv_ready.by(L, NTT))
            carry(pool)
            for b in range(SB):
                last = pool.tensor_scalar(vmask[:, b, :, :], va[0:TS, 2, :, 0:DK], bmask[0:TS, b:b + 1], None,
                                          ALU.mult)
            last.then_inc(vmask_ready.sem, 1)
            pool.wait_ge(rows_ready.sem, rows_ready.by(L, 1))
            carry(pool)
            dma(lay(O["p_m"]).rearrange("l b h -> h (l b)"), lim[:, 1:2],
                allow_slow_non_contiguous=True).then_inc(m_out.sem, 16)
            dma(lay(O["s_m"]).rearrange("l b h -> h (l b)"), lim[:, 16:16 + SB],
                allow_slow_non_contiguous=True).then_inc(m_out.sem, 16)
            pool.wait_ge(inter_mm.sem, inter_mm.by(L, 1))
            dec = rexp[:, :, :].rearrange("p h t -> p (h t)")[:, 0:HB * TS].rearrange(
                "p (h b t) -> p b h t", h=HB, t=ST)[:, :, :, ST - 1:ST]
            for b in range(SB):
                last = pool.tensor_tensor(C0[:, b, :, :], C0[:, b, :, :], bcast(dec[:, b, :, :], 2, DK), ALU.mult)
            last.then_inc(c0_decayed.sem, 1)
            pool.wait_ge(cs_ready.sem, cs_ready.by(L, 2 * HB))
            pool.wait_ge(nrow_ready.sem, nrow_ready.by(L, 1))
            carry(pool)
            dma(lay(O["s_C"]).rearrange("l b h d e -> d (l b h) e"),
                C0[:, :, :, :].rearrange("d b h e -> d (b h) e")).then_inc(c_out.sem, 16)
            dma(lay(O["p_C"]).rearrange("l b h d e -> d (l b h) e"), Caug[:, :, 0:DK]).then_inc(c_out.sem, 16)
            dma(lay(O["p_n"]).rearrange("l b h d -> (l b h) d"), nrow[0:HB, :]).then_inc(c_out.sem, 16)
            dma(lay(O["s_n"]).rearrange("l b h d -> (l b h) d"), nrow[HB:HB + SB * HB, :]).then_inc(c_out.sem, 16)
            pool.memset(ar[:, :, :, :, :, :], 0.0)
            pool.wait_ge(m_out.sem, m_out.by(L, 32))
            pool.wait_ge(c_out.sem, c_out.by(L, 64))
            pool.wait_ge(yb_moved.sem, yb_moved.by(L, 1))
            carry(pool)
            pool.memset(w2p[RW:P, :], 0.0)
            pool.drain()
            pool.memset(a2p[0:P - RW, :], 0.0)
            pool.drain()
            dma(w2p[0:RW, :], lay(I["w2"]).rearrange("l r n -> (l r) n")).then_inc(lora_in.sem, 16)
            dma(a2p[P - RW:P, :], lay(I["a2"]).rearrange("l r n -> (l r) n")).then_inc(lora_in.sem, 16)
            dma(g2s[:, :], lay(I["g2"]).rearrange("l r n -> (l r) n")).then_inc(lora_in.sem, 16)
            pool.memset(ati[:, :, :, :], 0.0)
            pool.wait_ge(shift_ready.sem, shift_ready.by(L, 1))
            carry(pool)
            pool.memset(zv[:, :, :, :, :], 0.0).then_inc(pads_zero.sem, 1)
            pool.drain()
            for c in range(NCH):
                pool.wait_ge(score_ready.sem, score_ready.by(L, 2 * c + 2))
                for q in range(2):
                    part = slice(q * CH, (q + 1) * CH)
                    one = bcast(ident[part, part].rearrange("p (o t) -> p o t", o=1), 1, NJ)
                    last = pool.tensor_tensor(ati[part, c, :, part], scores[part, c, :, q, 0, :], one, ALU.add)
                last.then_inc(ati_ready.sem, 1)
            pool.drain()
            pool.memset(t1[:, :, :, :], 0.0).then_inc(t1_zero.sem, 1)
            pool.wait_ge(x_copied.sem, x_copied.by(L, NSTEP))
            carry(pool)
            dma(wkv_rows[:, :, :, :, :].rearrange("v b j q k -> v (b j q) k"),
                lay(I["state_wkv"]).rearrange("l b h v k -> v (l b h) k")).then_inc(wkv_in.sem, 16)
            pool.wait_ge(s0_mm.sem, s0_mm.by(L, 1))
            for b in range(SB):
                last = pool.tensor_tensor(s0[:, b, :, :], s0[:, b, :, :],
                                          bcast(dlast[:, :, NPC + b:NPC + b + 1], 2, NA), ALU.mult)
            last.then_inc(s0_decayed.sem, 1)
            pool.wait_ge(sw_ready.sem, sw_ready.by(L, SB + 1))
            carry(pool)
            dma(lay(O["p_wkv"]).rearrange("l b h v k -> v (l b h) k"),
                pwkv_out[:, :, :, :].rearrange("v j q k -> v (j q) k")).then_inc(wkv_left.sem, 16)
            dma(lay(O["s_wkv"]).rearrange("l b h v k -> v (l b h) k"),
                wkv_out[:, :, :, :, :].rearrange("v b j q k -> v (b j q) k")).then_inc(wkv_left.sem, 16)
            pool.wait_ge(wkv_left.sem, wkv_left.by(L, 32))

        def each(eng, first, count, body):
            turns = (count - (steps_of[first + count - 1] > 1)) // RS
            if turns > 1:
                with eng.Fori(0, turns) as i:
                    for u in range(RS):
                        body(first + u, i)
            else:
                for u in range(RS * turns):
                    body(first + u, 0)
            for u in range(RS * turns, count):
                body(first + u, 0)

        @block.sync
        def _(sp):
            tok = [I["x_prompt"][0, 0:P, :], I["x_prompt"][0, P:2 * P, :],
                   I["x_sample"].rearrange("b t d -> (b t) d")]
            for n, (_, rows) in enumerate(TT):
                sp.dma_start(xrows[0:rows, n, :], tok[n]).then_inc(rows_in.sem, 16)
            with sp.Fori(0, DEPTH) as L:

                def load(p, i, src):
                    dst = raw[:, p % RS, :].rearrange("p (k n) -> p k n", n=src.shape[-1])
                    sp.wait_ge(lo_ready.sem, lo_ready.by(L, RS * i + max(0, p - RS + 1)))
                    sp.dma_start(dst, src).then_inc(raw_in[p % RS].sem, 16)

                def columns(w, col, n=P):
                    return w[bass.ds(L, 1), :, bass.ds(col, n)].rearrange("l (k p) n -> p (l k) n", p=P)

                def ffn(base, wg, wu, wd):
                    def up(p, i):
                        d = p - base
                        src = columns(wg if d % 2 == 0 else wu, (i * (RS // 2) + d // 2) * P)
                        load(p, i, src)
                    each(sp, base, NUP, up)
                    for half in range(2):
                        first = base + NUP + half * NDN

                        def down(p, i):
                            src = wd[bass.ds(L, 1), bass.ds((i * RS + (p - first)) * 2 * P, 2 * P),
                                     half * 4 * P:(half + 1) * 4 * P]
                            load(p, i, src.rearrange("l (k p) n -> p (l k) n", p=P))
                        each(sp, first, NDN, down)

                ffn(U1, I["ffn1_wg"], I["ffn1_wu"], I["ffn1_wd"])
                each(sp, WI, TR, lambda p, i: load(p, i, columns(I["w_in"], (i * RS + (p - WI)) * P + RCOLS)))
                each(sp, WI + TR, NRW, lambda p, i: load(p, i, columns(I["w_in"], (i * RS + (p - WI - TR)) * P)))
                each(sp, WO, KT, lambda p, i: load(p, i, columns(I["w_out"], (i * RS + (p - WO)) * P)))
                ffn(U2, I["ffn2_wg"], I["ffn2_wu"], I["ffn2_wd"])
            for n, (at, rows) in enumerate(TT):
                sp.wait_ge(end_low.sem, n + 1)
                sp.wait_ge(end_high.sem, n + 1)
                dst = (O["y_prompt"][0, at:at + rows, :] if n < 2 else O["y_sample"].rearrange("b t d -> (b t) d"))
                sp.dma_start(dst, xrows[0:rows, n, :]).then_inc(y_out.sem, 16)
            sp.wait_ge(y_out.sem, 16 * NTT)

        def three_passes(pe, out, slot, at, hi, lo, start, stop):
            w_hi, w_lo = whi[:, slot, at:at + P], wlo[:, slot, at:at + P]
            pe.matmul(out, w_hi, hi, start=start, stop=False)
            pe.matmul(out, w_hi, lo, start=False, stop=False)
            return pe.matmul(out, w_lo, hi, start=False, stop=stop)

        @block.tensor
        def _(pe):
            pe.wait_ge(consts.sem, 1)
            pe.wait_ge(rows_in.sem, 16 * NTT)
            for k in range(KT):
                for n, (at, rows) in enumerate(TT):
                    last = pe.transpose(bank[k][:, at:at + rows], xrows[0:rows, n, k * P:(k + 1) * P],
                                        ident[0:rows, 0:rows])
                last.then_inc(x_turned.sem, 1)
            with pe.Fori(0, DEPTH) as L:

                def chunk_of_columns(p, i, out):
                    pe.wait_ge(lo_ready.sem, lo_ready.by(L, RS * i + p + 1))
                    for k in range(KT):
                        last = three_passes(pe, out, p % RS, k * P, xh[:, k, :], xl[:, k, :], k == 0, k == KT - 1)
                    last.then_inc(used.sem, steps_of[p])

                def ln_sums(first, last, which):
                    for o in range(first, last):
                        pe.wait_ge(z_ready.sem, z_ready.by(L, which * KT + o + 1))
                        pe.matmul(bank[4][:, 0:T], ones[:, :], z[:, o, :], start=(o == 0), stop=(o == KT - 1))
                        pe.wait_ge(sq_ready.sem, sq_ready.by(L, which * KT + o + 1))
                        mm = pe.matmul(bank[5][:, 0:T], ones[:, :], sq[:, o, :], start=(o == 0), stop=(o == KT - 1))
                    if last == KT:
                        mm.then_inc(stats_ready.sem, 1)

                def ffn(base, f, which):
                    def up(p, i):
                        d = p - base
                        if d == 0:
                            pe.wait_ge(x_ready.sem, x_ready.by(L, KT * 2 * f))
                        if d % 2 == 0:
                            pe.wait_ge(up_done.sem, up_done.by(L, f * NFF + (RS // 2) * i + d // 2 - 1))
                        chunk_of_columns(p, i, bank[d % RS][:, 0:T])
                    each(pe, base, NUP, up)
                    if f == 0:
                        pe.wait_ge(vrows_in.sem, vrows_in.by(L, 16 * 17))
                        pe.transpose(bank[7][:, 0:NV1], vrow1[0:NV1, :], ident[0:NV1, 0:NV1])
                        pe.transpose(bank[7][:, NV1:NV1 + NV2], vrow2[0:NV2, :],
                                     ident[0:NV2, 0:NV2]).then_inc(vec_turned.sem, 1)
                        pe.wait_ge(vec_ready.sem, vec_ready.by(L, 1))
                    for half in range(2):
                        first = base + NUP + half * NDN
                        banks = [bank[4 * (1 - half) + o][:, 0:T] for o in range(4)]
                        if half:
                            pe.wait_ge(up_done.sem, up_done.by(L, (f + 1) * NFF))

                        def down(p, i, c=None):
                            pe.wait_ge(lo_ready.sem, lo_ready.by(L, RS * i + p + 1))
                            if half == 0:
                                pe.wait_ge(hl_done.sem, hl_done.by(L, f * NFF + 2 * RS * i + 2 * (p - first) + 2))
                            for k2 in range(2):
                                k = 2 * RS * i + 2 * (p - first) + k2
                                for o in range(4):
                                    hid = lambda t: (t[:, k, :] if isinstance(i, int) else
                                                     t[:, bass.ds(k, 1), :].rearrange("p k t -> p (k t)"))
                                    last = three_passes(
                                        pe, banks[o], p % RS, (4 * k2 + o) * P, hid(hh), hid(hl),
                                        p == first and k2 == 0, p == first + NDN - 1 and k2 == 1)
                            last.then_inc(used.sem, steps_of[p])
                        down(first, 0)
                        each(pe, first + 1, 2 * RS, down)
                        if half:
                            ln_sums(0, 4, which)
                        down(first + 2 * RS + 1, 0)
                        down(first + 2 * RS + 2, 0)
                    ln_sums(4, KT, which)

                ffn(U1, 0, 0)

                pe.wait_ge(hist_in.sem, hist_in.by(L, 32))
                for n in range(NRW):
                    turn(pe, bank[6][:, n * SB:(n + 1) * SB], hist_shift[:, n * P:(n + 1) * P])
                for n in range(NQK):
                    last = turn(pe, bank[7][:, n * 24:(n + 1) * 24], hist_conv[:, n * P:(n + 1) * P])
                last.then_inc(hist_turned.sem, 1)

                def in_tile(p, i):
                    if p == WI:
                        pe.wait_ge(x_ready.sem, x_ready.by(L, KT))
                    pe.wait_ge(proj_ready.sem, proj_ready.by(L, RS * i + (p - WI) - RS + 1))
                    chunk_of_columns(p, i, bank[(p - WI) % RS][:, 0:T])
                each(pe, WI, NIN, in_tile)
                tensor_mixers(pe, L)

                pe.wait_ge(mix_ready.sem, mix_ready.by(L, 1))
                for p in range(WO, WO + KT):
                    if p - WO >= 4:
                        pe.wait_ge(z_ready.sem, z_ready.by(L, KT + p - WO - 3))
                    chunk_of_columns(p, 0, bank[(p - WO) % 4][:, 0:T])
                ln_sums(0, KT, 1)
                ffn(U2, 1, 2)
            pe.wait_ge(x_ready.sem, KT + DEPTH * 3 * KT)
            for n, (at, rows) in enumerate(TT):
                for half in range(2):
                    for k in range(4):
                        last = pe.transpose(bank[2 * n + half][0:rows, k * P:(k + 1) * P],
                                            x[:, 4 * half + k, at:at + rows], ident[:, :])
                    last.then_inc(end_turned.sem, 1)

        @block.scalar
        def _(act):
            act.wait_ge(consts.sem, 1)
            for k in range(KT):
                act.wait_ge(x0_ready.sem, k + 1)
                act.activation(xh[:, k, :], x[:, k, :], ACT.Copy).then_inc(x0_hi.sem, 1)
            with act.Fori(0, DEPTH) as L:

                def split_hi(p, i=0):
                    act.wait_ge(raw_in[p % RS].sem, raw_in[p % RS].by(L, 16 * (i + loads_before[p] + 1)))
                    act.wait_ge(used.sem, used.by(L, RS * i + max(0, p - RS + 1)))
                    act.activation(whi[:, p % RS, :], raw[:, p % RS, :], ACT.Copy).then_inc(
                        hi_ready.sem, steps_of[p])

                def squares(first, last, which):
                    for o in range(first, last):
                        act.wait_ge(z_ready.sem, z_ready.by(L, which * KT + o + 1))
                        act.activation(sq[:, o, :], z[:, o, :], ACT.Square).then_inc(sq_ready.sem, 1)

                def layer_norm(which):
                    act.wait_ge(var_ready.sem, var_ready.by(L, which + 1))
                    act.activation(rstd, var, ACT.Sqrt).then_inc(sd_ready.sem, 1)
                    g0 = V_LN + which * 2 * KT
                    for o in range(KT):
                        act.wait_ge(norm_ready.sem, norm_ready.by(L, which * KT + o + 1))
                        g, b = vec[:, g0 + o:g0 + o + 1], vec[:, g0 + KT + o:g0 + KT + o + 1]
                        act.activation(xh[:, o, :], z[:, o, :], ACT.Identity, scale=g, bias=b)
                        act.activation(x[:, o, :], z[:, o, :], ACT.Identity, scale=g, bias=b).then_inc(
                            xh_ready.sem, 1)

                def ffn(base, f, which, follow):
                    def up(p, i):
                        split_hi(p + LOOK, i)
                        d = p - base
                        if d % 2:
                            pair = (RS // 2) * i + d // 2
                            act.wait_ge(used.sem, used.by(L, RS * i + p))
                            act.wait_ge(up_done.sem, up_done.by(L, f * NFF + pair - 1))
                            act.activation(silu[:, (d // 2) % 2, :], bank[d - 1][:, 0:T], ACT.Silu).then_inc(
                                silu_ready.sem, 1)
                    each(act, base, NUP, up)
                    if f == 0:
                        act.wait_ge(vec_turned.sem, vec_turned.by(L, 1))
                        act.activation(vec[:, :], bank[7][:, 0:NV1 + NV2], ACT.Copy).then_inc(vec_ready.sem, 1)
                    each(act, base + NUP + LOOK, NDN, split_hi)
                    squares(0, 4, which)
                    each(act, base + NUP + NDN + LOOK, NDN - LOOK, split_hi)
                    for p in follow:
                        split_hi(p)
                    squares(4, KT, which)
                    layer_norm(which)

                for p in range(LOOK):
                    split_hi(p)
                ffn(U1, 0, 0, range(WI, WI + LOOK))

                act.wait_ge(hist_turned.sem, hist_turned.by(L, 1))
                act.activation(hist(proj[:, TR:NIN, :])[:, :, :, LEAD - 1],
                               bank[6][:, 0:NRW * SB].rearrange("p (n b) -> p n b", b=SB), ACT.Copy)
                act.activation(hist(proj[:, 0:NQK, :])[:, :, :, 0:LEAD],
                               bank[7][:, 0:NQK * 24].rearrange("p (n b j) -> p n b j", b=SB, j=LEAD),
                               ACT.Copy).then_inc(hist_ready.sem, 1)

                def in_tile(p, i):
                    act.wait_ge(used.sem, used.by(L, RS * i + p + 1))
                    n = RS * i + (p - WI)
                    for dst, src in ((slice(LEAD, LEAD + TP), bank[(p - WI) % RS][:, 0:TP]),
                                     (None, bank[(p - WI) % RS][:, TP:T])):
                        if isinstance(i, int):
                            tile = proj[:, n:n + 1, :]
                        else:
                            tile = proj[:, bass.ds(n, 1), :]
                        if dst:
                            act.activation(tile[:, :, dst].rearrange("p k t -> p (k t)"), src, ACT.Copy)
                        else:
                            out = tile[:, :, S0C:W].rearrange("p k (b t) -> p (k b) t", t=SEG)[:, :, LEAD:SEG]
                            act.activation(out, src.rearrange("p (b t) -> p b t", t=ST), ACT.Copy).then_inc(
                                proj_ready.sem, 1)

                def in_step(p, i):
                    if p + LOOK < WI + NIN:
                        split_hi(p + LOOK, i)
                    in_tile(p, i)
                each(act, WI, NIN - 6, in_step)
                for p in range(WI + NIN - 6, WI + NIN):
                    q = p + LOOK
                    split_hi(q if q < WI + NIN else WO + q - WI - NIN)
                    in_tile(p, 0)

                scalar_mixers(act, L)

                for p in range(WO, WO + KT):
                    split_hi(p + LOOK)
                    squares(p - WO, p - WO + 1, 1)
                layer_norm(1)
                ffn(U2, 1, 2, [])
            for n, (_, rows) in enumerate(TT):
                act.wait_ge(end_turned.sem, 2 * n + 2)
                act.activation(xrows[0:rows, n, 4 * P:8 * P], bank[2 * n + 1][0:rows, :], ACT.Copy).then_inc(
                    end_high.sem, 1)

        @block.vector
        def _(dve):
            dve.wait_ge(consts.sem, 1)
            dve.nop().then_inc(up_done.sem, 2)
            dve.nop().then_inc(proj_ready.sem, RS)
            dve.nop().then_inc(hl_done.sem, 2)
            for k in range(KT):
                dve.wait_ge(x_turned.sem, k + 1)
                dve.tensor_copy(x[:, k, :], bank[k][:, 0:T]).then_inc(x0_ready.sem, 1)
            for k in range(KT):
                dve.wait_ge(x0_hi.sem, k + 1)
                dve.tensor_tensor(xl[:, k, :], x[:, k, :], xh[:, k, :].bitcast(F32), ALU.subtract).then_inc(
                    x_ready.sem, 1)
            with dve.Fori(0, DEPTH) as L:

                def split_lo(p, i=0):
                    dve.wait_ge(hi_ready.sem, hi_ready.by(L, RS * i + p + 1))
                    dve.tensor_tensor(wlo[:, p % RS, :], raw[:, p % RS, :], whi[:, p % RS, :].bitcast(F32),
                                      ALU.subtract).then_inc(lo_ready.sem, steps_of[p])

                def residual(first, last, which, c, b0, done):
                    for o in range(first, last):
                        dve.wait_ge(used.sem, used.by(L, done(o)))
                        dve.scalar_tensor_tensor(out=z[:, o, :], in0=bank[b0 + (o - first) % 4][:, 0:T], scalar=c,
                                                 in1=x[:, o, :], op0=ALU.mult, op1=ALU.add).then_inc(
                            z_ready.sem, 1)

                def layer_norm(which):
                    dve.wait_ge(stats_ready.sem, stats_ready.by(L, which + 1))
                    dve.tensor_scalar(mean, bank[4][:, 0:T], 1.0 / DM, None, ALU.mult)
                    dve.drain()
                    dve.tensor_tensor(rstd, mean, mean, ALU.mult)
                    dve.drain()
                    dve.scalar_tensor_tensor(out=var, in0=bank[5][:, 0:T], scalar=1.0 / DM, in1=rstd,
                                             op0=ALU.mult, op1=ALU.subtract)
                    dve.drain()
                    dve.tensor_scalar(var, var, 0.0, LN_EPS / ALPHA ** 2, ALU.max, ALU.add).then_inc(
                        var_ready.sem, 1)
                    for h in range(2):
                        dve.tensor_tensor(z[:, 4 * h:4 * h + 4, :], z[:, 4 * h:4 * h + 4, :],
                                          bcast(mean.rearrange("p (k t) -> p k t", k=1), 1, 4), ALU.subtract)
                    dve.wait_ge(sd_ready.sem, sd_ready.by(L, which + 1))
                    dve.reciprocal(rstd, rstd)
                    dve.drain()
                    for o in range(KT):
                        dve.tensor_tensor(z[:, o, :], z[:, o, :], rstd, ALU.mult).then_inc(norm_ready.sem, 1)

                def ffn(base, f, which, follow):
                    def up(p, i):
                        split_lo(p + LOOK, i)
                        d = p - base
                        if d % 2:
                            s = (d // 2) % 2
                            pair = f * NFF + (RS // 2) * i + d // 2
                            dve.wait_ge(used.sem, used.by(L, RS * i + p + 1))
                            dve.wait_ge(silu_ready.sem, silu_ready.by(L, pair + 1))
                            dve.wait_ge(hl_done.sem, hl_done.by(L, pair - 1))
                            if f == 1 and d == 1:
                                dve.wait_ge(wkv_left.sem, wkv_left.by(L, 32))
                            k = (RS // 2) * i + d // 2
                            out = (hh[:, k, :] if isinstance(i, int) else
                                   hh[:, bass.ds(k, 1), :].rearrange("p k t -> p (k t)"))
                            dve.tensor_tensor(out, silu[:, s, :], bank[d][:, 0:T], ALU.mult)
                            dve.tensor_tensor(hval[:, s, :], silu[:, s, :], bank[d][:, 0:T], ALU.mult).then_inc(
                                up_done.sem, 1)
                    each(dve, base, NUP, up)
                    c = 0.5 / ALPHA
                    each(dve, base + NUP + LOOK, NDN, split_lo)
                    residual(0, 4, which, c, 4, lambda o: base + NUP + NDN)
                    each(dve, base + NUP + NDN + LOOK, NDN - LOOK, split_lo)
                    for p in follow:
                        split_lo(p)
                    residual(4, KT, which, c, 0, lambda o: base + FFN)
                    layer_norm(which)

                for p in range(LOOK):
                    split_lo(p)
                ffn(U1, 0, 0, range(WI, WI + LOOK))

                each(dve, WI + LOOK, NQK, split_lo)
                for n in range(NQK):
                    split_lo(WI + LOOK + NQK + n)
                    conv(dve, L, n)
                each(dve, WI + LOOK + 2 * NQK, NIN - LOOK - 2 * NQK, split_lo)
                for p in range(WO, WO + LOOK):
                    split_lo(p)

                vector_mixers(dve, L)

                for p in range(WO, WO + KT):
                    split_lo(p + LOOK)
                    residual(p - WO, p - WO + 1, 1, 1.0 / ALPHA, (p - WO) % 4, lambda o: WO + o + 1)
                layer_norm(1)
                ffn(U2, 1, 2, [])
            for n, (_, rows) in enumerate(TT):
                dve.wait_ge(end_turned.sem, 2 * n + 1)
                dve.tensor_copy(xrows[0:rows, n, 0:4 * P], bank[2 * n][0:rows, :]).then_inc(end_low.sem, 1)

        @block.gpsimd
        def _(pool):
            make_constants(pool)
            pool.wait_ge(x_turned.sem, KT)
            with pool.Fori(0, DEPTH) as L:
                start_layer(pool, L)

                def hidden_lo(f):
                    def one(k, i):
                        pair = f * NFF + k + 2 * i
                        pool.wait_ge(up_done.sem, up_done.by(L, pair + 1))
                        at = lambda t: (t[:, bass.ds(k + 2 * i, 1), :].rearrange("p k t -> p (k t)"))
                        pool.tensor_tensor(at(hl), hval[:, k % 2, :], at(hh).bitcast(F32), ALU.subtract).then_inc(
                            hl_done.sem, 1)
                    with pool.Fori(0, NFF // 2) as i:
                        one(0, i)
                        one(1, i)

                def x_lo(which):
                    for o in range(KT):
                        pool.wait_ge(xh_ready.sem, xh_ready.by(L, which * KT + o + 1))
                        pool.tensor_tensor(xl[:, o, :], x[:, o, :], xh[:, o, :].bitcast(F32), ALU.subtract).then_inc(
                            x_ready.sem, 1)

                hidden_lo(0)
                x_lo(0)
                pool_mixers(pool, L)
                x_lo(1)
                hidden_lo(1)
                x_lo(2)


_INS = ["x_prompt", "x_sample", "state_shift", "state_wkv", "state_conv", "state_C", "state_n", "state_m",
        "ffn1_wg", "ffn1_wu", "ffn1_wd", "ln1_g", "ln1_b", "w_in", "mu_shift", "w0", "w2", "a0", "a2", "g2", "k_k",
        "k_a", "r_k", "gn_g", "gn_b", "conv_w", "conv_b", "i_bias", "f_bias", "mh_g", "w_out", "ln2_g", "ln2_b",
        "ffn2_wg", "ffn2_wu", "ffn2_wd", "ln3_g", "ln3_b"]
_OUTS = [("y_prompt", "x_prompt"), ("y_sample", "x_sample"), ("p_shift", "state_shift"), ("p_wkv", "state_wkv"),
         ("p_conv", "state_conv"), ("p_C", "state_C"), ("p_n", "state_n"), ("p_m", "state_m"),
         ("s_shift", "state_shift"), ("s_wkv", "state_wkv"), ("s_conv", "state_conv"), ("s_C", "state_C"),
         ("s_n", "state_n"), ("s_m", "state_m")]


def kernel(**inputs):
    import numpy as _np
    import concourse.bacc as _bacc
    from concourse.bass_utils import run_bass_kernel_spmd as _run

    nc = _bacc.Bacc("TRN2", target_bir_lowering=False, num_devices=1)
    arrays, ins, outs = {}, {}, {}
    for name in _INS:
        a = _np.ascontiguousarray(inputs[name])
        arrays[f"in_{name}"] = a
        ins[name] = nc.dram_tensor(f"in_{name}", a.shape, mybir.dt.from_np(a.dtype), kind="ExternalInput").ap()
    for name, like in _OUTS:
        shape = list(inputs[like].shape)
        if name.startswith("p_"):
            shape[1] = inputs["x_prompt"].shape[0]
        outs[name] = nc.dram_tensor(f"out_{name}", shape, F32, kind="ExternalOutput").ap()
    hymba_kernel(nc, ins, outs)
    r = _run(nc, [arrays], core_ids=[0])
    return tuple(r.results[0][f"out_{name}"] for name, _ in _OUTS)
```

```python
import math
from contextlib import ExitStack

import concourse.bass as bass
from concourse import mybir

ALU = mybir.AluOpType
ACT = mybir.ActivationFunctionType
F32 = mybir.dt.float32
F32R = mybir.dt.float32r
AX_X = mybir.AxisListType.X
P = 128
NEG = -1e30
E_HALF = math.exp(-0.5)


class Signal:

    def __init__(self, sem, n, head=0):
        self.sem, self.n, self.head = sem, n, head

    def by(self, L, k):
        return L * self.n + (self.head + k)


def hymba_kernel(nc, I, O):
    DEPTH, DM, FF = I["ffn1_wg"].shape
    TP = I["x_prompt"].shape[1]
    SB, ST, _ = I["x_sample"].shape
    TS = SB * ST
    T = TP + TS
    HA, NA = I["state_wkv"].shape[2:4]
    HB, DK = I["state_C"].shape[2:4]
    CW = I["conv_w"].shape[1]
    DA, DB = HA * NA, HB * DK
    RW = I["w2"].shape[1]
    ALPHA = (2.0 * DEPTH) ** 0.25
    LN_EPS, GN_EPS, MH_EPS = 1e-5, 64e-5, 1e-6
    KSCALE = DK ** -0.5
    KT = DM // P
    NFF = FF // P
    CH = 64
    NPC = TP // CH
    NCH = NPC + 1
    NJ = DA // P
    NRW = 3 * NJ + 2
    NQK = 2 * DB // P
    NIN = NQK + 2 * HB + NRW
    TV, TO, TR = NQK, NQK + HB, NQK + 2 * HB
    RCOLS = I["mu_shift"].shape[1]
    GCOL = RCOLS + 4 * DB
    LEAD = CW - 1
    SEG = LEAD + ST
    S0C = LEAD + TP
    W = S0C + SB * SEG
    NTT = 3
    TT = [(0, P), (P, P), (2 * P, TS)]
    assert T == 320 and TP == 2 * P and NA == CH == TS and 2 * NA == P == DK and RW == CH and KT == 8 and ST == 8

    RS = 4
    NUP, NDN = 2 * NFF, NFF // 2
    FFN = NUP + 2 * NDN
    up4 = lambda n: -(-n // RS) * RS
    U1 = 0
    WI = up4(FFN)
    WO = WI + up4(NIN)
    U2 = WO + KT
    NPOS = U2 + up4(FFN)
    PADS = [(U1 + FFN, WI), (WI + NIN, WO), (U2 + FFN, NPOS)]
    REAL = [p for p in range(NPOS) if not any(a <= p < b for a, b in PADS)]
    steps_of = {p: 1 + sum(b - a for a, b in PADS if a == p + 1) for p in REAL}
    loads_before = {p: sum(q % RS == p % RS and q < p for q in REAL) for p in REAL}
    slot_loads = [sum(p % RS == s for p in REAL) for s in range(RS)]
    LOOK = 3
    assert NUP % RS == 0 and NDN == 2 * RS + 3 and NIN == 7 * RS + 2

    with ExitStack() as ctx:
        def sb(name, shape, dt=F32):
            return ctx.enter_context(nc.sbuf_tensor(name, shape, dt))

        def signal(name, n, head=0):
            return Signal(ctx.enter_context(nc.semaphore(name)), n, head)

        raw = sb("raw", [P, RS, KT * P])
        whi = sb("whi", [P, RS, KT * P], F32R)
        wlo = sb("wlo", [P, RS, KT * P], F32R)
        x = sb("x", [P, KT, T])
        with ExitStack() as split:
            xh = split.enter_context(nc.sbuf_tensor("xh", [P, KT, T], F32R))
            xl = split.enter_context(nc.sbuf_tensor("xl", [P, KT, T], F32R))
        spare = sb("spare", [P, 2 * KT * T])
        z = sb("z", [P, KT, T])
        ident = sb("ident", [P, P])
        ones = sb("ones", [P, P])
        headones = sb("headones", [P, P])
        scmask = sb("scmask", [P, 2, 2, CH])
        lvmask = sb("lvmask", [P, 6, CH])
        negmask = sb("negmask", [P, 2, P])
        bmask = sb("bmask", [P, SB])
        keep64 = sb("keep64", [P, T])
        keep128 = sb("keep128", [HB, T])
        segneg = sb("segneg", [HB, TS])
        sel = sb("sel", [HB, HB, P])
        gbias = sb("gbias", [HB, 4])
        early = gbias[0:1, 3:4]
        mark = gbias[0:1, 2:3]
        V_MU = 0
        V_W0, V_A0, V_KK, V_KA, V_RK, V_GG, V_GB, V_MH = (NRW + NJ * i for i in range(8))
        V_CB = NRW + 8 * NJ
        V_CW = V_CB + NQK
        NV1 = V_CW + CW * NQK
        V_LN = NV1
        NV2 = 6 * KT
        vec = sb("vec", [P, NV1 + NV2])

        with ExitStack() as hidden:
            hh = hidden.enter_context(nc.sbuf_tensor("hh", [P, NFF, T], F32R))
            hl = hidden.enter_context(nc.sbuf_tensor("hl", [P, NFF, T], F32R))
        SCW = 28032
        scratch = sb("scratch", [P, SCW])
        OPEN = 2 * NFF * T

        def area(at, *dims, rows=P, of=scratch):
            n = math.prod(dims)
            assert at + n <= of.shape[1], (at, dims)
            v = of[0:rows, at:at + n]
            if len(dims) == 1:
                return v
            names = " ".join(f"d{i}" for i in range(len(dims)))
            return v.rearrange(f"p ({names}) -> p {names}", **{f"d{i}": d for i, d in enumerate(dims)})

        FB = 16000 + RCOLS + 2 * DB
        silu = area(FB, 2, T)
        hval = area(FB + 2 * T, 2, T)
        sq = area(FB + 4 * T, KT, T)
        mean, var, rstd, zsum, sqsum = (area(FB + (4 + KT + i) * T, T) for i in range(5))
        vrow1 = area(OPEN, P)
        vrow2 = area(OPEN + P, P)
        hist_shift = area(16000, RCOLS, rows=SB)
        hist_conv = area(16000 + RCOLS, 2 * DB, rows=SB * LEAD)
        xrows = area(OPEN, NTT, DM)
        proj = area(0, NIN, W)
        zflat = z[:, :, :].rearrange("p a b -> p (a b)")
        A0 = NIN * W
        qk = area(A0, NQK, T)
        og = area(A0 + NQK * T, HB, T)
        A1 = A0 + (NQK + HB) * T
        row = area(A1, 12, T, rows=HB)
        lim = area(A1 + 12 * T, 32, rows=HB)
        A2 = A1 + 12 * T + 32
        va = area(A2, NTT, HB, DK + 1)
        kt = area(A2 + NTT * HB * (DK + 1), NTT, HB, DK)
        A3 = A2 + NTT * HB * (2 * DK + 1)
        qh = area(A3, HB, T)
        ends = area(A3 + 1280, NQK, SB + 1, LEAD)
        vs = area(A3 + 1280 + NQK * (SB + 1) * LEAD, HB, TS)
        num = area(A3 + 1280, NTT, HB, DK + 1)
        wexp = area(A3 + 2828, HB, P)
        rexp = area(A3 + 3340, HB, P)
        Caug = area(A3 + 3852, HB, DK + 1)
        cols = area(A3 + 4368, NTT, 4, HB)
        small = area(A3 + 4416, 96)
        n0 = area(A3 + 4512, SB, HB)
        nout = area(A3 + 4544, HB + SB * HB)
        nrow = area(A3 + 4580, DK, rows=HB + SB * HB)
        A4 = A3 + 4580 + DK
        omu = area(A4 + KT * CH + HB * T, NRW)
        gatew = area(A4, KT, CH)
        ctail = area(A4 + KT * CH, 2 * DB, rows=LEAD * (SB + 1))
        yb_new = area(A4 + KT * CH, HB, T)
        tail = area(0, RCOLS, rows=SB + 1, of=spare)
        C0 = area(0, SB, HB, DK, of=spare)
        yb = area((KT + NJ) * T, HB, T, of=spare)
        vmask = area(0, SB, HB, DK, rows=TS)
        QM = SB * (TS + ST)
        qm = [area(TO * W, QM), area(TO * W + QM, QM), area(SB * HB * DK, QM, of=spare), zflat[:, 3 * DA:3 * DA + QM]]
        hc = area(A0, NTT, HB, DK)
        hsq = area(A1, NTT, HB, DK)
        assert SB * HB * DK <= TO * W and TO * W + 2 * QM <= TR * W
        ar = area(0, NJ, NCH, 2, 2, CH)
        zv = area(5552, NJ, NCH, 2, CH)
        bk = area(8112, NJ, NCH, 2, CH)
        rm = area(10752, NRW, T)
        C1 = 15232
        lw, cum, aa, kk, e1, e2, kn, gg = (area(C1 + i * NJ * T, NJ, T) for i in range(8))
        bkh = area(25472, NJ, NCH, 2, CH)
        kksq = area(8112, NJ, T)
        w2p, a2p, g2s = (zflat[:, i * DA:(i + 1) * DA] for i in range(3))
        scores = area(10752, NCH, NJ, 2, 2, CH)
        bkt = area(16512, NCH, NJ, 2, CH)
        uv = area(19072, NCH, NJ, 2, CH)
        bonus = kn
        ati = area(0, NCH, NJ, P, of=spare)
        xti = area(25472, NCH, NJ, P)
        xi = z[:, :, :].rearrange("p a b -> p (a b)").rearrange("p (c j n) -> p c j n", c=NCH, j=NJ)
        t1 = area(8112, NCH, NJ, P)
        SMALLR = 5120
        dlast = area(SMALLR, NJ, NPC + SB)
        gnst = area(SMALLR + 48, 2, NCH * NJ)
        state = area(9648, 2, NJ, NA)
        sdec = area(9648 + 512, NJ, NA)
        rsb = area(9648 + 768, NJ, NA)
        wkv_rows = area(5552, SB, NJ, 2, NA, rows=NA)
        s0 = area(0, SB, NJ, NA, of=spare)
        uvm = area(5552, SB, NJ, 2, CH)
        snew = z[:, :, :].rearrange("p a b -> p (a b)")[:, 0:SB * NJ * NA].rearrange(
            "p (b j n) -> p b j n", b=SB, j=NJ)
        s0sum = area(15872, NJ, 2, 2, TS, rows=NA)
        wkv_out = area(0, SB, NJ, 2, NA, rows=NA)
        pwkv_out = area(15872, NJ, 2, NA, rows=NA)
        yr = area(21632, NCH, NJ, NA)
        yc = area(10752, NCH, NJ, NA)
        ysq = area(12032, NCH, NJ, NA)
        ya = area(13312, NJ, T)

        bank = [ctx.enter_context(nc.psum_tensor(f"bank{i}", [P, 512], F32)) for i in range(8)]

        raw_in = [signal(f"raw_in{s}", 16 * slot_loads[s]) for s in range(RS)]
        hi_ready = signal("hi_ready", NPOS)
        lo_ready = signal("lo_ready", NPOS)
        used = signal("used", NPOS)
        ident_ready = signal("ident_ready", 0, 1)
        consts = signal("consts", 0, 1)
        rows_in = signal("rows_in", 0, 16 * NTT)
        x_turned = signal("x_turned", 0, KT)
        x0_ready = signal("x0_ready", 0, KT)
        x0_hi = signal("x0_hi", 0, KT)
        x_ready = signal("x_ready", 3 * KT, KT)
        silu_ready = signal("silu_ready", 2 * NFF)
        up_done = signal("up_done", 2 * NFF, 2)
        hl_done = signal("hl_done", 2 * NFF, 2)
        z_ready = signal("z_ready", 3 * KT)
        sq_ready = signal("sq_ready", 3 * KT)
        group_ready = signal("group_ready", 3)
        stats_ready = signal("stats_ready", 3)
        var_ready = signal("var_ready", 3)
        rstd_ready = signal("rstd_ready", 3)
        norm_ready = signal("norm_ready", 3 * KT)
        xh_ready = signal("xh_ready", 3 * KT)
        xf_ready = signal("xf_ready", 3 * KT)
        vrows_in = signal("vrows_in", 16 * 17)
        vec_turned = signal("vec_turned", 1)
        vec_ready = signal("vec_ready", 1)
        hist_in = signal("hist_in", 32)
        hist_turned = signal("hist_turned", 1)
        hist_ready = signal("hist_ready", 1)
        leads_zero = signal("leads_zero", 1)
        proj_ready = signal("proj_ready", NIN, RS)
        conv_ready = signal("conv_ready", NQK)
        qk_ready = signal("qk_ready", 1)
        og_ready = signal("og_ready", 1)
        gatew_in = signal("gatew_in", 64)
        gates_mm = signal("gates_mm", 1)
        m_in = signal("m_in", 16)
        absf_ready = signal("absf_ready", 1)
        lnf_ready = signal("lnf_ready", 1)
        rows_ready = signal("rows_ready", 1)
        m_out = signal("m_out", 32)
        ends_ready = signal("ends_ready", 1)
        ends_turned = signal("ends_turned", 1)
        ends_out = signal("ends_out", 1)
        ends_left = signal("ends_left", 32)
        tail_turned = signal("tail_turned", 1)
        tail_ready = signal("tail_ready", 1)
        tail_out = signal("tail_out", 32)
        c0_in = signal("c0_in", 16)
        n0_in = signal("n0_in", 16)
        n0_turned = signal("n0_turned", 1)
        n0_ready = signal("n0_ready", 1)
        kv_turned = signal("kv_turned", NTT)
        kv_ready = signal("kv_ready", NTT)
        cols_turned = signal("cols_turned", 1)
        cols_ready = signal("cols_ready", 1)
        kw_ready = signal("kw_ready", 1)
        tile_mm = signal("tile_mm", NTT)
        wlog_ready = signal("wlog_ready", NTT)
        wexp_ready = signal("wexp_ready", NTT)
        tile_w = signal("tile_w", NTT)
        inter_mm = signal("inter_mm", 1)
        inter_read = signal("inter_read", 1)
        qm_zero = signal("qm_zero", 1)
        c0_read = signal("c0_read", 1)
        num_mm = signal("num_mm", NTT)
        num_ready = signal("num_ready", NTT)
        cadd_mm = signal("cadd_mm", 2)
        caug_ready = signal("caug_ready", 2)
        hvar_ready = signal("hvar_ready", 1)
        hsd_ready = signal("hsd_ready", 1)
        h_ready = signal("h_ready", 1)
        h_turned = signal("h_turned", NTT)
        yb_ready = signal("yb_ready", NTT)
        vmask_ready = signal("vmask_ready", 1)
        c0_decayed = signal("c0_decayed", 1)
        cs_mm = signal("cs_mm", 2 * HB)
        cs_ready = signal("cs_ready", 2 * HB)
        ns_mm = signal("ns_mm", 1)
        nout_ready = signal("nout_ready", 1)
        nout_turned = signal("nout_turned", 1)
        nrow_ready = signal("nrow_ready", 1)
        c_out = signal("c_out", 16 * 4)
        yb_moved = signal("yb_moved", 1)
        prev_ready = signal("prev_ready", 2)
        shift_ready = signal("shift_ready", 2)
        zv_ready = signal("zv_ready", 1)
        lora_in = signal("lora_in", 48)
        lora_act = signal("lora_act", 1)
        lora_mm = signal("lora_mm", 3)
        lora_ready = signal("lora_ready", 3)
        pads_zero = signal("pads_zero", 1)
        kk_sq = signal("kk_sq", 1)
        kk_mm = signal("kk_mm", 1)
        kk_norm2 = signal("kk_norm2", 1)
        kk_norm = signal("kk_norm", 1)
        rk_ready = signal("rk_ready", 1)
        rk_mm = signal("rk_mm", 1)
        cum_ready = signal("cum_ready", 1)
        exp_ready = signal("exp_ready", 3)
        cumx_ready = signal("cumx_ready", 1)
        ab_ready = signal("ab_ready", 1)
        k_ready = signal("k_ready", 1)
        unit_key = signal("unit_key", 1)
        bkh_ready = signal("bkh_ready", 1)
        dlast_ready = signal("dlast_ready", 1)
        score_mm = signal("score_mm", 2 * NCH)
        score_ready = signal("score_ready", 2 * NCH)
        ati_ready = signal("ati_ready", NCH)
        turned = signal("turned", 2 * NCH)
        turned_out = signal("turned_out", 2 * NCH)
        NLV = [6] * NPC + [3]
        NSTEP = sum(NLV)
        t1_mm = signal("t1_mm", NSTEP - NCH)
        t1_ready = signal("t1_ready", NSTEP)
        x_mm = signal("x_mm", NSTEP)
        x_copied = signal("x_copied", NSTEP)
        wkv_in = signal("wkv_in", 16)
        s0_turned = signal("s0_turned", SB)
        s0_ready = signal("s0_ready", SB)
        s0_mm = signal("s0_mm", 1)
        s0sum_ready = signal("s0sum_ready", 1)
        r_mm = signal("r_mm", NCH)
        r_ready = signal("r_ready", NCH)
        u_mm = signal("u_mm", NCH)
        u_ready = signal("u_ready", NCH)
        y_mm = signal("y_mm", NCH)
        y_ready = signal("y_ready", NCH)
        s_mm = signal("s_mm", NPC)
        s_ready = signal("s_ready", NPC)
        uvm_ready = signal("uvm_ready", 1)
        s0_decayed = signal("s0_decayed", 1)
        ss_mm = signal("ss_mm", NJ)
        snew_ready = signal("snew_ready", 1)
        pw_turned = signal("pw_turned", 1)
        sw_turned = signal("sw_turned", SB)
        sw_ready = signal("sw_ready", SB + 1)
        wkv_left = signal("wkv_left", 32)
        bonus_read = signal("bonus_read", 1)
        t1_zero = signal("t1_zero", 1)
        gvar_ready = signal("gvar_ready", 1)
        gsd_ready = signal("gsd_ready", 1)
        yn_ready = signal("yn_ready", 1)
        y_back = signal("y_back", 1)
        ya_ready = signal("ya_ready", 1)
        mix_hi = signal("mix_hi", 2)
        mix_ready = signal("mix_ready", 1)
        end_turned = signal("end_turned", 0, 2 * NTT)
        end_low = signal("end_low", 0, NTT)
        end_high = signal("end_high", 0, NTT)
        y_out = signal("y_out", 0, 16 * NTT)

        block = ctx.enter_context(nc.Block())

        def carry(pool):
            pool.tensor_tensor(mark[:, :], ones[0:1, 0:1], ones[0:1, 0:1], ALU.mult)
            pool.drain()

        def seqs(ap):
            s = ap.shape
            names = " ".join(f"q{i}" for i in range(len(s) - 1))
            return ap.rearrange(f"{names} (b t) -> {names} b t", t=ST)

        def hist(ap):
            s = ap.shape
            names = " ".join(f"q{i}" for i in range(len(s) - 1))
            return ap[(slice(None),) * (len(s) - 1) + (slice(S0C, W),)].rearrange(
                f"{names} (b t) -> {names} b t", t=SEG)

        def bcast(ap, dim, n):
            sh = list(ap.shape)
            sh[dim] = n
            return ap.broadcast_to(sh)

        def conv(dve, L, n):
            dve.wait_ge(proj_ready.sem, proj_ready.by(L, n + 1))
            if n == 0:
                dve.wait_ge(hist_ready.sem, hist_ready.by(L, 1))
                dve.wait_ge(leads_zero.sem, leads_zero.by(L, 1))
            out_p, out_s = qk[:, n, 0:TP], seqs(qk[:, n, TP:T])
            hs = hist(proj[:, n, :])
            for j in range(CW):
                w = vec[:, V_CW + j * NQK + n:V_CW + j * NQK + n + 1]
                src_p, src_s = proj[:, n, j:j + TP], hs[:, :, j:j + ST]
                if j:
                    dve.drain()
                    dve.scalar_tensor_tensor(out=out_p, in0=src_p, scalar=w, in1=out_p, op0=ALU.mult, op1=ALU.add)
                    last = dve.scalar_tensor_tensor(out=out_s, in0=src_s, scalar=w, in1=out_s, op0=ALU.mult,
                                                    op1=ALU.add)
                else:
                    b = vec[:, V_CB + n:V_CB + n + 1]
                    dve.tensor_scalar(out_p, src_p, w, b, ALU.mult, ALU.add)
                    dve.tensor_scalar(out_s, src_s, w, b, ALU.mult, ALU.add)
            last.then_inc(conv_ready.sem, 1)

        def tile_views(n):
            at, rows = TT[n]
            return at, rows, 0 if n < 2 else 1

        def v_tokens(h, n):
            if n < 2:
                return proj[:, TV + h, LEAD + n * P:LEAD + (n + 1) * P]
            return vs[:, h, :]

        def turn(pe, out, src):
            rows = src.shape[0]
            if tuple(src.shape) == (P, P):
                return pe.transpose(out, src, ident[:, :])
            return pe.matmul(out, src, ident[0:rows, 0:rows], start=True, stop=True)

        def gates_product(pe, L):
            pe.wait_ge(gatew_in.sem, gatew_in.by(L, 64))
            pe.wait_ge(hist_ready.sem, hist_ready.by(L, 1))
            for k in range(KT):
                last = pe.matmul(bank[6][0:CH, 0:T], gatew[:, k, :], x[:, k, :], start=(k == 0), stop=(k == KT - 1))
            last.then_inc(gates_mm.sem, 1)

        def conv_ends_turned(pe, L):
            pe.wait_ge(ends_ready.sem, ends_ready.by(L, 1))
            for n in range(NQK):
                last = pe.transpose(bank[4 + n // 4][0:LEAD * (SB + 1), (n % 4) * P:(n % 4 + 1) * P],
                                    ends[:, n, :, :].rearrange("p s j -> p (s j)"), ident[:, :])
            last.then_inc(ends_turned.sem, 1)

        def keys_values_turned(pe, L, n):
            at, rows, _ = tile_views(n)
            if n == 0:
                pe.wait_ge(ends_out.sem, ends_out.by(L, 1))
                pe.wait_ge(qk_ready.sem, qk_ready.by(L, 1))
            else:
                pe.wait_ge(kv_ready.sem, kv_ready.by(L, n))
            for h in range(HB):
                turn(pe, bank[4][0:rows, h * DK:(h + 1) * DK], qk[:, HB + h, at:at + rows])
            for h in range(HB):
                last = pe.transpose(bank[5][0:rows, h * DK:(h + 1) * DK], v_tokens(h, n), ident[:, :])
            last.then_inc(kv_turned.sem, 1)

        def gate_columns(pe, L):
            pe.wait_ge(rows_ready.sem, rows_ready.by(L, 1))
            pe.wait_ge(n0_in.sem, n0_in.by(L, 16))
            turn(pe, bank[6][:, 0:SB * HB], nrow[0:SB * HB, :]).then_inc(n0_turned.sem, 1)
            for n in range(NTT):
                at, rows, _ = tile_views(n)
                for q, r in enumerate((5, 9, 10, 11)):
                    last = turn(pe, bank[7][0:rows, (n * 4 + q) * HB:(n * 4 + q + 1) * HB], row[:, r, at:at + rows])
            last.then_inc(cols_turned.sem, 1)

        SHIFT_TILES = ((3 * NJ, 3 * NJ + 1), range(3 * NJ))
        CS_BANKS = (0, 1, 2, 3, 6, 0, 1, 2)

        def tensor_mixers(pe, L):
            pe.wait_ge(proj_ready.sem, proj_ready.by(L, NIN))
            pe.wait_ge(n0_ready.sem, n0_ready.by(L, 1))
            pe.wait_ge(cols_ready.sem, cols_ready.by(L, 1))
            for n in range(NRW):
                src = proj[:, TR + n, S0C - SEG:W].rearrange("p (s t) -> p s t", t=SEG)[:, :, SEG - 1]
                last = pe.transpose(bank[4 + n // 4][0:SB + 1, (n % 4) * P:(n % 4 + 1) * P], src, ident[:, :])
            last.then_inc(tail_turned.sem, 1)
            for n in range(NTT):
                at, rows, _ = tile_views(n)
                if n:
                    pe.wait_ge(tile_w.sem, tile_w.by(L, n))
                for h in range(HB):
                    pe.matmul(bank[0][:, h * rows:(h + 1) * rows], sel[:, h, :], row[:, 7, at:at + rows],
                              start=True, stop=True)
                for h in range(HB):
                    pe.matmul(bank[1][:, h * rows:(h + 1) * rows], sel[:, h, :], row[:, 9, at:at + rows],
                              start=True, stop=True)
                for h in range(HB):
                    last = pe.matmul(bank[2][0:rows, h * rows:(h + 1) * rows], qk[:, HB + h, at:at + rows],
                                     qk[:, h, at:at + rows], start=True, stop=True)
                last.then_inc(tile_mm.sem, 1)
                pe.wait_ge(tile_w.sem, tile_w.by(L, n + 1))
                if n == 2:
                    pe.wait_ge(caug_ready.sem, caug_ready.by(L, 2))
                    for h in range(HB):
                        last = pe.matmul(bank[6][0:TS, h * SB:(h + 1) * SB], qh[:, h, TP:T], n0[:, :, h],
                                         start=True, stop=True)
                    last.then_inc(inter_mm.sem, 1)
                if n == 0:
                    pe.wait_ge(tail_ready.sem, tail_ready.by(L, 1))
                else:
                    pe.wait_ge(num_ready.sem, num_ready.by(L, n))
                for h in range(HB):
                    out = bank[3 + h // 2][0:rows, (h % 2) * (DK + 1):(h % 2 + 1) * (DK + 1)]
                    if n == 2:
                        if h == 0:
                            pe.wait_ge(c0_in.sem, c0_in.by(L, 16))
                        for b in range(SB):
                            last = pe.matmul(out[:, 0:DK], qm[h][:, b * TS:(b + 1) * TS], C0[:, b, h, :],
                                             start=(b == 0), stop=False, skip_group_check=True)
                        if h == HB - 1:
                            last.then_inc(c0_read.sem, 1)
                    last = pe.matmul(out, wexp[0:rows, h, 0:rows], va[0:rows, n, h, :], start=(n < 2),
                                     stop=(n != 1), skip_group_check=(n == 2))
                    if n == 1:
                        if h == 0:
                            pe.wait_ge(caug_ready.sem, caug_ready.by(L, 1))
                        last = pe.matmul(out, qh[:, h, at:at + rows], Caug[:, h, :], start=False, stop=True)
                last.then_inc(num_mm.sem, 1)
                if n < 2:
                    pe.wait_ge(kw_ready.sem, kw_ready.by(L, 1))
                    for h in range(HB):
                        out = bank[5 + h // 2][:, (h % 2) * (DK + 1):(h % 2 + 1) * (DK + 1)]
                        last = pe.matmul(out, kt[0:rows, n, h, :], va[0:rows, n, h, :], start=True, stop=True)
                    last.then_inc(cadd_mm.sem, 1)
            pe.wait_ge(vmask_ready.sem, vmask_ready.by(L, 1))
            pe.wait_ge(num_ready.sem, num_ready.by(L, NTT))
            for i, b in enumerate(CS_BANKS):
                if i == 4:
                    pe.wait_ge(inter_read.sem, inter_read.by(L, 1))
                if i == 5:
                    pe.wait_ge(h_ready.sem, h_ready.by(L, 1))
                    for n in range(NTT):
                        rows = TT[n][1]
                        for h in range(HB):
                            last = turn(pe, bank[(7, 4, 5)[n]][:, h * rows:(h + 1) * rows], hc[0:rows, n, h, :])
                        last.then_inc(h_turned.sem, 1)
                if i >= 5:
                    pe.wait_ge(cs_ready.sem, cs_ready.by(L, i - 4))
                last = pe.matmul(bank[b][:, :], kt[0:TS, 2, i // 2, :],
                                 vmask[:, 4 * (i % 2):4 * (i % 2) + 4, i // 2, :], start=True, stop=True)
                last.then_inc(cs_mm.sem, 1)
            pe.wait_ge(cs_ready.sem, cs_ready.by(L, 4))
            for h in range(HB):
                last = pe.matmul(bank[3][:, h * SB:(h + 1) * SB], kt[0:TS, 2, h, :], bmask[0:TS, :],
                                 start=True, stop=True)
            last.then_inc(ns_mm.sem, 1)
            pe.wait_ge(nout_ready.sem, nout_ready.by(L, 1))
            turn(pe, bank[5][0:HB + SB * HB, 0:P], nout[:, :]).then_inc(nout_turned.sem, 1)

            pe.wait_ge(cs_ready.sem, cs_ready.by(L, 2 * HB))
            pe.wait_ge(lora_act.sem, lora_act.by(L, 1))
            pe.wait_ge(lora_in.sem, lora_in.by(L, 48))
            for j in range(NJ):
                last = pe.matmul(bank[j][:, 0:T], w2p[:, j * P:(j + 1) * P], rm[:, 3 * NJ, :], start=True, stop=True)
            last.then_inc(lora_mm.sem, 1)
            pe.wait_ge(yb_ready.sem, yb_ready.by(L, NTT))
            pe.wait_ge(nrow_ready.sem, nrow_ready.by(L, 1))
            for j in range(NJ):
                last = pe.matmul(bank[4 + j][:, 0:T], a2p[:, j * P:(j + 1) * P], rm[:, 3 * NJ, :],
                                 start=True, stop=True)
            last.then_inc(lora_mm.sem, 1)
            pe.wait_ge(lora_ready.sem, lora_ready.by(L, 1))
            for j in range(NJ):
                last = pe.matmul(bank[j][:, 0:T], g2s[:, j * P:(j + 1) * P], rm[:, 3 * NJ + 1, :],
                                 start=True, stop=True)
            last.then_inc(lora_mm.sem, 1)
            pe.wait_ge(lora_ready.sem, lora_ready.by(L, 2))
            pe.wait_ge(kk_sq.sem, kk_sq.by(L, 1))
            for j in range(NJ):
                last = pe.matmul(bank[4 + j][:, 0:T], headones[:, :], kksq[:, j, :], start=True, stop=True)
            last.then_inc(kk_mm.sem, 1)
            pe.wait_ge(rk_ready.sem, rk_ready.by(L, 1))
            pe.wait_ge(kk_norm2.sem, kk_norm2.by(L, 1))
            for j in range(NJ):
                last = pe.matmul(bank[4 + j][:, 0:T], headones[:, :], e2[:, j, :], start=True, stop=True)
            last.then_inc(rk_mm.sem, 1)
            pe.wait_ge(lora_ready.sem, lora_ready.by(L, 3))
            pe.wait_ge(ab_ready.sem, ab_ready.by(L, 1))
            pe.wait_ge(k_ready.sem, k_ready.by(L, 1))
            for c in range(NCH):
                if c == 2:
                    pe.wait_ge(bonus_read.sem, bonus_read.by(L, 1))
                    pe.wait_ge(zv_ready.sem, zv_ready.by(L, 1))
                if c in (2, 3):
                    token_rows(pe, L, 2 * c - 4)
                    token_rows(pe, L, 2 * c - 3)
                for g in range(2):
                    i = 2 * c + g
                    if i >= 4:
                        pe.wait_ge(score_ready.sem, score_ready.by(L, i - 3))
                    for q in range(2):
                        j = 2 * g + q
                        last = pe.matmul(bank[i % 4][:, q * 256:(q + 1) * 256],
                                         bk[:, j, c, :, :].rearrange("p s t -> p (s t)"),
                                         ar[:, j, c, :, :, :].rearrange("p q s t -> p (q s t)"),
                                         start=True, stop=True)
                    last.then_inc(score_mm.sem, 1)
            pe.wait_ge(bkh_ready.sem, bkh_ready.by(L, 1))
            for i in range(NPC, 2 * NCH):
                token_rows(pe, L, i)
            for c in range(NCH):
                pe.wait_ge(t1_ready.sem, t1_ready.by(L, c + 1))
                if c >= 2:
                    pe.wait_ge(x_copied.sem, x_copied.by(L, c - 1))
                for j in range(NJ):
                    last = pe.transpose(bank[2 + c % 2][:, j * P:(j + 1) * P], xti[:, c, j, :], ident[:, :])
                last.then_inc(x_mm.sem, 1)
            step, live_before = NCH, list(range(NCH))
            pe.wait_ge(turned_out.sem, turned_out.by(L, 2 * NCH))
            for lv in range(1, 6):
                live = [c for c in range(NCH) if lv < NLV[c]]
                for n, c in enumerate(live):
                    pe.wait_ge(x_copied.sem, x_copied.by(L, step - len(live_before) + live_before.index(c) + 1))
                    pe.wait_ge(t1_ready.sem, t1_ready.by(L, step + n - 1))
                    for j in range(NJ):
                        last = pe.matmul(bank[(step + n) % 2][:, j * P:(j + 1) * P], ati[:, c, j, :],
                                         xi[:, c, j, :], start=True, stop=True)
                    last.then_inc(t1_mm.sem, 1)
                    if n >= 1:
                        grow(pe, L, lv, live[n - 1], step + n - 1)
                grow(pe, L, lv, live[-1], step + len(live) - 1)
                step += len(live)
                live_before = live
            for c in range(NCH):
                out = bank[0][:, 0:NJ * NA]
                if c == NPC:
                    samples_memory_products(pe, L)
                if c == 0:
                    pe.wait_ge(x_copied.sem, x_copied.by(L, NSTEP))
                if 1 <= c < NPC:
                    pe.wait_ge(s_ready.sem, s_ready.by(L, c))
                for j in range(NJ):
                    for q in range(2):
                        o = bank[0][q * CH:(q + 1) * CH, j * NA:(j + 1) * NA]
                        last = pe.matmul(o, scores[:, c, j, q, 0, :], uv[:, c, j, q, :], start=True, stop=(c == 0))
                        if 0 < c < NPC:
                            last = pe.matmul(o, ar[:, j, c, q, 0, :], state[:, c % 2, j, :], start=False, stop=True)
                        if c == NPC:
                            last = pe.matmul(o, s0sum[:, j, q, 0, :], ident[0:NA, 0:NA], start=False, stop=True)
                last.then_inc(r_mm.sem, 1)
                turns = S0_TURNS.get(c, ((), (), ()))
                for b in turns[0]:
                    samples_memory_turned(pe, L, b)
                pe.wait_ge(r_ready.sem, r_ready.by(L, c + 1))
                for j in range(NJ):
                    last = pe.matmul(bank[1][:, j * NA:(j + 1) * NA], xti[:, c, j, :], rsb[:, j, :],
                                     start=True, stop=True)
                last.then_inc(u_mm.sem, 1)
                for b in turns[1]:
                    samples_memory_turned(pe, L, b)
                pe.wait_ge(u_ready.sem, u_ready.by(L, c + 1))
                if c < NPC:
                    for j in range(NJ):
                        for q in range(2):
                            last = pe.matmul(bank[3][q * CH:(q + 1) * CH, j * NA:(j + 1) * NA],
                                             bkt[:, c, j, q, :], uv[:, c, j, q, :], start=True, stop=True)
                    last.then_inc(s_mm.sem, 1)
                if c:
                    pe.wait_ge(y_ready.sem, y_ready.by(L, c))
                for j in range(NJ):
                    for q in range(2):
                        o = bank[2][q * CH:(q + 1) * CH, j * NA:(j + 1) * NA]
                        last = pe.matmul(o, scores[:, c, j, q, 1, :], uv[:, c, j, q, :], start=True, stop=(c == 0))
                        if 0 < c < NPC:
                            last = pe.matmul(o, ar[:, j, c, q, 1, :], state[:, c % 2, j, :], start=False, stop=True)
                        if c == NPC:
                            last = pe.matmul(o, s0sum[:, j, q, 1, :], ident[0:NA, 0:NA], start=False, stop=True)
                last.then_inc(y_mm.sem, 1)
                for b in turns[2]:
                    samples_memory_turned(pe, L, b)
            pe.wait_ge(uvm_ready.sem, uvm_ready.by(L, 1))
            for j in range(NJ):
                for q in range(2):
                    last = pe.matmul(bank[4 + j][q * CH:(q + 1) * CH, :], bkt[:, NPC, j, q, :],
                                     uvm[:, :, j, q, :], start=True, stop=True)
                last.then_inc(ss_mm.sem, 1)
            pe.wait_ge(yn_ready.sem, yn_ready.by(L, 1))
            for j in range(NJ):
                for c in range(NCH):
                    for q in range(2):
                        last = pe.matmul(bank[j][q * CH:(q + 1) * CH, c * CH:(c + 1) * CH], yc[:, c, j, :],
                                         ident[:, q * CH:(q + 1) * CH], start=True, stop=True)
            last.then_inc(y_back.sem, 1)
            pe.wait_ge(snew_ready.sem, snew_ready.by(L, 1))
            for j in range(NJ):
                last = turn(pe, bank[ST_BANKS[0]][0:NA, j * P:(j + 1) * P], state[:, NPC % 2, j, :])
            last.then_inc(pw_turned.sem, 1)
            for b in range(SB):
                if b == 3:
                    pe.wait_ge(ya_ready.sem, ya_ready.by(L, 1))
                if b == SB - 1:
                    pe.wait_ge(sw_ready.sem, sw_ready.by(L, 1))
                for j in range(NJ):
                    last = turn(pe, bank[ST_BANKS[b + 1]][0:NA, j * P:(j + 1) * P], snew[:, b, j, :])
                last.then_inc(sw_turned.sem, 1)

        ST_BANKS = (4, 5, 6, 7, 0, 1, 2, 3, 4)

        def grow(pe, L, lv, c, n):
            pe.wait_ge(t1_ready.sem, t1_ready.by(L, n + 1))
            pe.wait_ge(x_copied.sem, x_copied.by(L, n - 1))
            if lv < NLV[c] - 1:
                for j in range(NJ):
                    pe.matmul(bank[2 + n % 2][:, j * P:(j + 1) * P], xti[:, c, j, :], t1[:, c, j, :],
                              start=True, stop=True)
            for j in range(NJ):
                last = pe.matmul(bank[4 + n % 2][:, j * P:(j + 1) * P], t1[:, c, j, :], xti[:, c, j, :],
                                 start=True, stop=True)
            last.then_inc(x_mm.sem, 1)

        TURNS = [(True, c) for c in range(NPC)] + [(False, c) for c in range(NCH)] + [(True, NPC)]

        def token_rows(pe, L, i):
            of_v, c = TURNS[i]
            if i >= 4:
                pe.wait_ge(turned_out.sem, turned_out.by(L, i - 3))
            for j in range(NJ):
                last = pe.transpose(bank[4 + i % 4][:, j * P:(j + 1) * P],
                                    (zv if of_v else bkh)[:, j, c, :, :].rearrange("p s t -> p (s t)"), ident[:, :])
            last.then_inc(turned.sem, 1)

        def samples_memory_turned(pe, L, b):
            if b == 0:
                pe.wait_ge(wkv_in.sem, wkv_in.by(L, 16))
            if b >= 2:
                pe.wait_ge(s0_ready.sem, s0_ready.by(L, b - 1))
            for j in range(NJ):
                last = turn(pe, bank[4 + b % 2][:, j * NA:(j + 1) * NA],
                            wkv_rows[:, b, j, :, :].rearrange("v q k -> v (q k)"))
            last.then_inc(s0_turned.sem, 1)

        def samples_memory_products(pe, L):
            pe.wait_ge(s0_ready.sem, s0_ready.by(L, SB))
            for j in range(NJ):
                for b in range(SB):
                    out = bank[6 + j // 2][0:NA, (j % 2) * 4 * TS:(j % 2 + 1) * 4 * TS].rearrange(
                        "p (q s t) -> p q s t", q=2, s=2)[:, :, :, b * ST:(b + 1) * ST]
                    last = pe.matmul(out, s0[:, b, j, :], ar[:, j, NPC, :, :, b * ST:(b + 1) * ST],
                                     start=True, stop=True)
            last.then_inc(s0_mm.sem, 1)
            pe.wait_ge(s0sum_ready.sem, s0sum_ready.by(L, 1))

        S0_TURNS = {1: ((0,), (1,), ()), 2: ((2,), (3,), ()), 3: ((4,), (5,), (6, 7))}

        LEVELS = [(lv, c) for lv in range(6) for c in range(NCH) if lv < NLV[c]]

        def copy_ends(act, L):
            act.activation(ends[:, :, :, :], proj[:, 0:NQK, S0C - SEG:W].rearrange(
                "p n (s t) -> p n s t", t=SEG)[:, :, :, SEG - LEAD:SEG], ACT.Copy)
            act.activation(seqs(vs[:, :, :]), hist(proj[:, TV:TO, :])[:, :, :, LEAD:SEG],
                           ACT.Copy).then_inc(ends_ready.sem, 1)

        def output_gate(act, L):
            act.activation(og[:, :, 0:TP], proj[:, TO:TR, LEAD:LEAD + TP], ACT.Sigmoid)
            act.activation(seqs(og[:, :, TP:T]), hist(proj[:, TO:TR, :])[:, :, :, LEAD:SEG],
                           ACT.Sigmoid).then_inc(og_ready.sem, 1)

        def log_forget(act, L):
            act.wait_ge(absf_ready.sem, absf_ready.by(L, 1))
            act.activation(row[:, 2, :], row[:, 2, :], ACT.Exp, scale=-1.0)
            act.drain()
            act.activation(row[:, 2, :], row[:, 2, :], ACT.Ln, bias=ones[0:HB, 0:1]).then_inc(lnf_ready.sem, 1)

        def copy_ends_out(act, L):
            act.wait_ge(ends_turned.sem, ends_turned.by(L, 1))
            for i in range(2):
                last = act.activation(ctail[:, i * 512:(i + 1) * 512], bank[4 + i][0:LEAD * (SB + 1), :], ACT.Copy)
            last.then_inc(ends_out.sem, 1)

        def copy_keys_values(act, L, n):
            rows = TT[n][1]
            act.wait_ge(kv_turned.sem, kv_turned.by(L, n + 1))
            act.activation(kt[0:rows, n, :, :], bank[4][0:rows, :].rearrange("p (h d) -> p h d", h=HB), ACT.Copy)
            act.activation(va[0:rows, n, :, 0:DK], bank[5][0:rows, :].rearrange("p (h d) -> p h d", h=HB),
                           ACT.Copy).then_inc(kv_ready.sem, 1)

        def copy_gate_columns(act, L):
            act.wait_ge(n0_turned.sem, n0_turned.by(L, 1))
            act.activation(n0[:, :, :], bank[6][:, 0:SB * HB].rearrange("p (b h) -> p b h", b=SB),
                           ACT.Copy).then_inc(n0_ready.sem, 1)
            act.wait_ge(cols_turned.sem, cols_turned.by(L, 1))
            for n in range(NTT):
                rows = TT[n][1]
                src = bank[7][0:rows, n * 4 * HB:(n + 1) * 4 * HB].rearrange("p (q h) -> p q h", q=4)
                act.activation(cols[0:rows, n, 0, :], src[:, 0, :], ACT.Copy)
                last = act.activation(cols[0:rows, n, 1:4, :], src[:, 1:4, :], ACT.Exp)
            last.then_inc(cols_ready.sem, 1)

        def scalar_mixers(act, L):
            act.wait_ge(tail_turned.sem, tail_turned.by(L, 1))
            for i in range(4):
                n = min(512, RCOLS - i * 512)
                last = act.activation(tail[:, i * 512:i * 512 + n], bank[4 + i][0:SB + 1, 0:n], ACT.Copy)
            last.then_inc(tail_ready.sem, 1)
            for n in range(NTT):
                at, rows, _ = tile_views(n)
                flat = lambda t: t[:, :, :].rearrange("p a b -> p (a b)")
                act.wait_ge(tile_mm.sem, tile_mm.by(L, n + 1))
                if n == 2:
                    act.wait_ge(caug_ready.sem, caug_ready.by(L, 2))
                elif n:
                    act.wait_ge(tile_w.sem, tile_w.by(L, n))
                act.activation(flat(rexp)[:, 0:HB * rows], bank[1][:, 0:HB * rows], ACT.Exp)
                act.wait_ge(wlog_ready.sem, wlog_ready.by(L, n + 1))
                act.activation(wexp[0:rows, :, 0:rows], wexp[0:rows, :, 0:rows], ACT.Exp).then_inc(wexp_ready.sem, 1)
                act.wait_ge(num_mm.sem, num_mm.by(L, n + 1))
                for g in range(2):
                    last = act.activation(num[0:rows, n, 2 * g:2 * g + 2, :], bank[3 + g][0:rows, 0:2 * (DK + 1)]
                                          .rearrange("p (h d) -> p h d", h=2), ACT.Copy)
                last.then_inc(num_ready.sem, 1)
            act.wait_ge(hvar_ready.sem, hvar_ready.by(L, 1))
            act.activation(small[:, 48:60], small[:, 36:48], ACT.Sqrt).then_inc(hsd_ready.sem, 1)
            act.wait_ge(yb_ready.sem, yb_ready.by(L, NTT))
            for part, tiles in enumerate(SHIFT_TILES):
                for n in tiles:
                    mu, p_ = vec[:, V_MU + n:V_MU + n + 1], proj[:, TR + n, :]
                    act.activation(rm[:, n, 0:TP], p_[:, LEAD - 1:LEAD - 1 + TP], ACT.Identity, scale=mu)
                    last = act.activation(seqs(rm[:, n, TP:T]), hist(p_)[:, :, LEAD - 1:SEG - 1], ACT.Identity,
                                          scale=mu)
                last.then_inc(prev_ready.sem, 1)
            act.wait_ge(nout_turned.sem, nout_turned.by(L, 1))
            act.activation(nrow[:, :], bank[5][0:HB + SB * HB, 0:P], ACT.Copy).then_inc(nrow_ready.sem, 1)
            act.wait_ge(shift_ready.sem, shift_ready.by(L, 1))
            act.activation(rm[:, 3 * NJ + 1, :], rm[:, 3 * NJ + 1, :], ACT.Sigmoid)
            act.activation(rm[0:RW, 3 * NJ, :], rm[0:RW, 3 * NJ, :], ACT.Tanh).then_inc(lora_act.sem, 1)
            act.wait_ge(m_out.sem, m_out.by(L, 32))
            act.wait_ge(lora_mm.sem, lora_mm.by(L, 1))
            for j in range(NJ):
                last = act.activation(lw[:, j, :], bank[j][:, 0:T], ACT.Sigmoid,
                                      bias=vec[:, V_W0 + j:V_W0 + j + 1])
            last.then_inc(lora_ready.sem, 1)
            act.wait_ge(shift_ready.sem, shift_ready.by(L, 2))
            for j in range(NJ):
                act.activation(kk[:, j, :], rm[:, NJ + j, :], ACT.Identity, scale=vec[:, V_KK + j:V_KK + j + 1])
            act.wait_ge(lora_mm.sem, lora_mm.by(L, 2))
            for j in range(NJ):
                last = act.activation(aa[:, j, :], bank[4 + j][:, 0:T], ACT.Sigmoid,
                                      bias=vec[:, V_A0 + j:V_A0 + j + 1])
            last.then_inc(lora_ready.sem, 1)
            act.drain()
            act.activation(kksq[:, :, :], kk[:, :, :], ACT.Square).then_inc(kk_sq.sem, 1)
            act.wait_ge(lora_mm.sem, lora_mm.by(L, 3))
            act.wait_ge(c_out.sem, c_out.by(L, 64))
            for j in range(NJ):
                last = act.activation(gg[:, j, :], bank[j][:, 0:T], ACT.Copy)
            last.then_inc(lora_ready.sem, 1)
            act.wait_ge(cum_ready.sem, cum_ready.by(L, 1))
            act.activation(e1[:, :, :], cum[:, :, :], ACT.Exp, scale=-E_HALF).then_inc(exp_ready.sem, 1)
            act.wait_ge(kk_norm2.sem, kk_norm2.by(L, 1))
            act.activation(kksq[:, :, :], kksq[:, :, :], ACT.Ln)
            act.drain()
            act.activation(kksq[:, :, :], kksq[:, :, :], ACT.Exp, scale=-0.5).then_inc(kk_norm.sem, 1)
            act.wait_ge(cumx_ready.sem, cumx_ready.by(L, 1))
            act.activation(e2[:, :, :], e2[:, :, :], ACT.Exp, scale=-E_HALF).then_inc(exp_ready.sem, 1)
            act.activation(lw[:, :, :], cum[:, :, :], ACT.Exp, scale=E_HALF).then_inc(exp_ready.sem, 1)
            act.wait_ge(pads_zero.sem, pads_zero.by(L, 1))
            for q in range(2):
                part = slice(q * CH, (q + 1) * CH)
                last = act.activation(zv[part, :, :, 1 - q, :], rm[part, 2 * NJ:3 * NJ, :].rearrange(
                    "p j (c t) -> p j c t", t=CH), ACT.Copy)
            last.then_inc(zv_ready.sem, 1)
            act.activation(yb[:, :, :], yb_new[:, :, :], ACT.Copy).then_inc(yb_moved.sem, 1)
            act.wait_ge(ab_ready.sem, ab_ready.by(L, 1))
            act.wait_ge(k_ready.sem, k_ready.by(L, 1))
            for i, (of_v, c) in enumerate(TURNS):
                act.wait_ge(turned.sem, turned.by(L, i + 1))
                act.activation((uv if of_v else bkt)[:, c, :, :, :].rearrange("p j s t -> p (j s t)"),
                               bank[4 + i % 4][:, :], ACT.Copy).then_inc(turned_out.sem, 1)
            for n, (lv, c) in enumerate(LEVELS):
                act.wait_ge(x_mm.sem, x_mm.by(L, n + 1))
                if lv < NLV[c] - 1:
                    last = act.activation(xi[:, c, :, :], bank[2 + n % 2][:, :].rearrange(
                        "p (j s) -> p j s", j=NJ), ACT.Copy)
                if lv:
                    last = act.activation(xti[:, c, :, :], bank[4 + n % 2][:, :].rearrange(
                        "p (j s) -> p j s", j=NJ), ACT.Copy)
                last.then_inc(x_copied.sem, 1)
            for c in range(NCH):
                if c == NPC:
                    act.wait_ge(s0_mm.sem, s0_mm.by(L, 1))
                    for g in range(2):
                        last = act.activation(s0sum[:, 2 * g:2 * g + 2, :, :, :].rearrange("p j q s t -> p (j q s t)"),
                                              bank[6 + g][0:NA, :], ACT.Copy)
                    last.then_inc(s0sum_ready.sem, 1)
                act.wait_ge(r_mm.sem, r_mm.by(L, c + 1))
                act.activation(rsb[:, :, :], bank[0][:, 0:NJ * NA].rearrange("p (j v) -> p j v", j=NJ),
                               ACT.Copy).then_inc(r_ready.sem, 1)
                turns = S0_TURNS.get(c, ((), (), ()))
                for b in turns[0] + turns[1]:
                    act.wait_ge(s0_turned.sem, s0_turned.by(L, b + 1))
                    act.activation(s0[:, b, :, :], bank[4 + b % 2][:, 0:NJ * NA].rearrange("p (j v) -> p j v", j=NJ),
                                   ACT.Copy).then_inc(s0_ready.sem, 1)
                act.wait_ge(y_mm.sem, y_mm.by(L, c + 1))
                act.activation(yr[:, c, :, :], bank[2][:, 0:NJ * NA].rearrange("p (j v) -> p j v", j=NJ),
                               ACT.Copy).then_inc(y_ready.sem, 1)
                for b in turns[2]:
                    act.wait_ge(s0_turned.sem, s0_turned.by(L, b + 1))
                    act.activation(s0[:, b, :, :], bank[4 + b % 2][:, 0:NJ * NA].rearrange("p (j v) -> p j v", j=NJ),
                                   ACT.Copy).then_inc(s0_ready.sem, 1)
            act.wait_ge(gvar_ready.sem, gvar_ready.by(L, 1))
            act.activation(gnst[:, 1, :], gnst[:, 1, :], ACT.Sqrt).then_inc(gsd_ready.sem, 1)
            act.wait_ge(snew_ready.sem, snew_ready.by(L, 1))
            act.activation(xh[:, NJ:KT, :], yb[:, :, :], ACT.Copy).then_inc(mix_hi.sem, 1)
            act.wait_ge(pw_turned.sem, pw_turned.by(L, 1))
            act.activation(pwkv_out[:, :, :, :].rearrange("p j q k -> p (j q k)"), bank[ST_BANKS[0]][0:NA, :],
                           ACT.Copy).then_inc(sw_ready.sem, 1)
            for b in range(SB):
                if b == 3:
                    act.wait_ge(ya_ready.sem, ya_ready.by(L, 1))
                    act.activation(xh[:, 0:NJ, :], ya[:, :, :], ACT.Copy).then_inc(mix_hi.sem, 1)
                act.wait_ge(sw_turned.sem, sw_turned.by(L, b + 1))
                act.activation(wkv_out[:, b, :, :, :].rearrange("p j q k -> p (j q k)"),
                               bank[ST_BANKS[b + 1]][0:NA, :], ACT.Copy).then_inc(sw_ready.sem, 1)

        def gate_rows(dve, L):
            stt, ts = dve.scalar_tensor_tensor, dve.tensor_scalar
            dve.wait_ge(gates_mm.sem, gates_mm.by(L, 1))
            dve.wait_ge(gatew_in.sem, gatew_in.by(L, 64))
            ts(row[:, 0, :], bank[6][0:HB, 0:T], gbias[:, 0:1], None, ALU.add)
            ts(row[:, 1, :], bank[6][32:32 + HB, 0:T], gbias[:, 1:2], None, ALU.add)
            dve.drain()
            stt(out=row[:, 2, :], in0=row[:, 1, :], scalar=-1.0, in1=row[:, 1, :], op0=ALU.mult,
                op1=ALU.max).then_inc(absf_ready.sem, 1)

        def gate_sums(dve, L):
            tt, stt, ts = dve.tensor_tensor, dve.scalar_tensor_tensor, dve.tensor_scalar
            dve.wait_ge(og_ready.sem, og_ready.by(L, 1))
            for h in range(HB):
                ts(og[:, h, :], og[:, h, :], vec[:, V_MH + h:V_MH + h + 1], None, ALU.mult)
            dve.wait_ge(lnf_ready.sem, lnf_ready.by(L, 1))
            stt(out=row[:, 3, :], in0=row[:, 1, :], scalar=0.0, in1=row[:, 2, :], op0=ALU.min, op1=ALU.subtract)
            dve.drain()
            dve.tensor_tensor_scan(row[:, 4, :], keep128[:, :], row[:, 3, :], 0.0, ALU.mult, ALU.add)
            dve.drain()
            tt(row[:, 5, :], row[:, 0, :], row[:, 4, :], ALU.subtract)
            dve.drain()
            dve.wait_ge(m_in.sem, m_in.by(L, 16))
            b_, g_, m_ = row[:, 4, :], row[:, 5, :], row[:, 6, :]
            dve.tensor_tensor_scan(m_[:, 0:P], ones[0:HB, :], g_[:, 0:P], 0.0, ALU.mult, ALU.max)
            dve.tensor_copy(row[:, 2, TP:T], g_[:, TP:T])
            dve.drain()
            tt(lim[:, 0:1], b_[:, P - 1:P], m_[:, P - 1:P], ALU.add)
            tt(row[:, 2, TP:T:ST], g_[:, TP:T:ST], lim[:, 8:8 + SB], ALU.max)
            dve.drain()
            dve.tensor_tensor_scan(m_[:, P:TP], ones[0:HB, :], g_[:, P:TP], lim[:, 0:1], ALU.mult, ALU.max)
            dve.tensor_tensor_scan(m_[:, TP:T], segneg[:, :], row[:, 2, TP:T], 0.0, ALU.add, ALU.max)
            dve.drain()
            tt(lim[:, 1:2], b_[:, TP - 1:TP], m_[:, TP - 1:TP], ALU.add)
            tt(lim[:, 16:16 + SB], b_[:, TP + ST - 1:T:ST], m_[:, TP + ST - 1:T:ST], ALU.add)
            ts(row[:, 7, :], m_, -1.0, None, ALU.mult)
            ts(row[:, 9, 0:P], m_[:, 0:P], -1.0, None, ALU.mult)
            ts(row[:, 9, P:TP], m_[:, P:TP], -1.0, lim[:, 0:1], ALU.mult, ALU.add)
            per_seq = lambda ap: bcast(ap.rearrange("h (b t) -> h b t", t=1), 2, ST)
            tt(seqs(row[:, 9, TP:T]), per_seq(lim[:, 8:8 + SB]), seqs(m_[:, TP:T]), ALU.subtract)
            stt(out=row[:, 10, :], in0=b_, scalar=-1.0, in1=m_, op0=ALU.mult, op1=ALU.subtract)
            for at in (0, P):
                ts(row[:, 11, at:at + P], g_[:, at:at + P], m_[:, at + P - 1:at + P], None, ALU.subtract)
            tt(seqs(row[:, 11, TP:T]), seqs(g_[:, TP:T]), per_seq(m_[:, TP + ST - 1:T:ST]),
               ALU.subtract).then_inc(rows_ready.sem, 1)

        def weighted_keys(dve, L):
            tt, ts = dve.tensor_tensor, dve.tensor_scalar
            dve.wait_ge(cols_ready.sem, cols_ready.by(L, 1))
            dve.wait_ge(kv_ready.sem, kv_ready.by(L, NTT))
            for n in range(NTT):
                rows = TT[n][1]
                ts(cols[0:rows, n, 3, :], cols[0:rows, n, 3, :], KSCALE, None, ALU.mult)
            dve.drain()
            for n in range(NTT):
                rows = TT[n][1]
                ws = cols[0:rows, n, 3, :].rearrange("p (h o) -> p h o", o=1)
                last = tt(kt[0:rows, n, :, :], kt[0:rows, n, :, :], bcast(ws, 2, DK), ALU.mult)
            last.then_inc(kw_ready.sem, 1)

        def vector_mixers(dve, L):
            tt, stt, ts = dve.tensor_tensor, dve.scalar_tensor_tensor, dve.tensor_scalar
            dve.memset(num[TS:P, 2, :, :], 1.0)
            dve.memset(cols[TS:P, 2, :, :], 1.0)
            for n in range(NTT):
                at, rows, kind = tile_views(n)
                dve.wait_ge(tile_mm.sem, tile_mm.by(L, n + 1))
                if n:
                    dve.wait_ge(num_mm.sem, num_mm.by(L, n))
                for h in range(HB):
                    last = stt(out=wexp[0:rows, h, 0:rows], in0=bank[0][0:rows, h * rows:(h + 1) * rows],
                               scalar=cols[0:rows, n, 0, h:h + 1], in1=negmask[0:rows, kind, 0:rows],
                               op0=ALU.add, op1=ALU.add)
                last.then_inc(wlog_ready.sem, 1)
                dve.wait_ge(wexp_ready.sem, wexp_ready.by(L, n + 1))
                if n:
                    tt(qh[:, :, at:at + rows], qk[:, 0:HB, at:at + rows],
                       rexp[:, :, :].rearrange("p h t -> p (h t)")[:, 0:HB * rows].rearrange(
                           "p (h t) -> p h t", h=HB), ALU.mult)
                if n == 2:
                    dve.wait_ge(qm_zero.sem, qm_zero.by(L, 1))
                    for h in range(HB):
                        own = qm[h].rearrange("p (b s) -> p b s", b=SB)[:, :, 0:ST]
                        tt(own, seqs(qk[:, h, TP:T]), seqs(rexp[:, :, :].rearrange("p h t -> p (h t)")[
                            :, h * TS:(h + 1) * TS]), ALU.mult)
                stt(out=wexp[0:rows, :, 0:rows],
                    in0=bank[2][0:rows, 0:HB * rows].rearrange("p (h t) -> p h t", h=HB), scalar=KSCALE,
                    in1=wexp[0:rows, :, 0:rows], op0=ALU.mult, op1=ALU.mult).then_inc(tile_w.sem, 1)
                if n < 2:
                    dve.wait_ge(cadd_mm.sem, cadd_mm.by(L, n + 1))
                    for h in range(HB):
                        add = bank[5 + h // 2][:, (h % 2) * (DK + 1):(h % 2 + 1) * (DK + 1)]
                        if n == 0:
                            last = dve.tensor_copy(Caug[:, h, :], add)
                        else:
                            last = stt(out=Caug[:, h, :], in0=Caug[:, h, :], scalar=rexp[:, h, P - 1:P], in1=add,
                                       op0=ALU.mult, op1=ALU.add)
                    last.then_inc(caug_ready.sem, 1)
            dve.wait_ge(inter_mm.sem, inter_mm.by(L, 1))
            sel_b = bcast(bmask[0:TS, :].rearrange("p (o b) -> p o b", o=1), 1, HB)
            tmp = small[0:TS, 64:96].rearrange("p (h b) -> p h b", h=HB)
            tt(tmp, bank[6][0:TS, 0:HB * SB].rearrange("p (h b) -> p h b", h=HB), sel_b, ALU.mult).then_inc(
                inter_read.sem, 1)
            dve.drain()
            dve.tensor_reduce(small[0:TS, 60:64], tmp, AX_X, ALU.add)
            dve.drain()
            dve.wait_ge(num_ready.sem, num_ready.by(L, NTT))
            tt(num[0:TS, 2, :, DK], num[0:TS, 2, :, DK], small[0:TS, 60:64], ALU.add)
            dve.drain()
            den = num[:, :, :, DK]
            s12 = lambda i: small[:, 12 * i:12 * i + 12]
            wide = lambda i: bcast(s12(i).rearrange("p (h o) -> p h o", o=1), 2, DK)
            heads = lambda t: t[:, :, :, :].rearrange("p n h d -> p (n h) d")
            by_tile = s12(0).rearrange("p (n h) -> p n h", n=NTT)
            stt(out=by_tile, in0=den, scalar=-1.0, in1=den, op0=ALU.mult, op1=ALU.max)
            dve.drain()
            tt(by_tile, by_tile, cols[:, :, 2, :], ALU.max)
            dve.drain()
            dve.reciprocal(s12(0), s12(0))
            dve.drain()
            tt(heads(hc), heads(num)[:, :, 0:DK], wide(0), ALU.mult)
            dve.drain()
            dve.tensor_reduce(s12(1), heads(hc), AX_X, ALU.add)
            dve.drain()
            ts(s12(1), s12(1), 1.0 / DK, None, ALU.mult)
            dve.drain()
            tt(heads(hc), heads(hc), wide(1), ALU.subtract)
            dve.drain()
            tt(heads(hsq), heads(hc), heads(hc), ALU.mult)
            dve.drain()
            dve.tensor_reduce(s12(2), heads(hsq), AX_X, ALU.add)
            dve.drain()
            ts(s12(3), s12(2), 1.0 / DK, MH_EPS, ALU.mult, ALU.add).then_inc(hvar_ready.sem, 1)
            dve.wait_ge(hsd_ready.sem, hsd_ready.by(L, 1))
            dve.reciprocal(s12(4), s12(4))
            dve.drain()
            tt(heads(hc), heads(hc), wide(4), ALU.mult).then_inc(h_ready.sem, 1)
            dve.wait_ge(ends_left.sem, ends_left.by(L, 32))
            for n, (at, rows) in enumerate(TT):
                dve.wait_ge(h_turned.sem, h_turned.by(L, n + 1))
                tt(yb_new[:, :, at:at + rows], bank[(7, 4, 5)[n]][:, 0:HB * rows].rearrange(
                    "p (h t) -> p h t", h=HB), og[:, :, at:at + rows], ALU.mult).then_inc(yb_ready.sem, 1)
            dve.wait_ge(c0_decayed.sem, c0_decayed.by(L, 1))
            for h in range(HB):
                for half in range(2):
                    i = 2 * h + half
                    dve.wait_ge(cs_mm.sem, cs_mm.by(L, i + 1))
                    mem = C0[:, 4 * half:4 * half + 4, h, :]
                    tt(mem, mem, bank[CS_BANKS[i]][:, :].rearrange("p (b e) -> p b e", b=4),
                       ALU.add).then_inc(cs_ready.sem, 1)
            dve.wait_ge(ns_mm.sem, ns_mm.by(L, 1))
            dve.tensor_copy(nout[:, 0:HB], Caug[:, :, DK])
            nb = nout[:, HB:HB + SB * HB].rearrange("p (b h) -> p b h", b=SB)
            dec = rexp[:, :, :].rearrange("p h t -> p (h t)")[:, 0:HB * TS].rearrange(
                "p (h b t) -> p b h t", h=HB, t=ST)[:, :, :, ST - 1]
            tt(nb, n0[:, :, :], dec, ALU.mult)
            dve.drain()
            tt(nb, nb, bank[3][:, 0:HB * SB].rearrange("p (h b) -> p b h", h=HB), ALU.add).then_inc(
                nout_ready.sem, 1)
            cur = proj[:, TR:NIN, :]
            for part, tiles in enumerate(SHIFT_TILES):
                dve.wait_ge(prev_ready.sem, prev_ready.by(L, part + 1))
                for n in tiles:
                    stt(out=rm[:, n, 0:TP], in0=cur[:, n, LEAD:LEAD + TP], scalar=omu[:, n:n + 1],
                        in1=rm[:, n, 0:TP], op0=ALU.mult, op1=ALU.add)
                    last = stt(out=seqs(rm[:, n, TP:T]), in0=hist(cur[:, n, :])[:, :, LEAD:SEG],
                               scalar=omu[:, n:n + 1], in1=seqs(rm[:, n, TP:T]), op0=ALU.mult, op1=ALU.add)
                last.then_inc(shift_ready.sem, 1)
            dve.drain()
            r, k, v = rm[:, 0:NJ, :], rm[:, NJ:2 * NJ, :], rm[:, 2 * NJ:3 * NJ, :]
            flat = lambda t: t.rearrange("p j t -> p (j t)")
            col = lambda at, j: vec[:, at + j:at + j + 1]
            dve.wait_ge(lora_ready.sem, lora_ready.by(L, 1))
            for j in range(NJ):
                last = dve.tensor_tensor_scan(cum[:, j, :], keep64[:, :], lw[:, j, :], 0.0, ALU.mult, ALU.add)
            last.then_inc(cum_ready.sem, 1)
            dve.wait_ge(lora_ready.sem, lora_ready.by(L, 2))
            for j in range(NJ):
                ts(kn[:, j, :], aa[:, j, :], -1.0, col(V_KA, j), ALU.add, ALU.mult)
            dve.drain()
            stt(out=flat(kn[:, :, :]), in0=flat(kn[:, :, :]), scalar=1.0, in1=flat(k), op0=ALU.add, op1=ALU.mult)
            dve.drain()
            for j in range(NJ):
                last = stt(out=e2[:, j, :], in0=r[:, j, :], scalar=col(V_RK, j), in1=kn[:, j, :],
                           op0=ALU.mult, op1=ALU.mult)
            last.then_inc(rk_ready.sem, 1)
            dve.wait_ge(kk_mm.sem, kk_mm.by(L, 1))
            for j in range(NJ):
                last = ts(kksq[:, j, :], bank[4 + j][:, 0:T], 1e-24, None, ALU.max)
            last.then_inc(kk_norm2.sem, 1)
            halves = [(q, slice(q * CH, (q + 1) * CH)) for q in range(2)]
            chunks = lambda t: t.rearrange("p j (c t) -> p j c t", t=CH)
            dve.wait_ge(exp_ready.sem, exp_ready.by(L, 1))
            dve.wait_ge(pads_zero.sem, pads_zero.by(L, 1))
            for q, part in halves:
                tt(ar[part, :, :, q, 1, :], chunks(r[part]), chunks(e1[part, :, :]), ALU.mult)
            dve.wait_ge(rk_mm.sem, rk_mm.by(L, 1))
            tt(e2[:, :, :], cum[:, :, :], lw[:, :, :], ALU.subtract).then_inc(cumx_ready.sem, 1)
            dve.tensor_copy(dlast[:, :, 0:NPC], e1[:, :, CH - 1:TP:CH])
            dve.tensor_copy(dlast[:, :, NPC:NPC + SB], e1[:, :, TP + ST - 1:T:ST]).then_inc(dlast_ready.sem, 1)
            dve.wait_ge(kk_norm.sem, kk_norm.by(L, 1))
            stt(out=flat(kk[:, :, :]), in0=flat(kk[:, :, :]), scalar=-1.0, in1=flat(kksq[:, :, :]), op0=ALU.mult,
                op1=ALU.mult).then_inc(unit_key.sem, 1)
            dve.drain()
            stt(out=flat(aa[:, :, :]), in0=flat(kk[:, :, :]), scalar=-1.0, in1=flat(aa[:, :, :]), op0=ALU.mult,
                op1=ALU.mult)
            dve.drain()
            dve.wait_ge(exp_ready.sem, exp_ready.by(L, 2))
            for q, part in halves:
                tt(ar[part, :, :, q, 0, :], chunks(kk[part, :, :]), chunks(e2[part, :, :]), ALU.mult)
            dve.wait_ge(exp_ready.sem, exp_ready.by(L, 3))
            for q, part in halves:
                last = tt(bk[part, :, :, q, :], chunks(aa[part, :, :]), chunks(lw[part, :, :]), ALU.mult)
            last.then_inc(ab_ready.sem, 1)
            dve.drain()
            dve.wait_ge(k_ready.sem, k_ready.by(L, 1))
            for j in range(NJ):
                last = tt(bonus[:, j, :], bank[4 + j][:, 0:T], v[:, j, :], ALU.mult)
            last.then_inc(bonus_read.sem, 1)
            dve.drain()
            dve.wait_ge(zv_ready.sem, zv_ready.by(L, 1))
            for c in range(NCH):
                for g in range(2):
                    dve.wait_ge(score_mm.sem, score_mm.by(L, 2 * c + g + 1))
                    tri = scmask[:, 0 if c < NPC else 1, :, :].rearrange("p (o s) t -> p o (s t)", o=1)
                    tt(scores[:, c, 2 * g:2 * g + 2, :, :, :].rearrange("p j q s t -> p (j q) (s t)"),
                       bank[(2 * c + g) % 4][:, :].rearrange("p (i s) -> p i s", i=4), bcast(tri, 1, 4),
                       ALU.mult).then_inc(score_ready.sem, 1)
            dve.wait_ge(turned.sem, turned.by(L, 2 * NCH - 1))
            for c in range(NCH):
                dve.wait_ge(ati_ready.sem, ati_ready.by(L, c + 1))
                pairs = bcast(lvmask[:, 0, :].rearrange("p (o t) -> p o t", o=1), 1, 2 * NJ)
                tt(xti[:, c, :, :].rearrange("p j (h t) -> p (j h) t", h=2),
                   ati[:, c, :, :].rearrange("p j (h t) -> p (j h) t", h=2), pairs, ALU.mult).then_inc(
                    t1_ready.sem, 1)
            dve.wait_ge(t1_zero.sem, t1_zero.by(L, 1))
            for n, (lv, c) in enumerate(LEVELS):
                if lv == 0:
                    continue
                dve.wait_ge(t1_mm.sem, t1_mm.by(L, n - NCH + 1))
                for q, part in halves:
                    m = bcast(lvmask[part, lv, :].rearrange("p (o t) -> p o t", o=1), 1, NJ)
                    last = tt(t1[part, c, :, part], bank[n % 2][part, :].rearrange("p (j s) -> p j s", j=NJ)[
                        :, :, part], m, ALU.mult)
                last.then_inc(t1_ready.sem, 1)
            for c in range(NCH):
                dve.wait_ge(u_mm.sem, u_mm.by(L, c + 1))
                for q, part in halves:
                    last = dve.tensor_copy(uv[part, c, :, q, :],
                                           bank[1][part, 0:NJ * NA].rearrange("p (j v) -> p j v", j=NJ))
                last.then_inc(u_ready.sem, 1)
                if c < NPC:
                    dve.wait_ge(s_mm.sem, s_mm.by(L, c + 1))
                    add = bank[3][:, 0:NJ * NA].rearrange("p (j v) -> p j v", j=NJ)
                    if c == 0:
                        last = dve.tensor_copy(state[:, 1, :, :], add)
                    else:
                        last = tt(state[:, (c + 1) % 2, :, :], sdec[:, :, :], add, ALU.add)
                    last.then_inc(s_ready.sem, 1)
                    if c + 1 < NPC:
                        dve.drain()
                        tt(sdec[:, :, :], state[:, (c + 1) % 2, :, :],
                           bcast(dlast[:, :, c + 1:c + 2], 2, NA), ALU.mult)
                        dve.drain()
            dve.drain()
            for b in range(SB):
                last = ts(uvm[:, b, :, :, :].rearrange("p j q v -> p (j q v)"),
                          uv[:, NPC, :, :, :].rearrange("p j q v -> p (j q v)"), bmask[:, b:b + 1], None, ALU.mult)
            last.then_inc(uvm_ready.sem, 1)
            dve.wait_ge(y_ready.sem, y_ready.by(L, NCH))
            hd = lambda t: t[:, :, :, :].rearrange("p c j v -> p (c j) v")
            st = lambda i: bcast(gnst[:, i, :].rearrange("p (n o) -> p n o", o=1), 2, NA)
            dve.tensor_reduce(gnst[:, 0, :], hd(yr), AX_X, ALU.add)
            dve.drain()
            ts(gnst[:, 0, :], gnst[:, 0, :], 1.0 / NA, None, ALU.mult)
            dve.drain()
            tt(hd(yc), hd(yr), st(0), ALU.subtract)
            dve.drain()
            tt(hd(ysq), hd(yc), hd(yc), ALU.mult)
            dve.drain()
            dve.tensor_reduce(gnst[:, 1, :], hd(ysq), AX_X, ALU.add)
            dve.drain()
            ts(gnst[:, 1, :], gnst[:, 1, :], 1.0 / NA, GN_EPS, ALU.mult, ALU.add).then_inc(gvar_ready.sem, 1)
            dve.wait_ge(s0_decayed.sem, s0_decayed.by(L, 1))
            for j in range(NJ):
                dve.wait_ge(ss_mm.sem, ss_mm.by(L, j + 1))
                last = tt(snew[:, :, j, :], s0[:, :, j, :], bank[4 + j][:, :].rearrange("p (b v) -> p b v", b=SB),
                          ALU.add)
            last.then_inc(snew_ready.sem, 1)
            dve.wait_ge(gsd_ready.sem, gsd_ready.by(L, 1))
            dve.reciprocal(gnst[:, 1, :], gnst[:, 1, :])
            dve.drain()
            tt(hd(yc), hd(yc), st(1), ALU.mult).then_inc(yn_ready.sem, 1)
            dve.wait_ge(mix_hi.sem, mix_hi.by(L, 1))
            tt(xl[:, NJ:KT, :], yb[:, :, :], xh[:, NJ:KT, :].bitcast(F32), ALU.subtract)
            dve.wait_ge(y_back.sem, y_back.by(L, 1))
            for j in range(NJ):
                stt(out=ya[:, j, :], in0=bank[j][:, 0:T], scalar=col(V_GG, j), in1=bonus[:, j, :], op0=ALU.mult,
                    op1=ALU.add)
            dve.drain()
            for j in range(NJ):
                last = stt(out=ya[:, j, :], in0=ya[:, j, :], scalar=col(V_GB, j), in1=gg[:, j, :], op0=ALU.add,
                           op1=ALU.mult)
            last.then_inc(ya_ready.sem, 1)
            dve.wait_ge(mix_hi.sem, mix_hi.by(L, 2))
            tt(xl[:, 0:NJ, :], ya[:, :, :], xh[:, 0:NJ, :].bitcast(F32), ALU.subtract).then_inc(mix_ready.sem, 1)

        def make_constants(pool):
            def ms(t, value):
                pool.memset(t, value)
                pool.drain()

            def sel_(**how):
                pool.affine_select(**how)
                pool.drain()

            ms(ident[:, :], 0.0)
            sel_(out=ident[:, :], in_=ident[:, :], compare_op=ALU.not_equal, fill=1.0, base=0, pattern=[[-1, P]],
                 channel_multiplier=1)
            pool.nop().then_inc(ident_ready.sem, 1)
            for t, val in ((ones[:, :], 1.0), (headones[:, :], 0.0), (scmask[:, :, :, :], 1.0),
                           (lvmask[:, :, :], 0.0), (negmask[:, :, :], 0.0), (bmask[:, :], 1.0), (keep64[:, :], 1.0),
                           (keep128[:, :], 1.0), (segneg[:, :], 0.0), (sel[:, :, :], 1.0)):
                ms(t, val)
            for q in range(2):
                part = slice(q * CH, (q + 1) * CH)
                ms(headones[part, part], 1.0)
                for kind in range(2):
                    for incl in range(2):
                        m = scmask[part, kind, incl, :]
                        sel_(out=m, in_=m, compare_op=ALU.is_ge, fill=0.0, base=incl - 1, pattern=[[1, CH]],
                             channel_multiplier=-1)
                for lv in range(6):
                    b = 1 << lv
                    m = lvmask[part, lv, :].rearrange("p (g s t) -> p g s t", s=2, t=b)[:, :, int(lv == 0), :]
                    ms(m, 1.0)
                bm = bmask[part, :]
                sel_(out=bm, in_=bm, compare_op=ALU.is_ge, fill=0.0, base=0, pattern=[[-ST, SB]],
                     channel_multiplier=1)
            for q in range(2):
                part = slice(q * CH, (q + 1) * CH)
                bm = bmask[part, :]
                sel_(out=bm, in_=bm, compare_op=ALU.is_ge, fill=0.0, base=ST - 1, pattern=[[ST, SB]],
                     channel_multiplier=-1)
                for incl in range(2):
                    m = seqs(scmask[part, 1, incl, :])
                    sel_(out=m, in_=m, compare_op=ALU.is_ge, fill=0.0, base=0, pattern=[[-ST, SB], [0, ST]],
                         channel_multiplier=1)
                for lv in range(6):
                    b = 1 << lv
                    m = lvmask[part, lv, :].rearrange("p (g s t) -> p g s t", s=2, t=b)[:, :, int(lv == 0), :]
                    n = CH // (2 * b)
                    sel_(out=m, in_=m, compare_op=ALU.is_ge, fill=0.0, base=-b if lv else 0,
                         pattern=[[-2 * b, n], [0, b]], channel_multiplier=1)
            m = negmask[:, 0, :]
            sel_(out=m, in_=m, compare_op=ALU.is_ge, fill=NEG, base=0, pattern=[[1, P]], channel_multiplier=-1)
            m = negmask[0:TS, 1, 0:TS]
            sel_(out=m, in_=m, compare_op=ALU.is_ge, fill=NEG, base=0, pattern=[[1, TS]], channel_multiplier=-1)
            for h in range(HB):
                m = sel[:, h, :]
                sel_(out=m, in_=m, compare_op=ALU.is_equal, fill=0.0, base=-h, pattern=[[0, P]],
                     channel_multiplier=1)
            ms(keep64[:, 0:TP:CH], 0.0)
            ms(keep64[:, TP:T:ST], 0.0)
            ms(keep128[:, 0:TP:P], 0.0)
            ms(keep128[:, TP:T:ST], 0.0)
            ms(segneg[:, 0:TS:ST], NEG)
            for q in range(2):
                part = slice(q * CH, (q + 1) * CH)
                for lv in range(6):
                    b = 1 << lv
                    m = lvmask[part, lv, :].rearrange("p (g s t) -> p g s t", s=2, t=b)[:, :, int(lv == 0), :]
                    sel_(out=m, in_=m, compare_op=ALU.is_ge, fill=0.0, base=2 * b - 1 if lv else 0,
                         pattern=[[2 * b, CH // (2 * b)], [0, b]], channel_multiplier=-1)
            m = seqs(negmask[0:TS, 1, 0:TS])
            sel_(out=m, in_=m, compare_op=ALU.is_ge, fill=NEG, base=0, pattern=[[-ST, SB], [0, ST]],
                 channel_multiplier=1)
            for q in range(2):
                part = slice(q * CH, (q + 1) * CH)
                for lv in range(6):
                    m = lvmask[part, lv, :]
                    sel_(out=m, in_=m, compare_op=ALU.not_equal, fill=1.0, base=0, pattern=[[-1, CH]],
                         channel_multiplier=1)
            pool.nop().then_inc(consts.sem, 1)

        def start_layer(pool, L):
            at = 0
            lay = lambda w: w[bass.ds(L, 1)]
            for name, n in (("mu_shift", NRW), ("w0", NJ), ("a0", NJ), ("k_k", NJ), ("k_a", NJ), ("r_k", NJ),
                            ("gn_g", NJ), ("gn_b", NJ), ("mh_g", NJ), ("conv_b", NQK), ("conv_w", CW * NQK)):
                w = lay(I[name])
                if name == "r_k":
                    src = w.rearrange("l (j h) n -> (l j) (h n)", h=2)
                elif name == "conv_w":
                    src = w.rearrange("l c (n p) -> (l c n) p", p=P)
                else:
                    src = w.rearrange("l (n p) -> (l n) p", p=P)
                pool.dma_start(vrow1[at:at + n, :], src).then_inc(vrows_in.sem, 16)
                at += n
            assert at == NV1
            for i, name in enumerate(("ln1_g", "ln1_b", "ln2_g", "ln2_b", "ln3_g", "ln3_b")):
                pool.dma_start(vrow2[i * KT:(i + 1) * KT, :], lay(I[name]).rearrange(
                    "l (n p) -> (l n) p", p=P)).then_inc(vrows_in.sem, 16)
            pool.dma_start(hist_shift[:, :], lay(I["state_shift"]).rearrange("l b c -> (l b) c")).then_inc(
                hist_in.sem, 16)
            pool.dma_start(hist_conv[:, :], lay(I["state_conv"]).rearrange("l b j c -> (l b j) c")).then_inc(
                hist_in.sem, 16)

        def pool_mixers(pool, L):
            lay = lambda w: w[bass.ds(L, 1)]
            dma = pool.dma_start
            pool.memset(proj[:, :, 0:LEAD], 0.0).then_inc(leads_zero.sem, 1)
            pool.memset(gatew[:, :, :], 0.0)
            pool.drain()
            pool.memset(w2p[RW:P, :], 0.0)
            pool.drain()
            pool.memset(a2p[0:P - RW, :], 0.0)
            pool.drain()
            for q, at in enumerate((0, 32)):
                src = lay(I["w_in"])[:, :, GCOL + q * HB:GCOL + (q + 1) * HB].rearrange(
                    "l (k p) n -> p (l k) n", p=P)
                dma(gatew[:, :, at:at + HB], src).then_inc(gatew_in.sem, 16)
            for q, name in enumerate(("i_bias", "f_bias")):
                dma(gbias[:, q:q + 1], lay(I[name]).rearrange("l h -> h l")).then_inc(gatew_in.sem, 16)
            dma(w2p[0:RW, :], lay(I["w2"]).rearrange("l r n -> (l r) n")).then_inc(lora_in.sem, 16)
            dma(a2p[P - RW:P, :], lay(I["a2"]).rearrange("l r n -> (l r) n")).then_inc(lora_in.sem, 16)
            dma(g2s[:, :], lay(I["g2"]).rearrange("l r n -> (l r) n")).then_inc(lora_in.sem, 16)
            pool.wait_ge(hist_ready.sem, hist_ready.by(L, 1))
            carry(pool)
            dma(lim[:, 8:8 + SB], lay(I["state_m"]).rearrange("l b h -> h (l b)"),
                allow_slow_non_contiguous=True).then_inc(m_in.sem, 16)
            dma(nrow[0:SB * HB, :], lay(I["state_n"]).rearrange("l b h d -> (l b h) d")).then_inc(n0_in.sem, 16)
            pool.wait_ge(ends_out.sem, ends_out.by(L, 1))
            carry(pool)
            dma(lay(O["p_conv"]).rearrange("l b j c -> (l b j) c"), ctail[0:LEAD, :]).then_inc(ends_left.sem, 16)
            dma(lay(O["s_conv"]).rearrange("l b j c -> (l b j) c"), ctail[LEAD:LEAD * (SB + 1), :]).then_inc(
                ends_left.sem, 16)
            pool.wait_ge(kv_ready.sem, kv_ready.by(L, NTT))
            carry(pool)
            for b in range(SB):
                last = pool.tensor_scalar(vmask[:, b, :, :], va[0:TS, 2, :, 0:DK], bmask[0:TS, b:b + 1], None,
                                          ALU.mult)
            last.then_inc(vmask_ready.sem, 1)
            pool.memset(zflat[:, 3 * DA:3 * DA + QM], 0.0)
            pool.memset(area(TO * W, 2 * QM), 0.0)
            pool.wait_ge(tail_ready.sem, tail_ready.by(L, 1))
            carry(pool)
            dma(lay(O["p_shift"]).rearrange("l b c -> (l b) c"), tail[0:1, :]).then_inc(tail_out.sem, 16)
            dma(lay(O["s_shift"]).rearrange("l b c -> (l b) c"), tail[1:SB + 1, :]).then_inc(tail_out.sem, 16)
            pool.memset(qm[2], 0.0).then_inc(qm_zero.sem, 1)
            pool.wait_ge(tail_out.sem, tail_out.by(L, 32))
            carry(pool)
            dma(C0[:, :, :, :].rearrange("d b h e -> d (b h) e"),
                lay(I["state_C"]).rearrange("l b h d e -> d (l b h) e")).then_inc(c0_in.sem, 16)
            pool.wait_ge(rows_ready.sem, rows_ready.by(L, 1))
            carry(pool)
            dma(lay(O["p_m"]).rearrange("l b h -> h (l b)"), lim[:, 1:2],
                allow_slow_non_contiguous=True).then_inc(m_out.sem, 16)
            dma(lay(O["s_m"]).rearrange("l b h -> h (l b)"), lim[:, 16:16 + SB],
                allow_slow_non_contiguous=True).then_inc(m_out.sem, 16)
            pool.wait_ge(c0_read.sem, c0_read.by(L, 1))
            dec = rexp[:, :, :].rearrange("p h t -> p (h t)")[:, 0:HB * TS].rearrange(
                "p (h b t) -> p b h t", h=HB, t=ST)[:, :, :, ST - 1:ST]
            for b in range(SB):
                last = pool.tensor_tensor(C0[:, b, :, :], C0[:, b, :, :], bcast(dec[:, b, :, :], 2, DK), ALU.mult)
            last.then_inc(c0_decayed.sem, 1)
            pool.wait_ge(cs_ready.sem, cs_ready.by(L, 2 * HB))
            pool.wait_ge(nrow_ready.sem, nrow_ready.by(L, 1))
            carry(pool)
            dma(lay(O["s_C"]).rearrange("l b h d e -> d (l b h) e"),
                C0[:, :, :, :].rearrange("d b h e -> d (b h) e")).then_inc(c_out.sem, 16)
            dma(lay(O["p_C"]).rearrange("l b h d e -> d (l b h) e"), Caug[:, :, 0:DK]).then_inc(c_out.sem, 16)
            dma(lay(O["p_n"]).rearrange("l b h d -> (l b h) d"), nrow[0:HB, :]).then_inc(c_out.sem, 16)
            dma(lay(O["s_n"]).rearrange("l b h d -> (l b h) d"), nrow[HB:HB + SB * HB, :]).then_inc(c_out.sem, 16)
            pool.memset(ar[:, :, :, :, :, :], 0.0)
            pool.wait_ge(m_out.sem, m_out.by(L, 32))
            pool.wait_ge(shift_ready.sem, shift_ready.by(L, 2))
            carry(pool)
            pool.memset(zv[:, :, :, :, :], 0.0).then_inc(pads_zero.sem, 1)
            pool.wait_ge(c_out.sem, c_out.by(L, 64))
            carry(pool)
            pool.memset(ati[:, :, :, :], 0.0)
            pool.drain()
            pool.wait_ge(exp_ready.sem, exp_ready.by(L, 3))
            pool.wait_ge(unit_key.sem, unit_key.by(L, 1))
            for q in range(2):
                part = slice(q * CH, (q + 1) * CH)
                last = pool.tensor_tensor(
                    bk[part, :, :, 1 - q, :], kn[part, :, :].rearrange("p j (c t) -> p j c t", t=CH),
                    lw[part, :, :].rearrange("p j (c t) -> p j c t", t=CH), ALU.mult)
            last.then_inc(k_ready.sem, 1)
            pool.drain()
            pool.wait_ge(ab_ready.sem, ab_ready.by(L, 1))
            pool.wait_ge(dlast_ready.sem, dlast_ready.by(L, 1))
            pool.wait_ge(yb_moved.sem, yb_moved.by(L, 1))
            pool.wait_ge(lora_ready.sem, lora_ready.by(L, 3))
            carry(pool)
            two = lambda t: t.rearrange("p j c s t -> p j c (s t)")
            pool.tensor_tensor(two(bkh[:, :, 0:NPC, :, :]), two(bk[:, :, 0:NPC, :, :]),
                               bcast(dlast[:, :, 0:NPC].rearrange("p j (c o) -> p j c o", o=1), 3, 2 * CH), ALU.mult)
            for s in range(2):
                last = pool.tensor_tensor(
                    seqs(bkh[:, :, NPC, s, :]), seqs(bk[:, :, NPC, s, :]),
                    bcast(dlast[:, :, NPC:NPC + SB].rearrange("p j (c o) -> p j c o", o=1), 3, ST), ALU.mult)
            last.then_inc(bkh_ready.sem, 1)
            pool.drain()
            for c in range(NCH):
                pool.wait_ge(score_ready.sem, score_ready.by(L, 2 * c + 2))
                for q in range(2):
                    part = slice(q * CH, (q + 1) * CH)
                    one = bcast(ident[part, part].rearrange("p (o t) -> p o t", o=1), 1, NJ)
                    last = pool.tensor_tensor(ati[part, c, :, part], scores[part, c, :, q, 0, :], one, ALU.add)
                last.then_inc(ati_ready.sem, 1)
            pool.drain()
            pool.memset(t1[:, :, :, :], 0.0).then_inc(t1_zero.sem, 1)
            pool.wait_ge(x_copied.sem, x_copied.by(L, NSTEP))
            carry(pool)
            dma(wkv_rows[:, :, :, :, :].rearrange("v b j q k -> v (b j q) k"),
                lay(I["state_wkv"]).rearrange("l b h v k -> v (l b h) k")).then_inc(wkv_in.sem, 16)
            pool.wait_ge(s0_mm.sem, s0_mm.by(L, 1))
            for b in range(SB):
                last = pool.tensor_tensor(s0[:, b, :, :], s0[:, b, :, :],
                                          bcast(dlast[:, :, NPC + b:NPC + b + 1], 2, NA), ALU.mult)
            last.then_inc(s0_decayed.sem, 1)
            pool.wait_ge(sw_ready.sem, sw_ready.by(L, SB + 1))
            carry(pool)
            dma(lay(O["p_wkv"]).rearrange("l b h v k -> v (l b h) k"),
                pwkv_out[:, :, :, :].rearrange("v j q k -> v (j q) k")).then_inc(wkv_left.sem, 16)
            dma(lay(O["s_wkv"]).rearrange("l b h v k -> v (l b h) k"),
                wkv_out[:, :, :, :, :].rearrange("v b j q k -> v (b j q) k")).then_inc(wkv_left.sem, 16)

        def each(eng, first, count, body):
            turns = (count - (steps_of[first + count - 1] > 1)) // RS
            if turns > 1:
                with eng.Fori(0, turns) as i:
                    for u in range(RS):
                        body(first + u, i)
            else:
                for u in range(RS * turns):
                    body(first + u, 0)
            for u in range(RS * turns, count):
                body(first + u, 0)

        LN_SUMS = [(bank[4], bank[5]), (bank[0], bank[1]), (bank[4], bank[5])]
        WO_BANKS = (5, 6, 7, 4)
        GROUP = (4, KT - 1, 4)

        @block.sync
        def _(sp):
            tok = [I["x_prompt"][0, 0:P, :], I["x_prompt"][0, P:2 * P, :],
                   I["x_sample"].rearrange("b t d -> (b t) d")]
            for n, (_, rows) in enumerate(TT):
                sp.dma_start(xrows[0:rows, n, :], tok[n]).then_inc(rows_in.sem, 16)
            with sp.Fori(0, DEPTH) as L:

                def load(p, i, src):
                    dst = raw[:, p % RS, :].rearrange("p (k n) -> p k n", n=src.shape[-1])
                    sp.wait_ge(lo_ready.sem, lo_ready.by(L, RS * i + max(0, p - RS + 1)))
                    sp.dma_start(dst, src).then_inc(raw_in[p % RS].sem, 16)

                def columns(w, col, n=P):
                    return w[bass.ds(L, 1), :, bass.ds(col, n)].rearrange("l (k p) n -> p (l k) n", p=P)

                def ffn(base, wg, wu, wd):
                    def up(p, i):
                        d = p - base
                        src = columns(wg if d % 2 == 0 else wu, (i * (RS // 2) + d // 2) * P)
                        load(p, i, src)
                    each(sp, base, NUP, up)
                    for half in range(2):
                        first = base + NUP + half * NDN

                        def down(p, i):
                            src = wd[bass.ds(L, 1), bass.ds((i * RS + (p - first)) * 2 * P, 2 * P),
                                     half * 4 * P:(half + 1) * 4 * P]
                            load(p, i, src.rearrange("l (k p) n -> p (l k) n", p=P))
                        each(sp, first, NDN, down)

                ffn(U1, I["ffn1_wg"], I["ffn1_wu"], I["ffn1_wd"])
                each(sp, WI, TR, lambda p, i: load(p, i, columns(I["w_in"], (i * RS + (p - WI)) * P + RCOLS)))
                each(sp, WI + TR, NRW, lambda p, i: load(p, i, columns(I["w_in"], (i * RS + (p - WI - TR)) * P)))
                each(sp, WO, KT, lambda p, i: load(p, i, columns(I["w_out"], (i * RS + (p - WO)) * P)))
                ffn(U2, I["ffn2_wg"], I["ffn2_wu"], I["ffn2_wd"])
            for n, (at, rows) in enumerate(TT):
                sp.wait_ge(end_low.sem, n + 1)
                sp.wait_ge(end_high.sem, n + 1)
                dst = (O["y_prompt"][0, at:at + rows, :] if n < 2 else O["y_sample"].rearrange("b t d -> (b t) d"))
                sp.dma_start(dst, xrows[0:rows, n, :]).then_inc(y_out.sem, 16)
            sp.wait_ge(y_out.sem, 16 * NTT)

        def three_passes(pe, out, slot, at, hi, lo, start, stop):
            w_hi, w_lo = whi[:, slot, at:at + P], wlo[:, slot, at:at + P]
            pe.matmul(out, w_hi, hi, start=start, stop=False)
            pe.matmul(out, w_hi, lo, start=False, stop=False)
            return pe.matmul(out, w_lo, hi, start=False, stop=stop)

        @block.tensor
        def _(pe):
            pe.wait_ge(ident_ready.sem, 1)
            pe.wait_ge(rows_in.sem, 16 * NTT)
            for k in range(KT):
                for n, (at, rows) in enumerate(TT):
                    last = pe.transpose(bank[k][:, at:at + rows], xrows[0:rows, n, k * P:(k + 1) * P],
                                        ident[0:rows, 0:rows])
                last.then_inc(x_turned.sem, 1)
            with pe.Fori(0, DEPTH) as L:

                def chunk_of_columns(p, i, out):
                    pe.wait_ge(lo_ready.sem, lo_ready.by(L, RS * i + p + 1))
                    for k in range(KT):
                        last = three_passes(pe, out, p % RS, k * P, xh[:, k, :], xl[:, k, :], k == 0, k == KT - 1)
                    last.then_inc(used.sem, steps_of[p])

                def first_chunks(base, which, outs):
                    for n in range(LOOK):
                        pe.wait_ge(lo_ready.sem, lo_ready.by(L, base + n + 1))
                    for k in range(KT):
                        pe.wait_ge(x_ready.sem, x_ready.by(L, KT * (which - 1) + k + 1))
                        for n in range(LOOK):
                            last = three_passes(pe, outs[n], (base + n) % RS, k * P, xh[:, k, :], xl[:, k, :],
                                                k == 0, k == KT - 1)
                            if k == KT - 1:
                                last.then_inc(used.sem, 1)

                def ln_sums_of_group(which):
                    pe.wait_ge(group_ready.sem, group_ready.by(L, which + 1))
                    for out, src in zip(LN_SUMS[which], (zsum, sqsum)):
                        pe.matmul(out[:, 0:T], ones[:, :], src, start=True, stop=False)

                def ln_sums(which):
                    sums = LN_SUMS[which]
                    for o in range(GROUP[which], KT):
                        pe.wait_ge(z_ready.sem, z_ready.by(L, which * KT + o + 1))
                        pe.matmul(sums[0][:, 0:T], ones[:, :], z[:, o, :], start=False, stop=(o == KT - 1))
                        pe.wait_ge(sq_ready.sem, sq_ready.by(L, which * KT + o + 1))
                        mm = pe.matmul(sums[1][:, 0:T], ones[:, :], sq[:, o, :], start=False, stop=(o == KT - 1))
                    mm.then_inc(stats_ready.sem, 1)

                def ffn(base, f, which):
                    def up(p, i):
                        d = p - base
                        if d % 2 == 0:
                            pe.wait_ge(up_done.sem, up_done.by(L, f * NFF + (RS // 2) * i + d // 2 - 1))
                        chunk_of_columns(p, i, bank[d % RS][:, 0:T])
                    pe.wait_ge(up_done.sem, up_done.by(L, f * NFF))
                    first_chunks(base, 2 * f, [bank[n][:, 0:T] for n in range(LOOK)])
                    up(base + LOOK, 0)
                    each(pe, base + RS, NUP - RS, up)
                    if f == 0:
                        pe.wait_ge(vrows_in.sem, vrows_in.by(L, 16 * 17))
                        pe.transpose(bank[7][:, 0:NV1], vrow1[0:NV1, :], ident[0:NV1, 0:NV1])
                        pe.transpose(bank[7][:, NV1:NV1 + NV2], vrow2[0:NV2, :],
                                     ident[0:NV2, 0:NV2]).then_inc(vec_turned.sem, 1)
                        pe.wait_ge(vec_ready.sem, vec_ready.by(L, 1))
                    for half in range(2):
                        first = base + NUP + half * NDN
                        banks = [bank[4 * (1 - half) + o][:, 0:T] for o in range(4)]
                        if half:
                            pe.wait_ge(up_done.sem, up_done.by(L, (f + 1) * NFF))

                        def down(p, i, c=None):
                            pe.wait_ge(lo_ready.sem, lo_ready.by(L, RS * i + p + 1))
                            if half == 0:
                                pe.wait_ge(hl_done.sem, hl_done.by(L, f * NFF + 2 * RS * i + 2 * (p - first) + 2))
                            for k2 in range(2):
                                k = 2 * RS * i + 2 * (p - first) + k2
                                for o in range(4):
                                    hid = lambda t: (t[:, k, :] if isinstance(i, int) else
                                                     t[:, bass.ds(k, 1), :].rearrange("p k t -> p (k t)"))
                                    last = three_passes(
                                        pe, banks[o], p % RS, (4 * k2 + o) * P, hid(hh), hid(hl),
                                        p == first and k2 == 0, p == first + NDN - 1 and k2 == 1)
                            last.then_inc(used.sem, steps_of[p])
                        down(first, 0)
                        each(pe, first + 1, 2 * RS, down)
                        if half:
                            pe.wait_ge(consts.sem, 1)
                            ln_sums_of_group(which)
                        down(first + 2 * RS + 1, 0)
                        down(first + 2 * RS + 2, 0)
                    ln_sums(which)

                ffn(U1, 0, 0)

                pe.wait_ge(hist_in.sem, hist_in.by(L, 32))
                for n in range(NRW):
                    turn(pe, bank[6][:, n * SB:(n + 1) * SB], hist_shift[:, n * P:(n + 1) * P])
                for n in range(NQK):
                    last = turn(pe, bank[7][:, n * 24:(n + 1) * 24], hist_conv[:, n * P:(n + 1) * P])
                last.then_inc(hist_turned.sem, 1)

                def in_tile(p, i):
                    pe.wait_ge(proj_ready.sem, proj_ready.by(L, RS * i + (p - WI) - RS + 1))
                    chunk_of_columns(p, i, bank[(p - WI) % RS][:, 0:T])
                pe.wait_ge(proj_ready.sem, proj_ready.by(L, 0))
                first_chunks(WI, 1, [bank[n][:, 0:T] for n in range(LOOK)])
                in_tile(WI + LOOK, 0)
                each(pe, WI + RS, TR - RS, in_tile)
                for t in range(TR, NIN):
                    if t == TR + 1:
                        gates_product(pe, L)
                    if t == TR + 3:
                        conv_ends_turned(pe, L)
                    if t in (TR + 4, TR + 6, TR + 8):
                        keys_values_turned(pe, L, (t - TR - 4) // 2)
                    if t == TR + 10:
                        gate_columns(pe, L)
                    in_tile(WI + t, 0)
                tensor_mixers(pe, L)

                pe.wait_ge(mix_ready.sem, mix_ready.by(L, 1))
                for p in range(WO, WO + KT):
                    if p == WO:
                        pe.wait_ge(sw_ready.sem, sw_ready.by(L, 4))
                    if p == WO + 3:
                        pe.wait_ge(sw_ready.sem, sw_ready.by(L, SB + 1))
                    if p - WO >= 4:
                        pe.wait_ge(z_ready.sem, z_ready.by(L, KT + p - WO - 3))
                    chunk_of_columns(p, 0, bank[WO_BANKS[(p - WO) % 4]][:, 0:T])
                ln_sums_of_group(1)
                ln_sums(1)
                ffn(U2, 1, 2)
            pe.wait_ge(x_ready.sem, KT + DEPTH * 3 * KT)
            for n, (at, rows) in enumerate(TT):
                for half in range(2):
                    for k in range(4):
                        last = pe.transpose(bank[2 * n + half][0:rows, k * P:(k + 1) * P],
                                            x[:, 4 * half + k, at:at + rows], ident[:, :])
                    last.then_inc(end_turned.sem, 1)

        @block.scalar
        def _(act):
            for k in range(KT):
                act.wait_ge(x0_ready.sem, k + 1)
                act.activation(xh[:, k, :], x[:, k, :], ACT.Copy).then_inc(x0_hi.sem, 1)
            with act.Fori(0, DEPTH) as L:

                def split_hi(p, i=0):
                    act.wait_ge(raw_in[p % RS].sem, raw_in[p % RS].by(L, 16 * (i + loads_before[p] + 1)))
                    act.wait_ge(used.sem, used.by(L, RS * i + max(0, p - RS + 1)))
                    act.activation(whi[:, p % RS, :], raw[:, p % RS, :], ACT.Copy).then_inc(
                        hi_ready.sem, steps_of[p])

                def squares(first, last, which):
                    for o in range(first, last):
                        act.wait_ge(z_ready.sem, z_ready.by(L, which * KT + o + 1))
                        act.activation(sq[:, o, :], z[:, o, :], ACT.Square).then_inc(sq_ready.sem, 1)

                def layer_norm(which):
                    act.activation(early, sq[0:1, 0, 0:1], ACT.Ln)
                    act.wait_ge(var_ready.sem, var_ready.by(L, which + 1))
                    act.activation(rstd, var, ACT.Ln)
                    act.drain()
                    act.activation(rstd, rstd, ACT.Exp, scale=-0.5).then_inc(rstd_ready.sem, 1)
                    g0 = V_LN + which * 2 * KT
                    for o in range(KT):
                        act.wait_ge(norm_ready.sem, norm_ready.by(L, which * KT + o + 1))
                        g, b = vec[:, g0 + o:g0 + o + 1], vec[:, g0 + KT + o:g0 + KT + o + 1]
                        act.activation(xh[:, o, :], z[:, o, :], ACT.Identity, scale=g, bias=b).then_inc(
                            xh_ready.sem, 1)

                def ffn(base, f, which, follow):
                    def up(p, i):
                        split_hi(p + LOOK, i)
                        d = p - base
                        if d % 2:
                            pair = (RS // 2) * i + d // 2
                            act.wait_ge(used.sem, used.by(L, RS * i + p))
                            act.wait_ge(up_done.sem, up_done.by(L, f * NFF + pair - 1))
                            act.activation(silu[:, (d // 2) % 2, :], bank[d - 1][:, 0:T], ACT.Silu).then_inc(
                                silu_ready.sem, 1)
                    each(act, base, NUP, up)
                    if f == 0:
                        act.wait_ge(vec_turned.sem, vec_turned.by(L, 1))
                        act.activation(vec[:, :], bank[7][:, 0:NV1 + NV2], ACT.Copy).then_inc(vec_ready.sem, 1)
                    each(act, base + NUP + LOOK, NDN, split_hi)
                    squares(0, 4, which)
                    each(act, base + NUP + NDN + LOOK, NDN - LOOK, split_hi)
                    for p in follow:
                        split_hi(p)
                    squares(4, KT, which)
                    layer_norm(which)

                for p in range(LOOK):
                    split_hi(p)
                ffn(U1, 0, 0, range(WI, WI + LOOK))

                act.wait_ge(hist_turned.sem, hist_turned.by(L, 1))
                act.activation(hist(proj[:, TR:NIN, :])[:, :, :, LEAD - 1],
                               bank[6][:, 0:NRW * SB].rearrange("p (n b) -> p n b", b=SB), ACT.Copy)
                act.activation(hist(proj[:, 0:NQK, :])[:, :, :, 0:LEAD],
                               bank[7][:, 0:NQK * 24].rearrange("p (n b j) -> p n b j", b=SB, j=LEAD),
                               ACT.Copy).then_inc(hist_ready.sem, 1)

                def in_tile(p, i):
                    act.wait_ge(used.sem, used.by(L, RS * i + p + 1))
                    n = RS * i + (p - WI)
                    for dst, src in ((slice(LEAD, LEAD + TP), bank[(p - WI) % RS][:, 0:TP]),
                                     (None, bank[(p - WI) % RS][:, TP:T])):
                        if isinstance(i, int):
                            tile = proj[:, n:n + 1, :]
                        else:
                            tile = proj[:, bass.ds(n, 1), :]
                        if dst:
                            act.activation(tile[:, :, dst].rearrange("p k t -> p (k t)"), src, ACT.Copy)
                        else:
                            out = tile[:, :, S0C:W].rearrange("p k (b t) -> p (k b) t", t=SEG)[:, :, LEAD:SEG]
                            act.activation(out, src.rearrange("p (b t) -> p b t", t=ST), ACT.Copy).then_inc(
                                proj_ready.sem, 1)

                def in_step(p, i):
                    split_hi(p + LOOK, i)
                    in_tile(p, i)
                each(act, WI, TR, in_step)
                for t in range(TR, NIN):
                    split_hi(WI + t + LOOK if t + LOOK < NIN else WO + t + LOOK - NIN)
                    in_tile(WI + t, 0)
                    if t == TR:
                        act.drain()
                        copy_ends(act, L)
                        output_gate(act, L)
                    if t == TR + 1:
                        log_forget(act, L)
                    if t == TR + 2:
                        act.wait_ge(conv_ready.sem, conv_ready.by(L, NQK))
                        act.activation(qk[:, :, :], qk[:, :, :], ACT.Silu).then_inc(qk_ready.sem, 1)
                    if t == TR + 3:
                        copy_ends_out(act, L)
                    if t in (TR + 4, TR + 6, TR + 8):
                        copy_keys_values(act, L, (t - TR - 4) // 2)
                    if t == TR + 10:
                        copy_gate_columns(act, L)

                scalar_mixers(act, L)

                for p in range(WO, WO + KT):
                    split_hi(p + LOOK)
                    squares(p - WO, p - WO + 1, 1)
                layer_norm(1)
                ffn(U2, 1, 2, [])
            for n, (_, rows) in enumerate(TT):
                act.wait_ge(end_turned.sem, 2 * n + 2)
                act.activation(xrows[0:rows, n, 4 * P:8 * P], bank[2 * n + 1][0:rows, :], ACT.Copy).then_inc(
                    end_high.sem, 1)

        @block.vector
        def _(dve):
            dve.nop().then_inc(up_done.sem, 2)
            dve.nop().then_inc(proj_ready.sem, RS)
            dve.nop().then_inc(hl_done.sem, 2)
            for k in range(KT):
                dve.wait_ge(x_turned.sem, k + 1)
                dve.tensor_copy(x[:, k, :], bank[k][:, 0:T]).then_inc(x0_ready.sem, 1)
            for k in range(KT):
                dve.wait_ge(x0_hi.sem, k + 1)
                dve.tensor_tensor(xl[:, k, :], x[:, k, :], xh[:, k, :].bitcast(F32), ALU.subtract).then_inc(
                    x_ready.sem, 1)
            with dve.Fori(0, DEPTH) as L:

                def split_lo(p, i=0):
                    dve.wait_ge(hi_ready.sem, hi_ready.by(L, RS * i + p + 1))
                    dve.tensor_tensor(wlo[:, p % RS, :], raw[:, p % RS, :], whi[:, p % RS, :].bitcast(F32),
                                      ALU.subtract).then_inc(lo_ready.sem, steps_of[p])

                def residual(first, last, which, c, b0, done):
                    for o in range(first, last):
                        dve.wait_ge(used.sem, used.by(L, done(o)))
                        dve.scalar_tensor_tensor(out=z[:, o, :], in0=bank[b0 + (o - first) % 4][:, 0:T], scalar=c,
                                                 in1=x[:, o, :], op0=ALU.mult, op1=ALU.add).then_inc(
                            z_ready.sem, 1)

                def layer_norm(which):
                    dve.wait_ge(stats_ready.sem, stats_ready.by(L, which + 1))
                    dve.tensor_scalar(mean, LN_SUMS[which][0][:, 0:T], 1.0 / DM, None, ALU.mult)
                    dve.drain()
                    dve.tensor_tensor(rstd, mean, mean, ALU.mult)
                    dve.drain()
                    dve.scalar_tensor_tensor(out=var, in0=LN_SUMS[which][1][:, 0:T], scalar=1.0 / DM, in1=rstd,
                                             op0=ALU.mult, op1=ALU.subtract)
                    dve.drain()
                    dve.tensor_scalar(var, var, 0.0, LN_EPS / ALPHA ** 2, ALU.max, ALU.add).then_inc(
                        var_ready.sem, 1)
                    dve.tensor_tensor(z[:, 0:4, :], z[:, 0:4, :],
                                      bcast(mean.rearrange("p (k t) -> p k t", k=1), 1, 4), ALU.subtract)
                    dve.drain()
                    dve.wait_ge(rstd_ready.sem, rstd_ready.by(L, which + 1))
                    g0 = V_LN + which * 2 * KT
                    for o in range(KT):
                        g, b = vec[:, g0 + o:g0 + o + 1], vec[:, g0 + KT + o:g0 + KT + o + 1]
                        dve.tensor_tensor(z[:, o, :], z[:, o, :], rstd, ALU.mult).then_inc(norm_ready.sem, 1)
                        if o + 4 < KT:
                            dve.tensor_tensor(z[:, o + 4, :], z[:, o + 4, :], mean, ALU.subtract)
                        dve.drain()
                        dve.tensor_scalar(x[:, o, :], z[:, o, :], g, b, ALU.mult, ALU.add).then_inc(xf_ready.sem, 1)

                def ffn(base, f, which, follow):
                    def up(p, i):
                        split_lo(p + LOOK, i)
                        d = p - base
                        if d % 2:
                            s = (d // 2) % 2
                            pair = f * NFF + (RS // 2) * i + d // 2
                            dve.wait_ge(used.sem, used.by(L, RS * i + p + 1))
                            dve.wait_ge(silu_ready.sem, silu_ready.by(L, pair + 1))
                            dve.wait_ge(hl_done.sem, hl_done.by(L, pair - 1))
                            if f == 1 and d == 1:
                                dve.wait_ge(wkv_left.sem, wkv_left.by(L, 32))
                            k = (RS // 2) * i + d // 2
                            out = (hh[:, k, :] if isinstance(i, int) else
                                   hh[:, bass.ds(k, 1), :].rearrange("p k t -> p (k t)"))
                            dve.tensor_tensor(out, silu[:, s, :], bank[d][:, 0:T], ALU.mult)
                            dve.tensor_tensor(hval[:, s, :], silu[:, s, :], bank[d][:, 0:T], ALU.mult).then_inc(
                                up_done.sem, 1)
                    each(dve, base, NUP, up)
                    c = 0.5 / ALPHA
                    each(dve, base + NUP + LOOK, NDN, split_lo)
                    residual(0, 4, which, c, 4, lambda o: base + NUP + NDN)
                    each(dve, base + NUP + NDN + LOOK, NDN - LOOK, split_lo)
                    for p in follow:
                        split_lo(p)
                    residual(4, KT, which, c, 0, lambda o: base + FFN)
                    layer_norm(which)

                for p in range(LOOK):
                    split_lo(p)
                ffn(U1, 0, 0, range(WI, WI + LOOK))

                each(dve, WI + LOOK, NQK, split_lo)
                for n in range(NQK):
                    split_lo(WI + LOOK + NQK + n)
                    conv(dve, L, n)
                for t in range(TR, NIN):
                    split_lo(WI + t + LOOK if t + LOOK < NIN else WO + t + LOOK - NIN)
                    if t == TR:
                        dve.memset(va[:, :, :, DK:DK + 1], 1.0)
                        dve.tensor_scalar(omu, vec[:, V_MU:V_MU + NRW], -1.0, 1.0, ALU.mult, ALU.add)
                    if t == TR + 1:
                        gate_rows(dve, L)
                    if t == TR + 2:
                        gate_sums(dve, L)
                    if t == TR + 11:
                        weighted_keys(dve, L)

                vector_mixers(dve, L)

                for p in range(WO, WO + KT):
                    split_lo(p + LOOK)
                    residual(p - WO, p - WO + 1, 1, 1.0 / ALPHA, WO_BANKS[(p - WO) % 4], lambda o: WO + o + 1)
                layer_norm(1)
                ffn(U2, 1, 2, [])
            for n, (_, rows) in enumerate(TT):
                dve.wait_ge(end_turned.sem, 2 * n + 1)
                dve.tensor_copy(xrows[0:rows, n, 0:4 * P], bank[2 * n][0:rows, :]).then_inc(end_low.sem, 1)

        @block.gpsimd
        def _(pool):
            make_constants(pool)
            pool.wait_ge(x_turned.sem, KT)
            with pool.Fori(0, DEPTH) as L:
                start_layer(pool, L)

                def hidden_lo(f):
                    def one(k, i):
                        pair = f * NFF + k + 2 * i
                        pool.wait_ge(up_done.sem, up_done.by(L, pair + 1))
                        at = lambda t: (t[:, bass.ds(k + 2 * i, 1), :].rearrange("p k t -> p (k t)"))
                        pool.tensor_tensor(at(hl), hval[:, k % 2, :], at(hh).bitcast(F32), ALU.subtract).then_inc(
                            hl_done.sem, 1)
                    with pool.Fori(0, NFF // 2) as i:
                        one(0, i)
                        one(1, i)

                def group_sums(which):
                    for o in range(1, GROUP[which]):
                        for done, out, src in ((z_ready, zsum, z), (sq_ready, sqsum, sq)):
                            if o > 1:
                                pool.drain()
                            pool.wait_ge(done.sem, done.by(L, which * KT + o + 1))
                            last = pool.tensor_tensor(out, src[:, 0, :] if o == 1 else out, src[:, o, :], ALU.add)
                    last.then_inc(group_ready.sem, 1)

                def x_lo(which):
                    for o in range(KT):
                        pool.wait_ge(xh_ready.sem, xh_ready.by(L, which * KT + o + 1))
                        pool.wait_ge(xf_ready.sem, xf_ready.by(L, which * KT + o + 1))
                        pool.tensor_tensor(xl[:, o, :], x[:, o, :], xh[:, o, :].bitcast(F32), ALU.subtract).then_inc(
                            x_ready.sem, 1)

                hidden_lo(0)
                group_sums(0)
                x_lo(0)
                pool_mixers(pool, L)
                group_sums(1)
                x_lo(1)
                hidden_lo(1)
                group_sums(2)
                x_lo(2)


_INS = ["x_prompt", "x_sample", "state_shift", "state_wkv", "state_conv", "state_C", "state_n", "state_m",
        "ffn1_wg", "ffn1_wu", "ffn1_wd", "ln1_g", "ln1_b", "w_in", "mu_shift", "w0", "w2", "a0", "a2", "g2", "k_k",
        "k_a", "r_k", "gn_g", "gn_b", "conv_w", "conv_b", "i_bias", "f_bias", "mh_g", "w_out", "ln2_g", "ln2_b",
        "ffn2_wg", "ffn2_wu", "ffn2_wd", "ln3_g", "ln3_b"]
_OUTS = [("y_prompt", "x_prompt"), ("y_sample", "x_sample"), ("p_shift", "state_shift"), ("p_wkv", "state_wkv"),
         ("p_conv", "state_conv"), ("p_C", "state_C"), ("p_n", "state_n"), ("p_m", "state_m"),
         ("s_shift", "state_shift"), ("s_wkv", "state_wkv"), ("s_conv", "state_conv"), ("s_C", "state_C"),
         ("s_n", "state_n"), ("s_m", "state_m")]


def kernel(**inputs):
    import numpy as _np
    import concourse.bacc as _bacc
    from concourse.bass_utils import run_bass_kernel_spmd as _run

    nc = _bacc.Bacc("TRN2", target_bir_lowering=False, num_devices=1)
    arrays, ins, outs = {}, {}, {}
    for name in _INS:
        a = _np.ascontiguousarray(inputs[name])
        arrays[f"in_{name}"] = a
        ins[name] = nc.dram_tensor(f"in_{name}", a.shape, mybir.dt.from_np(a.dtype), kind="ExternalInput").ap()
    for name, like in _OUTS:
        shape = list(inputs[like].shape)
        if name.startswith("p_"):
            shape[1] = inputs["x_prompt"].shape[0]
        outs[name] = nc.dram_tensor(f"out_{name}", shape, F32, kind="ExternalOutput").ap()
    hymba_kernel(nc, ins, outs)
    r = _run(nc, [arrays], core_ids=[0])
    return tuple(r.results[0][f"out_{name}"] for name, _ in _OUTS)
```
